# Optimizing a Trainium2 kernel written in Bass

```python
import math
import jax, jax.numpy as jnp
from jax import lax
import numpy as np

D_MODEL = 1024
BATCH = 1
SEQ = 256
DEPTH = 1
DEC_BATCH = 1
DEC_SEQ = 1024
PAST_LEN = 256

GRID_W = 64
ROPE_THETA = 10000.0
NORM_EPS = 1e-6
MLA_HEADS = 4
QK_NOPE = 128
QK_ROPE = 64
V_HEAD = 128
Q_LORA = 384
KV_LORA = 256
MLA_WIDTH = MLA_HEADS * V_HEAD
SSM_HEADS = 8
SSM_HEAD_DIM = 64
SSM_WIDTH = SSM_HEADS * SSM_HEAD_DIM
SSM_GROUPS = 2
D_STATE = 128
D_CONV = 3
CHUNK = 128
CONV_DIM = SSM_WIDTH + 2 * SSM_GROUPS * D_STATE
MIX_WIDTH = MLA_WIDTH + SSM_WIDTH
IN_WIDTH = Q_LORA + KV_LORA + QK_ROPE + SSM_WIDTH + CONV_DIM + 2 * SSM_HEADS
D_FF = -(-8 * D_MODEL // (3 * 256)) * 256
Q_BLOCK = 128

kernel_name = "hybrid_mla_ssd_prefix_dit_step"

def rms_norm(x, g):
    xf = x.astype(jnp.float32)
    y = xf * lax.rsqrt(jnp.mean(xf * xf, axis=-1, keepdims=True) + NORM_EPS)
    return (y * g.astype(jnp.float32)).astype(x.dtype)

def adaln(cond, w_mod, b_mod):
    m = jax.nn.silu(cond) @ w_mod + b_mod
    if m.ndim == 2:
        m = m[:, None, :]
    return jnp.split(m, 6, axis=-1)

def rope_2d(x, length):
    rows = length // GRID_W
    row = jnp.repeat(jnp.arange(rows), GRID_W)
    col = jnp.tile(jnp.arange(GRID_W), rows)
    half = QK_ROPE // 2
    quarter = half // 2
    inv_freq = ROPE_THETA ** (-jnp.arange(quarter, dtype=jnp.float32) / quarter)
    bshape = (1, length) + (1,) * (x.ndim - 3) + (quarter,)

    def rot(xa, pos):
        ang = pos.astype(jnp.float32)[:, None] * inv_freq[None, :]
        cos = jnp.cos(ang).reshape(bshape)
        sin = jnp.sin(ang).reshape(bshape)
        xa = xa.astype(jnp.float32)
        x1, x2 = xa[..., :quarter], xa[..., quarter:]
        return jnp.concatenate([x1 * cos - x2 * sin, x2 * cos + x1 * sin], axis=-1)

    out = jnp.concatenate([rot(x[..., :half], row), rot(x[..., half:], col)], axis=-1)
    return out.astype(x.dtype)

def mla_attention(q_nope, q_rope, k_nope, k_rope, v):
    b, sq, h, _ = q_nope.shape
    nb = sq // Q_BLOCK
    scale = (QK_NOPE + QK_ROPE) ** -0.5

    def block(qs):
        qn, qr = qs
        s = jnp.einsum("bqhd,bkhd->bhqk", qn, k_nope) + jnp.einsum("bqhr,bkr->bhqk", qr, k_rope)
        p = jax.nn.softmax(s.astype(jnp.float32) * scale, axis=-1).astype(v.dtype)
        return jnp.einsum("bhqk,bkhd->bqhd", p, v)

    qn_b = q_nope.reshape(b, nb, Q_BLOCK, h, QK_NOPE).transpose(1, 0, 2, 3, 4)
    qr_b = q_rope.reshape(b, nb, Q_BLOCK, h, QK_ROPE).transpose(1, 0, 2, 3, 4)
    out = lax.map(block, (qn_b, qr_b))
    return out.transpose(1, 0, 2, 3, 4).reshape(b, sq, h * V_HEAD)

def depthwise_conv_centred(x, w, bias):
    l = x.shape[1]
    pad = D_CONV // 2
    xp = jnp.pad(x, ((0, 0), (pad, pad), (0, 0)))
    y = bias
    for k in range(D_CONV):
        y = y + xp[:, k:k + l] * w[k]
    return y

def ssd_chunked(x, dt, a, bm, cm, init_state):
    b, l, h, p = x.shape
    g, n = bm.shape[-2:]
    r = h // g
    c = l // CHUNK
    f32 = jnp.float32
    dt = dt.astype(f32)
    xr = (x.astype(f32) * dt[..., None]).reshape(b, c, CHUNK, g, r, p)
    da = (dt * a).reshape(b, c, CHUNK, g, r).transpose(0, 3, 4, 1, 2)
    bc = bm.astype(f32).reshape(b, c, CHUNK, g, n)
    cc = cm.astype(f32).reshape(b, c, CHUNK, g, n)
    a_cs = jnp.cumsum(da, axis=-1)
    seg = a_cs[..., :, None] - a_cs[..., None, :]
    causal = jnp.tril(jnp.ones((CHUNK, CHUNK), dtype=bool))
    lmat = jnp.exp(jnp.where(causal, seg, -jnp.inf))
    cb = jnp.einsum("bclgn,bcsgn->bgcls", cc, bc)
    y_diag = jnp.einsum("bgcls,bgrcls,bcsgrp->bclgrp", cb, lmat, xr)
    decay_states = jnp.exp(a_cs[..., -1:] - a_cs)
    chunk_states = jnp.einsum("bclgn,bgrcl,bclgrp->cbgrpn", bc, decay_states, xr)
    chunk_decay = jnp.exp(a_cs[..., -1]).transpose(3, 0, 1, 2)

    def step(state, inp):
        dec, st = inp
        return state * dec[..., None, None] + st, state

    final, entering = lax.scan(step, init_state.astype(f32).reshape(b, g, r, p, n),
                               (chunk_decay, chunk_states))
    y_off = jnp.einsum("bclgn,cbgrpn,bgrcl->bclgrp", cc, entering, jnp.exp(a_cs))
    y = (y_diag + y_off).reshape(b, l, h, p)
    return y, final.reshape(b, h, p, n)

def ssm_mixer(z, xbc, dt_f_raw, dt_b_raw, conv_w, conv_b, dt_bias, a_log, d_skip, g_out,
              init_f, init_b):
    b, l, _ = xbc.shape
    xbc = jax.nn.silu(depthwise_conv_centred(xbc, conv_w, conv_b))
    xs, bm, cm = jnp.split(xbc, [SSM_WIDTH, SSM_WIDTH + SSM_GROUPS * D_STATE], axis=-1)
    xs = xs.reshape(b, l, SSM_HEADS, SSM_HEAD_DIM)
    bm = bm.reshape(b, l, SSM_GROUPS, D_STATE)
    cm = cm.reshape(b, l, SSM_GROUPS, D_STATE)
    f32 = jnp.float32
    dt_f = jax.nn.softplus(dt_f_raw.astype(f32) + dt_bias[0].astype(f32))
    dt_b = jax.nn.softplus(dt_b_raw.astype(f32) + dt_bias[1].astype(f32))
    a_f = -jnp.exp(a_log[0].astype(f32))
    a_b = -jnp.exp(a_log[1].astype(f32))
    flip = lambda t: jnp.flip(t, axis=1)
    y_f, fin_f = ssd_chunked(xs, dt_f, a_f, bm, cm, init_f)
    y_b, fin_b = ssd_chunked(flip(xs), flip(dt_b), a_b, flip(bm), flip(cm), init_b)
    y = y_f + flip(y_b) + d_skip.astype(f32)[:, None] * xs.astype(f32)
    y = y.reshape(b, l, SSM_WIDTH) * jax.nn.silu(z.astype(f32))
    return rms_norm(y, g_out).astype(z.dtype), fin_f, fin_b

def split_in(proj):
    idx = np.cumsum([Q_LORA, KV_LORA, QK_ROPE, SSM_WIDTH, CONV_DIM, SSM_HEADS]).tolist()
    return jnp.split(proj, idx, axis=-1)

def token_mixing(h, w_in, g_q, w_uq, g_kv, w_ukv, conv_w, conv_b, dt_bias, a_log, d_skip,
                 g_ssm_out, w_out, ctx_ckv, ctx_krope, init_f, init_b):
    b, l, _ = h.shape
    q_c, kv_c, k_rope, z, xbc, dt_f, dt_b = split_in(h @ w_in)
    ckv = rms_norm(kv_c, g_kv)
    q = (rms_norm(q_c, g_q) @ w_uq).reshape(b, l, MLA_HEADS, QK_NOPE + QK_ROPE)
    q_nope, q_rope = q[..., :QK_NOPE], q[..., QK_NOPE:]
    if ctx_ckv is None:
        ckv_all, krope_all = ckv, k_rope
    else:
        q_rope = rope_2d(q_rope, l)
        ckv_all = jnp.concatenate([ctx_ckv, ckv], axis=1)
        krope_all = jnp.concatenate([ctx_krope, rope_2d(k_rope, l)], axis=1)
    sk = ckv_all.shape[1]
    kv = (ckv_all @ w_ukv).reshape(b, sk, MLA_HEADS, QK_NOPE + V_HEAD)
    k_nope, v = kv[..., :QK_NOPE], kv[..., QK_NOPE:]
    attn = mla_attention(q_nope, q_rope, k_nope, krope_all, v)
    ssm_out, fin_f, fin_b = ssm_mixer(z, xbc, dt_f, dt_b, conv_w, conv_b, dt_bias, a_log,
                                      d_skip, g_ssm_out, init_f, init_b)
    out = jnp.concatenate([attn, ssm_out], axis=-1) @ w_out
    return out, ckv, k_rope, fin_f, fin_b

def ffn_sublayer(x, shift, scale, gate, g_pre, g_post, w_gate, w_up, w_down):
    h = rms_norm(x, g_pre) * (1 + scale) + shift
    f = (jax.nn.silu(h @ w_gate) * (h @ w_up)) @ w_down
    return x + gate * rms_norm(f, g_post)

def setup_inputs(seed: int = 0) -> dict:
    key = jax.random.key(seed)
    ks = iter(jax.random.split(key, 32))
    nrm = lambda shape, s=1.0: jax.random.normal(next(ks), shape, jnp.float32) * s
    gain = lambda shape: 1.0 + 0.1 * jax.random.normal(next(ks), shape, jnp.float32)
    u = jax.random.uniform(next(ks), (DEPTH, 2, SSM_HEADS), jnp.float32)
    dt0 = jnp.exp(u * (math.log(0.1) - math.log(0.001)) + math.log(0.001))
    dt_bias = dt0 + jnp.log(-jnp.expm1(-dt0))
    a_log = jnp.log(jax.random.uniform(next(ks), (DEPTH, 2, SSM_HEADS), jnp.float32, 1.0, 16.0))
    return {
        "x_prompt": nrm((BATCH, SEQ, D_MODEL)),
        "x_sample": nrm((DEC_BATCH, DEC_SEQ, D_MODEL)),
        "cache_ckv": nrm((DEC_BATCH, DEPTH, PAST_LEN, KV_LORA)),
        "cache_krope": nrm((DEC_BATCH, DEPTH, PAST_LEN, QK_ROPE)),
        "state_ssm": nrm((DEC_BATCH, DEPTH, 2, SSM_HEADS, SSM_HEAD_DIM, D_STATE), 0.1),
        "c": nrm((DEC_BATCH, D_MODEL)),
        "c_ctx": nrm((D_MODEL,)),
        "w_mod": nrm((DEPTH, D_MODEL, 6 * D_MODEL), D_MODEL ** -0.5),
        "b_mod": nrm((DEPTH, 6 * D_MODEL), 0.01),
        "g_pre_mix": gain((DEPTH, D_MODEL)),
        "g_post_mix": gain((DEPTH, D_MODEL)),
        "w_in": nrm((DEPTH, D_MODEL, IN_WIDTH), D_MODEL ** -0.5),
        "g_q": gain((DEPTH, Q_LORA)),
        "w_uq": nrm((DEPTH, Q_LORA, MLA_HEADS * (QK_NOPE + QK_ROPE)), Q_LORA ** -0.5),
        "g_kv": gain((DEPTH, KV_LORA)),
        "w_ukv": nrm((DEPTH, KV_LORA, MLA_HEADS * (QK_NOPE + V_HEAD)), KV_LORA ** -0.5),
        "conv_w": nrm((DEPTH, D_CONV, CONV_DIM), D_CONV ** -0.5),
        "conv_b": nrm((DEPTH, CONV_DIM), 0.01),
        "dt_bias": dt_bias,
        "a_log": a_log,
        "d_skip": gain((DEPTH, SSM_HEADS)),
        "g_ssm_out": gain((DEPTH, SSM_WIDTH)),
        "w_out": nrm((DEPTH, MIX_WIDTH, D_MODEL), MIX_WIDTH ** -0.5),
        "g_pre_ffn": gain((DEPTH, D_MODEL)),
        "g_post_ffn": gain((DEPTH, D_MODEL)),
        "w_gate": nrm((DEPTH, D_MODEL, D_FF), D_MODEL ** -0.5),
        "w_up": nrm((DEPTH, D_MODEL, D_FF), D_MODEL ** -0.5),
        "w_down": nrm((DEPTH, D_FF, D_MODEL), D_FF ** -0.5),
    }

def reference(x_prompt, x_sample, cache_ckv, cache_krope, state_ssm, c, c_ctx, w_mod, b_mod,
              g_pre_mix, g_post_mix, w_in, g_q, w_uq, g_kv, w_ukv, conv_w, conv_b, dt_bias,
              a_log, d_skip, g_ssm_out, w_out, g_pre_ffn, g_post_ffn, w_gate, w_up, w_down):
    y_p = x_prompt
    y_s = x_sample
    new_ckv, new_krope, new_ssm = [], [], []
    zero_state = jnp.zeros((x_prompt.shape[0], SSM_HEADS, SSM_HEAD_DIM, D_STATE), jnp.float32)
    for l in range(DEPTH):
        mix_args = (w_in[l], g_q[l], w_uq[l], g_kv[l], w_ukv[l], conv_w[l], conv_b[l],
                    dt_bias[l], a_log[l], d_skip[l], g_ssm_out[l], w_out[l])
        ffn_args = (g_pre_ffn[l], g_post_ffn[l], w_gate[l], w_up[l], w_down[l])

        sh1, sc1, gt1, sh2, sc2, gt2 = adaln(c_ctx, w_mod[l], b_mod[l])
        h = rms_norm(y_p, g_pre_mix[l]) * (1 + sc1) + sh1
        out, ckv, k_rope, fin_f, fin_b = token_mixing(h, *mix_args, None, None,
                                                      zero_state, zero_state)
        y_p = y_p + gt1 * rms_norm(out, g_post_mix[l])
        y_p = ffn_sublayer(y_p, sh2, sc2, gt2, *ffn_args)
        new_ckv.append(ckv)
        new_krope.append(k_rope)
        new_ssm.append(jnp.stack([fin_f, fin_b], axis=1).astype(x_prompt.dtype))

        sh1, sc1, gt1, sh2, sc2, gt2 = adaln(c, w_mod[l], b_mod[l])
        h = rms_norm(y_s, g_pre_mix[l]) * (1 + sc1) + sh1
        out, _, _, _, _ = token_mixing(h, *mix_args, cache_ckv[:, l], cache_krope[:, l],
                                       state_ssm[:, l, 0], state_ssm[:, l, 1])
        y_s = y_s + gt1 * rms_norm(out, g_post_mix[l])
        y_s = ffn_sublayer(y_s, sh2, sc2, gt2, *ffn_args)

    new_cache_ckv = jnp.stack(new_ckv, axis=1)
    new_cache_krope = jnp.stack(new_krope, axis=1)
    new_state_ssm = jnp.stack(new_ssm, axis=1)
    return (y_p, y_s, new_cache_ckv, new_cache_krope, new_state_ssm)


_drawn_inputs = setup_inputs


def setup_inputs(seed=0):
    import zlib

    import numpy as np

    out = dict(_drawn_inputs(seed))
    spreads = {}
    factors = {'cache_ckv': 5.022,
     'cache_krope': 8.0,
     'b_mod': 3.304,
     'g_q': 8.0,
     'conv_b': 4.158,
     'd_skip': 22.349,
     'state_ssm': 53.891}
    for name, (base, spread) in spreads.items():
        noise = np.random.default_rng([zlib.crc32(name.encode()), seed]).standard_normal(out[name].shape)
        drawn = base * np.exp(spread * noise) if base else spread * noise
        out[name] = __import__('jax').numpy.asarray(drawn.astype(out[name].dtype))
    for name, factor in factors.items():
        out[name] = (out[name] * factor).astype(out[name].dtype)
    return out
```

```python
from contextlib import ExitStack

import concourse.bass as bass
from concourse import mybir

P = 128
F32 = mybir.dt.float32
F32R = mybir.dt.float32r
BF16 = mybir.dt.bfloat16
ALU = mybir.AluOpType
ACT = mybir.ActivationFunctionType
AX_X = mybir.AxisListType.X

D = 1024
KD = D // P
N_LAT, N_PROMPT, N_CACHE = 1024, 256, 256
T = N_LAT + N_PROMPT
NT = T // P
NT_LAT = N_LAT // P
BLOCKS = [(0, 512), (512, 512), (1024, 256)]
EPS = 1e-6
HEADS, NOPE, ROPE, VD = 4, 128, 64, 128
Q_LORA, KV_LORA = 384, 256
KQ, KKV = Q_LORA // P, KV_LORA // P
SCALE = float(NOPE + ROPE) ** -0.5
NKEY = T + N_CACHE
SH, SP_, DS = 8, 64, 128
SW = SH * SP_
D_FF = 2816
FT = D_FF // P
N_XBC, N_Z = 8, 4
TILE_KINDS = ["xbc"] * N_XBC + ["dt"] + ["z"] * N_Z + ["q"] * KQ + ["kv"] * KKV + ["rope"]
N_TILES = len(TILE_KINDS)
N_STAGED = N_Z + KQ + KKV + 1
FIRST = {k: TILE_KINDS.index(k) for k in ("xbc", "dt", "z", "q", "kv", "rope")}
MOD_W = 256
MOD_EARLY = 2 * D // MOD_W
MOD_ALL = 6 * D // MOD_W

C_GPRE, C_GFFN, C_BMOD, C_GQ, C_GKV, C_CW, C_CB, C_GS, C_DTB, C_ALOG = 0, 8, 16, 64, 67, 69, 93, 101, 105, 106
N_COLS = 107
K_ID, K_MASK, K_SEL, K_FOLD, K_SA, K_SB, K_MT, K_MD = 0, 128, 384, 400, 528, 529, 530, 531
N_CONST = 532


class Chain:

    def __init__(self, eng, sem):
        self.eng, self.sem, self.n = eng, sem, 0

    def mark(self, ins):
        ins.then_inc(self.sem, 1)
        self.n += 1

    def wait(self, back=0):
        self.eng.wait_ge(self.sem, self.n - back)

    def link(self, ins):
        self.mark(ins)
        self.wait()


class Layer:

    def __init__(self, nc, dram, outs):
        self.nc, self.dram, self.outs, self.sems = nc, dram, outs, []

    def sb(self, stack, name, shape, dt=F32, side="left"):
        return stack.enter_context(self.nc.sbuf_tensor(name, shape, dt, side=side))

    def ps(self, stack, name, shape):
        return stack.enter_context(self.nc.psum_tensor(name, shape, F32))

    def sem(self, name):
        self.sems.append(self.nc.alloc_semaphore(name=name))
        return self.sems[-1]

    def reuse_semaphores(self):
        for s in self.sems:
            self.nc.sync.sem_clear(s)
        for s in self.sems:
            self.nc.release_semaphore(s)
        self.sems = []
        self.nc.all_engine_barrier()


def flat(ap):
    return ap.rearrange("p a b -> p (a b)")


def across(ap, n):
    p, a = ap.shape
    return ap.unsqueeze(2).to_broadcast([p, a, n])


class NormStage:
    def __init__(self, L, st, tag, hT_hi, hT_lo, scale_col, shift_col):
        self.L, self.tag = L, tag
        self.hi, self.lo, self.a, self.s = hT_hi, hT_lo, scale_col, shift_col
        self.xin = L.sb(st, f"{tag}_xin", [P, 4, D])
        self.xn = L.sb(st, f"{tag}_xn", [P, NT, D])
        self.ssq = L.sb(st, f"{tag}_ssq", [P, NT])
        self.ms = L.sb(st, f"{tag}_ms", [P, NT])
        self.rstd = L.sb(st, f"{tag}_rstd", [P, NT])
        self.neghalf = L.sb(st, f"{tag}_nh", [P, 1])
        self.full = L.sb(st, f"{tag}_full", [P, 3, 512])
        self.psX = L.ps(st, f"{tag}_psX", [P, 4, 512])
        self.x_loaded = [L.sem(f"{tag}_x_loaded{i}") for i in range(4)]
        (self.squared, self.meansq, self.rstd_ready, self.xn_ready, self.transposed, self.modulated, self.rounded,
         self.h_ready, self.const) = (L.sem(f"{tag}_{n}") for n in (
             "squared", "meansq", "rstd_ready", "xn_ready", "transposed", "modulated", "rounded", "h_ready", "const"))
        self.steps = [(b, k) for b in range(len(BLOCKS)) for k in range(KD)]

    def load(self, eng, tiles, t):
        if t >= 4:
            eng.wait_ge(self.xn_ready, t - 3)
        eng.dma_start(self.xin[:, t % 4, :], tiles(t)).then_inc(self.x_loaded[t % 4], 16)

    def act_square(self, act, t):
        act.wait_ge(self.x_loaded[t % 4], 16 * (t // 4 + 1))
        act.activation(self.xn[:, t, :], self.xin[:, t % 4, :], ACT.Square,
                       accum_out=self.ssq[:, t:t + 1]).then_inc(self.squared, 1)

    def pool_begin(self, pool):
        pool.memset(self.neghalf[:], -0.5).then_inc(self.const, 1)
        pool.wait_ge(self.const, 1)

    def pool_rstd(self, pool, t):
        pool.wait_ge(self.meansq, t + 1)
        pool.tensor_tensor(self.rstd[:, t:t + 1], self.ms[:, t:t + 1], self.neghalf[:],
                           ALU.pow).then_inc(self.rstd_ready, 1)

    def dve_step(self, dve, t):
        if t < NT:
            dve.wait_ge(self.squared, t + 1)
            dve.tensor_scalar(self.ms[:, t:t + 1], self.ssq[:, t:t + 1], 1.0 / D, EPS, ALU.mult,
                              ALU.add).then_inc(self.meansq, 1)
        if t >= 1:
            u = t - 1
            dve.wait_ge(self.rstd_ready, u + 1)
            dve.tensor_scalar(self.xn[:, u, :], self.xin[:, u % 4, :], self.rstd[:, u:u + 1], None,
                              ALU.mult).then_inc(self.xn_ready, 1)

    def pe_transposes(self, pe, ident):
        for n, (b, k) in enumerate(self.steps):
            t0, w = BLOCKS[b][0] // P, BLOCKS[b][1] // P
            pe.wait_ge(self.xn_ready, t0 + w)
            if n >= 4:
                pe.wait_ge(self.modulated, n - 3)
            for i in range(w):
                mm = pe.transpose(self.psX[:, n % 4, i * P:(i + 1) * P], self.xn[:, t0 + i, k * P:(k + 1) * P],
                                  ident)
            mm.then_inc(self.transposed, 1)

    def act_modulate(self, act):
        for n, (b, k) in enumerate(self.steps):
            w, g = BLOCKS[b][1], int(BLOCKS[b][0] >= N_LAT)
            act.wait_ge(self.transposed, n + 1)
            if n >= 3:
                act.wait_ge(self.h_ready, n - 2)
            act.activation(self.full[:, n % 3, :w], self.psX[:, n % 4, :w], ACT.Identity,
                           bias=self.s[:, k, g:g + 1], scale=self.a[:, k, g:g + 1]).then_inc(self.modulated, 1)

    def dve_split(self, dve):
        for n, (b, k) in enumerate(self.steps):
            c0, w = BLOCKS[b]
            dve.wait_ge(self.modulated, n + 1)
            dve.tensor_copy(self.hi[:, k, c0:c0 + w], self.full[:, n % 3, :w]).then_inc(self.rounded, 1)
            dve.wait_ge(self.rounded, n + 1)
            dve.tensor_tensor(self.lo[:, k, c0:c0 + w], self.full[:, n % 3, :w],
                              self.hi[:, k, c0:c0 + w].bitcast(F32), ALU.subtract).then_inc(self.h_ready, 1)


class ModStage:
    def __init__(self, L, st, tag, first, last, banks):
        self.L, self.first, self.last, self.banks = L, first, last, banks
        self.ring = L.sb(st, f"{tag}_wring", [P, 2, KD, MOD_W])
        self.row = L.sb(st, f"{tag}_row", [P, 2, MOD_W])
        self.psM = L.ps(st, f"{tag}_psM", [P, banks, 512])
        self.psC = L.ps(st, f"{tag}_psC", [P, 2, P])
        self.loaded = [L.sem(f"{tag}_w_loaded{i}") for i in range(2)]
        self.row_out = [L.sem(f"{tag}_row_out{i}") for i in range(2)]
        self.product, self.row_ready, self.turned, self.col_ready = (
            L.sem(f"{tag}_{n}") for n in ("product", "row_ready", "turned", "col_ready"))

    @staticmethod
    def is_gate(j):
        return (j * MOD_W // D) % 3 == 2

    def n_turned(self, j):
        return sum(not self.is_gate(i) for i in range(self.first, j))

    def n_rows(self, j, slot):
        return sum(self.is_gate(i) for i in range(self.first + slot, j, 2))

    def load(self, eng, j):
        i = j - self.first
        if i >= 2:
            eng.wait_ge(self.product, i - 1)
        eng.dma_start(self.ring[:, i % 2, :, :],
                      self.L.dram["w_mod"].rearrange("(k p) n -> p k n", p=P)[:, :, j * MOD_W:(j + 1) * MOD_W]
                      ).then_inc(self.loaded[i % 2], 16)

    def pe_product(self, pe, j):
        i = j - self.first
        pe.wait_ge(self.loaded[i % 2], 16 * (i // 2 + 1))
        if i >= self.banks:
            pe.wait_ge(self.row_ready, i + 1 - self.banks)
        for k in range(KD):
            mm = pe.matmul(self.psM[:, i % self.banks, :MOD_W], self.L.cond_st[:, k, :], self.ring[:, i % 2, k, :],
                           start=(k == 0), stop=(k == KD - 1))
        mm.then_inc(self.product, 1)

    def dve_row(self, dve, j):
        i = j - self.first
        dve.wait_ge(self.product, i + 1)
        if i >= 2:
            if self.is_gate(j - 2):
                dve.wait_ge(self.row_out[i % 2], 32 * self.n_rows(j - 1, i % 2))
            else:
                dve.wait_ge(self.turned, self.n_turned(j - 1))
        dve.tensor_copy(self.row[:, i % 2, :], self.psM[:, i % self.banks, :MOD_W]).then_inc(self.row_ready, 1)

    def pe_turn(self, pe, j, ident):
        i, c = j - self.first, self.n_turned(j)
        pe.wait_ge(self.row_ready, i + 1)
        if c >= 1:
            pe.wait_ge(self.col_ready, c)
        for s in range(2):
            mm = pe.transpose(self.psC[:, s, :], self.row[:, i % 2, s * P:(s + 1) * P], ident)
        mm.then_inc(self.turned, 1)

    def dve_col(self, dve, j):
        c = self.n_turned(j)
        dve.wait_ge(self.turned, c + 1)
        dve.tensor_tensor(self.L.mod[:, 2 * j:2 * j + 2, :], self.psC[:, :, 0:P:P // 2],
                          across(self.L.cols[:, C_BMOD + 2 * j:C_BMOD + 2 * j + 2], 2),
                          ALU.add).then_inc(self.col_ready, 1)

    def store_gate(self, eng, j):
        i = j - self.first
        eng.wait_ge(self.row_ready, i + 1)
        for g in range(2):
            eng.dma_start(self.L.gate_rows[g:g + 1, j * MOD_W:(j + 1) * MOD_W],
                          self.row[g * (P // 2):g * (P // 2) + 1, i % 2, :]).then_inc(self.row_out[i % 2], 16)


def phase_norm1(L):
    nc = L.nc
    with ExitStack() as st:
        norm = NormStage(L, st, "n1", L.hT_hi, L.hT_lo, L.scale1, L.mod[:, 0:KD, :])
        mod = ModStage(L, st, "m1", 0, MOD_EARLY, 2)
        cond = L.sb(st, "cond", [P, KD * 2])
        scond = L.sb(st, "scond", [P, KD * 2])
        c_ld, k_ld, silu, dch = (L.sem(n) for n in ("cond_loaded", "const_loaded", "cond_silu", "n1_dve"))
        block = st.enter_context(nc.Block())

        def x_tile(t):
            if t < NT_LAT:
                return L.dram["x_sample"][t * P:(t + 1) * P, :]
            return L.dram["x_prompt"][(t - NT_LAT) * P:(t - NT_LAT + 1) * P, :]

        @block.sync
        def _(sp):
            sp.dma_start(cond[:], L.dram["cond"]).then_inc(c_ld, 16)
            sp.dma_start(L.const[:], L.dram["const"]).then_inc(k_ld, 16)
            sp.dma_start(L.cols[:], L.dram["cols"]).then_inc(k_ld, 16)
            for t in range(2):
                norm.load(sp, x_tile, t)
            for j in range(MOD_EARLY):
                mod.load(sp, j)
                if j + 2 < NT:
                    norm.load(sp, x_tile, j + 2)

        @block.gpsimd
        def _(pool):
            norm.pool_begin(pool)
            for t in range(NT):
                norm.pool_rstd(pool, t)

        @block.scalar
        def _(act):
            act.wait_ge(c_ld, 16)
            act.activation(scond[:], cond[:], ACT.Silu).then_inc(silu, 1)
            for t in range(NT):
                norm.act_square(act, t)
            act.wait_ge(dch, 2)
            norm.act_modulate(act)

        @block.vector
        def _(dve):
            dve.wait_ge(silu, 1)
            dve.tensor_copy(L.cond_st[:].rearrange("p k (g r) -> p (k g) r", g=2),
                            across(scond[:], P // 2)).then_inc(dch, 1)
            dve.wait_ge(k_ld, 32)
            for i in range(NT + 1):
                if i < MOD_EARLY:
                    mod.dve_row(dve, i)
                norm.dve_step(dve, i)
                if i < MOD_EARLY:
                    mod.dve_col(dve, i)
            dve.wait_ge(mod.col_ready, MOD_EARLY)
            dve.scalar_tensor_tensor(L.scale1[:], L.mod[:, KD:2 * KD, :], 1.0,
                                     across(L.cols[:, C_GPRE:C_GPRE + KD], 2), ALU.add,
                                     ALU.mult).then_inc(dch, 1)
            norm.dve_split(dve)

        @block.tensor
        def _(pe):
            pe.wait_ge(dch, 1)
            pe.wait_ge(k_ld, 32)
            for j in range(MOD_EARLY):
                mod.pe_product(pe, j)
                mod.pe_turn(pe, j, L.ident)
            norm.pe_transposes(pe, L.ident)


def split3(pe, out, w_hi, w_lo, x_hi, x_lo, first, last):
    pe.matmul(out, w_hi, x_hi, start=first, stop=False)
    pe.matmul(out, w_hi, x_lo, start=False, stop=False)
    return pe.matmul(out, w_lo, x_hi, start=False, stop=last)


def phase_in_proj(L):
    nc = L.nc
    with ExitStack() as st:
        raw = L.sb(st, "win_raw", [P, 2, KD, P])
        w_hi = L.sb(st, "win_hi", [P, 2, KD, P], F32R)
        w_lo = L.sb(st, "win_lo", [P, 2, KD, P], F32R)
        conv = L.sb(st, "conv_acc", [P, T])
        stage = L.sb(st, "stage", [P, 2, T])
        mod = ModStage(L, st, "m2", MOD_EARLY, MOD_ALL, 1)
        psP = L.ps(st, "psP", [P, 2, 3, 512])
        loaded = [L.sem(f"win_loaded{i}") for i in range(2)]
        stored = [L.sem(f"stage_stored{i}") for i in range(2)]
        hi_ready, lo_ready, used, drained, conv_ready, conv_read, dch, mod_done = (
            L.sem(n) for n in ("win_hi_ready", "win_lo_ready", "win_used", "proj_drained", "conv_ready",
                               "conv_read", "ip_dve", "mod2_scale"))
        block = st.enter_context(nc.Block())
        last_mod = MOD_ALL - MOD_EARLY

        @block.sync
        def _(sp):
            def load(ct):
                if ct >= 2:
                    sp.wait_ge(lo_ready, ct - 1)
                sp.dma_start(raw[:, ct % 2, :, :], L.dram["w_in"][ct]).then_inc(loaded[ct % 2], 16)

            load(0)
            load(1)
            for ct in range(N_TILES):
                if ct < last_mod:
                    mod.load(sp, MOD_EARLY + ct)
                if ct + 2 < N_TILES:
                    load(ct + 2)

        @block.gpsimd
        def _(pool):
            for ct in range(N_TILES):
                if ct < last_mod and mod.is_gate(MOD_EARLY + ct):
                    mod.store_gate(pool, MOD_EARLY + ct)
                if ct >= FIRST["z"]:
                    i = ct - FIRST["z"]
                    pool.wait_ge(drained, i + 2)
                    pool.dma_start(L.staged[i], stage[:, i % 2, :]).then_inc(stored[i % 2], 16)
            for i in range(2):
                pool.wait_ge(stored[i], 16 * (N_STAGED // 2))
            for i in range(2):
                pool.wait_ge(mod.row_out[i], 32 * mod.n_rows(MOD_ALL, i))

        @block.scalar
        def _(act):
            def split(ct):
                act.wait_ge(loaded[ct % 2], 16 * (ct // 2 + 1))
                if ct >= 2:
                    act.wait_ge(used, ct - 1)
                act.activation(w_hi[:, ct % 2, :, :], raw[:, ct % 2, :, :], ACT.Copy).then_inc(hi_ready, 1)

            split(0)
            for ct, kind in enumerate(TILE_KINDS):
                if ct + 1 < N_TILES:
                    split(ct + 1)
                i = ct - FIRST[kind]
                src = flat(psP[:, ct % 2, :, :])[:, 0:T]
                if kind == "xbc":
                    act.wait_ge(conv_ready, ct + 1)
                    act.activation(L.xbcT[:, i, :], conv[:], ACT.Silu,
                                   bias=L.cols[:, C_CB + i:C_CB + i + 1]).then_inc(conv_read, 1)
                    continue
                act.wait_ge(used, ct + 1)
                if kind == "dt":
                    act.activation(L.dtT[:], src, ACT.Copy).then_inc(drained, 1)
                    continue
                i = ct - FIRST["z"]
                if i >= 2:
                    act.wait_ge(stored[i % 2], 16 * (i // 2))
                act.activation(stage[:, i % 2, :], src, ACT.Silu if kind == "z" else ACT.Copy).then_inc(drained, 1)

        @block.vector
        def _(dve):
            chain = Chain(dve, dch)

            def split(ct):
                dve.wait_ge(hi_ready, ct + 1)
                dve.tensor_tensor(w_lo[:, ct % 2, :, :], raw[:, ct % 2, :, :],
                                  w_hi[:, ct % 2, :, :].bitcast(F32), ALU.subtract).then_inc(lo_ready, 1)

            split(0)
            for ct, kind in enumerate(TILE_KINDS):
                if ct + 1 < N_TILES:
                    split(ct + 1)
                if kind == "xbc":
                    src = flat(psP[:, ct % 2, :, :])
                    tap = [L.cols[:, C_CW + 8 * n + ct:C_CW + 8 * n + ct + 1] for n in range(3)]
                    dve.wait_ge(used, ct + 1)
                    if ct >= 1:
                        dve.wait_ge(conv_read, ct)
                    chain.link(dve.tensor_scalar(conv[:], src[:, 0:T], tap[1], None, ALU.mult))
                    for a, b in ((0, N_LAT), (N_LAT, T)):
                        chain.mark(dve.scalar_tensor_tensor(conv[:, a + 1:b], src[:, a:b - 1], tap[0],
                                                            conv[:, a + 1:b], ALU.mult, ALU.add))
                    chain.wait()
                    for a, b in ((0, N_LAT), (N_LAT, T)):
                        chain.mark(dve.scalar_tensor_tensor(conv[:, a:b - 1], src[:, a + 1:b], tap[2],
                                                            conv[:, a:b - 1], ALU.mult, ALU.add))
                    chain.wait()
                    dve.sem_inc(conv_ready, 1)
                if ct < last_mod:
                    mod.dve_row(dve, MOD_EARLY + ct)
                if 1 <= ct <= last_mod and not mod.is_gate(MOD_EARLY + ct - 1):
                    mod.dve_col(dve, MOD_EARLY + ct - 1)
            dve.wait_ge(mod.col_ready, mod.n_turned(MOD_ALL))
            dve.scalar_tensor_tensor(L.scale2[:], L.mod[:, 4 * KD:5 * KD, :], 1.0,
                                     across(L.cols[:, C_GFFN:C_GFFN + KD], 2), ALU.add,
                                     ALU.mult).then_inc(mod_done, 1)
            dve.wait_ge(mod_done, 1)

        @block.tensor
        def _(pe):
            for ct in range(N_TILES):
                s = ct % 2
                pe.wait_ge(lo_ready, ct + 1)
                if ct >= 2 and ct - 2 < N_XBC:
                    pe.wait_ge(conv_ready, ct - 1)
                elif ct >= 2:
                    pe.wait_ge(drained, ct - 1 - N_XBC)
                for b, (c0, w) in enumerate(BLOCKS):
                    for k in range(KD):
                        mm = split3(pe, psP[:, s, b, :w], w_hi[:, s, k, :], w_lo[:, s, k, :],
                                    L.hT_hi[:, k, c0:c0 + w], L.hT_lo[:, k, c0:c0 + w], k == 0, k == KD - 1)
                mm.then_inc(used, 1)
                if 1 <= ct <= last_mod and not mod.is_gate(MOD_EARLY + ct - 1):
                    mod.pe_turn(pe, MOD_EARLY + ct - 1, L.ident)
                if ct < last_mod:
                    mod.pe_product(pe, MOD_EARLY + ct)


def phase_dt(L):
    nc = L.nc
    with ExitStack() as st:
        v, e, w, lw, r = (L.sb(st, f"dt_{n}", [P, T]) for n in ("v", "e", "w", "lw", "r"))
        keep = L.sb(st, "dt_keep", [P, T])
        tot = L.sb(st, "dt_tot", [P, NT])
        tots = L.sb(st, "dt_tots", [P, 2, NT])
        cd = L.sb(st, "dt_cd", [P, NT])
        cdd = L.sb(st, "dt_cdd", [16, NT, 16])
        expa = L.sb(st, "dt_expa", [P, 1])
        psD = L.ps(st, "psD", [P, 512])
        dve_done, act_done, mm_done, dch = (L.sem(n) for n in ("dt_dve_done", "dt_act_done", "dt_mm", "dt_dve"))
        block = st.enter_context(nc.Block())
        const, cols = L.const, L.cols
        kc = lambda c: const[:, c:c + 1]

        @block.scalar
        def _(act):
            act.activation(expa[:], cols[:, C_ALOG:C_ALOG + 1], ACT.Exp).then_inc(act_done, 1)
            act.wait_ge(dve_done, 1)
            act.activation(e[:], e[:], ACT.Exp).then_inc(act_done, 1)
            act.wait_ge(dve_done, 2)
            act.activation(lw[:], w[:], ACT.Ln).then_inc(act_done, 1)
            act.wait_ge(dve_done, 3)
            act.activation(L.feat[64:96, :], v[64:96, :], ACT.Exp).then_inc(act_done, 1)
            act.activation(r[96:128, :], v[96:128, :], ACT.Exp).then_inc(act_done, 1)
            act.activation(cd[:], tot[:], ACT.Exp).then_inc(act_done, 1)

        @block.vector
        def _(dve):
            c = Chain(dve, dch)
            c.link(dve.tensor_scalar(v[:], L.dtT[:], cols[:, C_DTB:C_DTB + 1], None, ALU.add))
            dve.scalar_tensor_tensor(e[:], v[:], -1.0, v[:], ALU.mult, ALU.min).then_inc(dve_done, 1)
            c.mark(dve.memset(keep[:], 1.0))
            c.wait()
            c.mark(dve.memset(keep[:, 0:T:P], 0.0))
            dve.wait_ge(act_done, 2)
            dve.tensor_scalar(w[:], e[:], 1.0, None, ALU.add).then_inc(dve_done, 1)
            dve.wait_ge(dve_done, 2)
            c.link(dve.tensor_scalar(r[:], w[:], 1.0, 1e-30, ALU.subtract, ALU.max))
            c.link(dve.reciprocal(r[:], r[:]))
            c.link(dve.tensor_tensor(r[:], r[:], e[:], ALU.mult))
            dve.wait_ge(act_done, 3)
            c.link(dve.tensor_tensor(r[:], r[:], lw[:], ALU.mult))
            c.link(dve.scalar_tensor_tensor(w[:], w[:], 1.0, e[:], ALU.is_equal, ALU.mult))
            c.link(dve.tensor_tensor(r[:], r[:], w[:], ALU.add))
            c.link(dve.scalar_tensor_tensor(lw[:], v[:], 0.0, r[:], ALU.max, ALU.add))
            c.mark(dve.tensor_copy(L.feat[32:64, :], lw[32:64, :]))
            c.link(dve.tensor_scalar(e[:], lw[:], expa[:], -1.0, ALU.mult, ALU.mult))
            c.link(dve.tensor_tensor_scan(w[:], keep[:], e[:], 0.0, ALU.mult, ALU.add))
            c.mark(dve.tensor_copy(tot[:], w[:, P - 1:T:P]))
            c.link(dve.tensor_scalar(v[:], w[:], kc(K_SA), None, ALU.mult))
            c.link(dve.scalar_tensor_tensor(r[:], e[:], kc(K_SB), v[:], ALU.mult, ALU.add))
            c.mark(dve.tensor_copy(L.feat[0:32, :], r[0:32, :]))
            c.link(dve.tensor_copy(L.u2[:], r[0:64, :]))
            c.link(dve.tensor_tensor(L.u2[32:64, :], r[32:64, :], L.u2[32:64, :].bitcast(F32), ALU.subtract))
            c.mark(dve.tensor_scalar(tots[:, 0, :], tot[:], kc(K_MT), None, ALU.mult))
            c.link(dve.tensor_scalar(tots[:, 1, :], tot[:], kc(K_MD), None, ALU.mult))
            chunks = lambda ap: ap.rearrange("p (c l) -> p c l", l=P)
            c.mark(dve.tensor_tensor(chunks(v[64:96, :]), chunks(r[64:96, :]), across(tots[64:96, 0, :], P), ALU.add))
            c.mark(dve.tensor_tensor(chunks(v[96:128, :]), across(tots[96:128, 1, :], P), chunks(r[96:128, :]),
                                     ALU.subtract))
            c.wait()
            dve.sem_inc(dve_done, 1)
            dve.wait_ge(act_done, 6)
            c.mark(dve.tensor_tensor(L.feat[96:128, :], r[96:128, :], lw[96:128, :], ALU.mult))
            dve.tensor_tensor(cdd[:], across(cd[0:16, :], 16),
                              const[0:16, K_ID:K_ID + 16].unsqueeze(1).to_broadcast([16, NT, 16]),
                              ALU.mult).then_inc(dve_done, 1)
            sel = const[0:64, K_SEL:K_SEL + 16]
            c.mark(dve.tensor_copy(L.sel[:], across(sel, P)))
            c.mark(dve.tensor_scalar(L.negsel[:], across(sel, P), -1.0, None, ALU.mult))
            for d in range(2):
                c.mark(dve.tensor_copy(L.maskb[:, d, :, :], const[:, K_MASK + d * P:K_MASK + (d + 1) * P]
                                       .unsqueeze(1).to_broadcast([P, 4, P])))
            c.mark(dve.tensor_copy(L.identb[:], L.ident))
            dve.wait_ge(mm_done, 2)
            c.link(dve.tensor_copy(flat(L.cdrow[:]), psD[:, 0:NT * 16]))

        @block.gpsimd
        def _(pool):
            pool.memset(L.ones[:], 1.0).then_inc(mm_done, 1)

        @block.tensor
        def _(pe):
            pe.wait_ge(dve_done, 4)
            pe.wait_ge(mm_done, 1)
            pe.matmul(psD[:, 0:NT * 16], L.ones[0:16, :], flat(cdd[:]), start=True, stop=True).then_inc(mm_done, 1)


def phase_ssm(L):
    nc = L.nc
    with ExitStack() as st:
        xs = L.sb(st, "xs", [P, NT, SW])
        bt = L.sb(st, "bt", [P, NT, 2, DS])
        ft = L.sb(st, "ft", [P, NT, P])
        sb_in = L.sb(st, "sb_in", [P, NT, SW])
        sf = L.sb(st, "sf", [P, 2, SW])
        xw = L.sb(st, "xw", [P, 2, SW])
        tmp = L.sb(st, "s_tmp", [P, SW])
        st_in = L.sb(st, "st_in", [P, 2, 4, DS])
        fin = L.sb(st, "fin", [P, 2, SW])
        fin_t = L.sb(st, "fin_t", [P, 2, 4, DS])
        drow = L.sb(st, "drow", [P, SH])
        seg = L.sb(st, "seg", [P, 16, P])
        cb = L.sb(st, "cb", [P, 2, P])
        wt = L.sb(st, "wt", [P, SH, P])
        yv = L.sb(st, "yv", [P, SW])
        y2 = L.sb(st, "y2", [P, SW])
        zc = L.sb(st, "zc", [P, 2, 4, P])
        ss, ms, rs, nh = (L.sb(st, f"y_{n}", [P, NT] if n != "nh" else [P, 1]) for n in ("ss", "ms", "rs", "nh"))
        ps = [L.ps(st, f"psS{i}", [P, 512]) for i in range(4)]
        psSeg = L.ps(st, "psSeg", [P, 4, 512])
        (st_loaded, d_loaded, turned, t_copied, xw_ready, st_ready, bwd_done, fch, z0, z1, cb_done, cb_read, seg_done,
         exp_done, off_done, zt_done, w_ready, diag_done, y_ready, sq_done, ms_ready, rs_ready, yn_ready, yt_done,
         mix_ready, s_mm, fin_mm, fin_cp, fin_out, xf_ready, sf_ready, pch) = (
            L.sem("ss_" + n) for n in (
                "st_loaded", "d_loaded", "turned", "t_copied", "xw_ready", "st_ready", "bwd_done", "fch", "z0", "z1",
                "cb_done", "cb_read", "seg_done", "exp_done", "off_done", "zt_done", "w_ready", "diag_done",
                "y_ready", "sq_done", "ms_ready", "rs_ready", "yn_ready", "yt_done", "mix_ready", "s_mm", "fin_mm",
                "fin_cp", "fin_out", "xf_ready", "sf_ready", "pch"))
        z_loaded = [z0, z1]
        block = st.enter_context(nc.Block())
        down = list(range(NT_LAT - 1, -1, -1)) + list(range(NT - 1, NT_LAT - 1, -1))
        heads = lambda ap: ap.rearrange("p (h q) -> p h q", q=SP_)
        chunk = lambda c: slice(c * P, (c + 1) * P)

        @block.sync
        def _(sp):
            for d in range(2):
                sp.dma_start(st_in[:, d, :, :], L.dram["state_ssm"][0, 0, d].rearrange("(a h) p n -> (h p) a n", a=4)
                             ).then_inc(st_loaded, 16)
            sp.dma_start(drow[:], L.dram["d_skip"].to_broadcast([P, SH])).then_inc(d_loaded, 16)
            for c in range(NT):
                if c >= 2:
                    sp.wait_ge(zt_done, c - 1)
                sp.dma_start(zc[:, c % 2, :, :], L.staged[0:N_Z].rearrange("a p t -> p a t")[:, :, chunk(c)]
                             ).then_inc(z_loaded[c % 2], 16)
            sp.wait_ge(fin_cp, 2)
            for d in range(2):
                sp.dma_start(L.outs["ssm"][0, 0, d].rearrange("(a h) p n -> (h p) a n", a=4), fin_t[:, d, :, :]
                             ).then_inc(fin_out, 16)
            sp.wait_ge(fin_out, 32)

        @block.gpsimd
        def _(pool):
            pool.memset(nh[:], -0.5).then_inc(pch, 1)
            pool.wait_ge(pch, 1)
            for c in range(NT):
                pool.wait_ge(ms_ready, c + 1)
                pool.tensor_tensor(rs[:, c:c + 1], ms[:, c:c + 1], nh[:], ALU.pow).then_inc(rs_ready, 1)

        @block.scalar
        def _(act):
            for i, c in enumerate(down):
                act.wait_ge(turned, i + 2)
                act.activation(xs[:, c, :], ps[i % 2][:], ACT.Copy).then_inc(t_copied, 1)
            for c in range(NT):
                act.wait_ge(seg_done, c + 1)
                if c >= 1:
                    act.wait_ge(w_ready, c)
                act.activation(flat(seg[:]), flat(psSeg[:]), ACT.Exp).then_inc(exp_done, 1)
                act.wait_ge(y_ready, c + 1)
                act.activation(y2[:], yv[:], ACT.Square, accum_out=ss[:, c:c + 1]).then_inc(sq_done, 1)
                act.wait_ge(rs_ready, c + 1)
                act.wait_ge(sq_done, c + 1)
                act.activation(y2[:], yv[:], ACT.Copy, scale=rs[:, c:c + 1]).then_inc(yn_ready, 1)

        @block.vector
        def _(dve):
            f = Chain(dve, fch)
            dve.wait_ge(turned, 1)
            dve.tensor_copy(sb_in[:, down[0], :], ps[2][:]).then_inc(st_ready, 1)
            f.mark(dve.tensor_copy(sf[:, 0, :], ps[3][:]))
            f.mark(dve.memset(sb_in[:, NT - 1, :], 0.0))
            for i, c in enumerate(down):
                dve.wait_ge(turned, i + 2)
                f.mark(dve.tensor_copy(bt[:, c, :, :], ps[2 + i % 2][:, 0:2 * DS].rearrange("p (g n) -> p g n", g=2)))
                dve.tensor_copy(ft[:, c, :], ps[2 + i % 2][:, 2 * DS:2 * DS + P]).then_inc(bwd_done, 1)
                dve.wait_ge(bwd_done, i + 1)
                f.wait()
                dve.wait_ge(t_copied, i + 1)
                if i >= 2:
                    dve.wait_ge(s_mm, i - 1)
                dve.tensor_tensor(heads(xw[:, i % 2, :]), heads(xs[:, c, :]), across(ft[:, c, 104:112], SP_),
                                  ALU.mult).then_inc(xw_ready, 1)
                last_lat, last_pr = c == 0, c == NT_LAT
                dve.wait_ge(s_mm, i + 1)
                if last_lat:
                    dve.sem_inc(st_ready, 1)
                    continue
                f.link(dve.tensor_tensor(heads(tmp[:]), heads(sb_in[:, c, :]), across(L.cdrow[:, c, 8:16], SP_),
                                         ALU.mult))
                dst = fin[:, 1, :] if last_pr else sb_in[:, c - 1, :]
                f.link(dve.tensor_tensor(dst, tmp[:], psSeg[:, i % 2, :], ALU.add))
                dve.sem_inc(st_ready, 1)
            for c in range(NT):
                p0, p1, p2, p3 = ps
                cur, nxt = c % 2, 1 - c % 2
                if c == NT_LAT:
                    f.link(dve.memset(sf[:, cur, :], 0.0))
                    dve.sem_inc(sf_ready, 1)
                if c >= 1:
                    dve.wait_ge(s_mm, NT + c)
                dve.tensor_tensor(heads(xw[:, 0, :]), heads(xs[:, c, :]), across(ft[:, c, 96:104], SP_),
                                  ALU.mult).then_inc(xf_ready, 1)
                dve.wait_ge(cb_done, c + 1)
                f.link(dve.tensor_copy(flat(cb[:]), p0[:, 0:2 * P]))
                dve.sem_inc(cb_read, 1)
                dve.wait_ge(exp_done, c + 1)
                if c >= 1:
                    dve.wait_ge(diag_done, c)
                for h in range(SH):
                    f.mark(dve.scalar_tensor_tensor(wt[:, h, :], seg[:, h, :], ft[:, c, 32 + h:33 + h],
                                                    cb[:, h // 4, :], ALU.mult, ALU.mult))
                for h in range(SH):
                    f.mark(dve.scalar_tensor_tensor(seg[:, SH + h, :], seg[:, SH + h, :],
                                                    ft[:, c, 40 + h:41 + h], cb[:, h // 4, :], ALU.mult, ALU.mult))
                f.wait()
                dve.tensor_tensor(wt[:], wt[:], seg[:, SH:2 * SH, :], ALU.add).then_inc(w_ready, 1)
                dve.wait_ge(off_done, c + 1)
                if c >= 1:
                    dve.wait_ge(yn_ready, c)
                f.mark(dve.tensor_tensor(heads(yv[:]), heads(p1[:]), across(ft[:, c, 64:72], SP_), ALU.mult))
                f.link(dve.tensor_tensor(heads(tmp[:]), heads(p2[:]), across(ft[:, c, 72:80], SP_), ALU.mult))
                f.link(dve.tensor_tensor(yv[:], yv[:], tmp[:], ALU.add))
                if c == 0:
                    dve.wait_ge(d_loaded, 16)
                f.link(dve.tensor_tensor(heads(tmp[:]), heads(xs[:, c, :]), across(drow[:], SP_), ALU.mult))
                f.link(dve.tensor_tensor(yv[:], yv[:], tmp[:], ALU.add))
                dve.wait_ge(s_mm, NT + c + 1)
                if c != NT_LAT - 1:
                    f.link(dve.tensor_tensor(heads(tmp[:]), heads(sf[:, cur, :]), across(L.cdrow[:, c, 0:8], SP_),
                                             ALU.mult))
                    dst = fin[:, 0, :] if c == NT - 1 else sf[:, nxt, :]
                    f.link(dve.tensor_tensor(dst, tmp[:], psSeg[:, 0, :], ALU.add))
                dve.sem_inc(sf_ready, 1)
                dve.wait_ge(diag_done, c + 1)
                f.link(dve.tensor_tensor(yv[:], yv[:], p3[:], ALU.add))
                f.link(dve.tensor_tensor(yv[:], yv[:], p0[:], ALU.mult))
                dve.sem_inc(y_ready, 1)
                dve.wait_ge(sq_done, c + 1)
                dve.tensor_scalar(ms[:, c:c + 1], ss[:, c:c + 1], 1.0 / SW, EPS, ALU.mult, ALU.add
                                  ).then_inc(ms_ready, 1)
                dve.wait_ge(yt_done, c + 1)
                dve.tensor_tensor(L.mixS[:, :, chunk(c)], psSeg[:, 1, :].rearrange("p (a t) -> p a t", a=4),
                                  across(L.cols[:, C_GS:C_GS + 4], P), ALU.mult).then_inc(mix_ready, 1)
            for d in range(2):
                dve.wait_ge(fin_mm, d + 1)
                dve.tensor_copy(fin_t[:, d, :, :], ps[1 + d][:].rearrange("p (a n) -> p a n", a=4)).then_inc(fin_cp, 1)

        @block.tensor
        def _(pe):
            pe.wait_ge(st_loaded, 32)
            for a in range(4):
                pe.transpose(ps[2][:, chunk(a)], st_in[:, 1, a, :], L.ident)
            for a in range(4):
                mm = pe.transpose(ps[3][:, chunk(a)], st_in[:, 0, a, :], L.ident)
            mm.then_inc(turned, 1)

            def turn(i):
                c = down[i]
                if i >= 2:
                    pe.wait_ge(t_copied, i - 1)
                    pe.wait_ge(bwd_done, i - 1)
                elif i == 0:
                    pe.wait_ge(st_ready, 1)
                else:
                    pe.wait_ge(fch, 1)
                for a in range(4):
                    pe.transpose(ps[i % 2][:, chunk(a)], L.xbcT[:, a, chunk(c)], L.ident)
                for g in range(2):
                    pe.transpose(ps[2 + i % 2][:, chunk(g)], L.xbcT[:, 4 + g, chunk(c)], L.ident)
                pe.transpose(ps[2 + i % 2][:, chunk(2)], L.feat[:, chunk(c)], L.ident).then_inc(turned, 1)

            def contribution(c, src, dst, ready, n):
                pe.wait_ge(ready, n)
                for g in range(2):
                    mm = pe.matmul(dst[:, g * 256:(g + 1) * 256], bt[:, c, g, :], src[:, g * 256:(g + 1) * 256],
                                   start=True, stop=True)
                mm.then_inc(s_mm, 1)

            turn(0)
            for i, c in enumerate(down):
                if i + 1 < NT:
                    turn(i + 1)
                if i >= 2:
                    pe.wait_ge(st_ready, i)
                contribution(c, xw[:, i % 2, :], psSeg[:, i % 2, :], xw_ready, i + 1)

            pe.wait_ge(st_ready, NT + 1)
            for c in range(NT):
                if c >= 1:
                    pe.wait_ge(y_ready, c)
                for g in range(2):
                    mm = pe.matmul(ps[0][:, chunk(g)], L.xbcT[:, 4 + g, chunk(c)], L.xbcT[:, 6 + g, chunk(c)],
                                   start=True, stop=True)
                mm.then_inc(cb_done, 1)
                if c >= 1:
                    pe.wait_ge(mix_ready, c)
                for q in range(4):
                    pe.matmul(psSeg[:, q, :], L.u2[:, chunk(c)], flat(L.negsel[:, 4 * q:4 * q + 4, :]),
                              start=True, stop=False)
                    pe.matmul(psSeg[:, q, :], L.identb[:], flat(L.maskb[:, q // 2, :, :]), start=False, stop=False)
                    for h in range(4):
                        mm = pe.matmul(psSeg[:, q, chunk(h)], L.sel[:, 4 * q + h, :], L.u2[:, chunk(c)],
                                       start=False, stop=(h == 3))
                mm.then_inc(seg_done, 1)
                pe.wait_ge(sf_ready, c + (c >= NT_LAT)) if c else None
                for d, state in ((0, sf[:, c % 2, :]), (1, sb_in[:, c, :])):
                    for g in range(2):
                        mm = pe.matmul(ps[1 + d][:, g * 256:(g + 1) * 256], L.xbcT[:, 6 + g, chunk(c)],
                                       state[:, g * 256:(g + 1) * 256], start=True, stop=True)
                mm.then_inc(off_done, 1)
                pe.wait_ge(exp_done, c + 1)
                contribution(c, xw[:, 0, :], psSeg[:, 0, :], xf_ready, c + 1)
                pe.wait_ge(cb_read, c + 1)
                pe.wait_ge(z_loaded[c % 2], 16 * (c // 2 + 1))
                for a in range(4):
                    mm = pe.transpose(ps[0][:, chunk(a)], zc[:, c % 2, a, :], L.ident)
                mm.then_inc(zt_done, 1)
                pe.wait_ge(w_ready, c + 1)
                for h in range(SH):
                    mm = pe.matmul(ps[3][:, h * SP_:(h + 1) * SP_], wt[:, h, :], xs[:, c, h * SP_:(h + 1) * SP_],
                                   start=True, stop=True)
                mm.then_inc(diag_done, 1)
                pe.wait_ge(yn_ready, c + 1)
                for a in range(4):
                    mm = pe.transpose(psSeg[:, 1, chunk(a)], y2[:, chunk(a)], L.ident)
                mm.then_inc(yt_done, 1)
            pe.wait_ge(mix_ready, NT)
            for d in range(2):
                for a in range(4):
                    mm = pe.transpose(ps[1 + d][:, chunk(a)], fin[:, d, chunk(a)], L.ident)
                mm.then_inc(fin_mm, 1)


def phase_attn_prep(L):
    nc = L.nc
    with ExitStack() as st:
        qT = L.sb(st, "qT", [P, KQ, T])
        kvT = L.sb(st, "kvT", [P, KKV, T])
        ropeT = L.sb(st, "ropeT", [P, T])
        sq = L.sb(st, "sq", [P, KQ, T])
        rstd = L.sb(st, "bc_rstd", [P, 2, T])
        ckv = L.sb(st, "ckv", [P, KKV, NKEY])
        prod = L.sb(st, "rope_prod", [P, T])
        cc = L.sb(st, "cache_in", [P, 2, KV_LORA])
        cr = L.sb(st, "cachek_in", [P, 2, 2, ROPE])
        co = L.sb(st, "ckv_out", [P, 2, KV_LORA])
        ko = L.sb(st, "krope_out", [P, 2, ROPE])
        eps = L.sb(st, "eps", [P, 1])
        ps3 = L.ps(st, "ps3", [P, 3, 512])
        ps3b = L.ps(st, "ps3b", [P, 3, 512])
        psT = L.ps(st, "psT", [P, 2, 512])
        (c_loaded, t_loaded, q_loaded, kv_loaded, r_loaded, sq_done, sums, ms_ready, root, dch, turned, prod_ready, fold, ro_ready, out_ready,
         out_done, ones_rd) = (L.sem("ap_" + n) for n in (
             "c_loaded", "t_loaded", "q_loaded", "kv_loaded", "r_loaded", "sq_done", "sums", "ms_ready", "root", "dch", "turned", "prod_ready", "fold",
             "ro_ready", "out_ready", "out_done", "eps_ready"))
        block = st.enter_context(nc.Block())
        tok = lambda ap: flat(ap)[:, 0:T]

        @block.sync
        def _(sp):
            sp.dma_start(qT[:], L.staged[N_Z:N_Z + KQ].rearrange("a p t -> p a t")).then_inc(q_loaded, 16)
            sp.dma_start(kvT[:], L.staged[N_Z + KQ:N_Z + KQ + KKV].rearrange("a p t -> p a t")).then_inc(kv_loaded, 16)
            sp.dma_start(ropeT[:], L.staged[N_STAGED - 1]).then_inc(r_loaded, 16)
            sp.dma_start(L.table[:], L.dram["rope_table"]).then_inc(t_loaded, 16)
            sp.dma_start(cc[:], L.dram["cache_ckv"][0, 0].rearrange("(a p) n -> p a n", p=P)).then_inc(c_loaded, 16)
            for r in range(2):
                sp.dma_start(cr[:, :, r, :], L.dram["cache_krope"][0, 0].rearrange("(a p) n -> p a n", p=P)
                             ).then_inc(c_loaded, 16)
            sp.wait_ge(out_ready, 2)
            sp.dma_start(L.outs["ckv"][0, 0].rearrange("(a p) n -> p a n", p=P), co[:]).then_inc(out_done, 16)
            sp.dma_start(L.outs["krope"][0, 0].rearrange("(a p) n -> p a n", p=P), ko[:]).then_inc(out_done, 16)
            sp.wait_ge(out_done, 32)

        @block.gpsimd
        def _(pool):
            pool.memset(eps[:], EPS).then_inc(ones_rd, 1)

        @block.scalar
        def _(act):
            act.wait_ge(q_loaded, 16)
            act.activation(sq[:], qT[:], ACT.Square).then_inc(sq_done, 1)
            act.wait_ge(sums, 1)
            act.wait_ge(kv_loaded, 16)
            act.activation(sq[:, 0:KKV, :], kvT[:], ACT.Square).then_inc(sq_done, 1)
            act.wait_ge(ones_rd, 1)
            act.activation(rstd[:, 0, :], tok(ps3[:]), ACT.Sqrt, bias=eps[:], scale=1.0 / Q_LORA).then_inc(root, 1)
            act.wait_ge(sums, 2)
            act.activation(rstd[:, 1, :], tok(ps3b[:]), ACT.Sqrt, bias=eps[:], scale=1.0 / KV_LORA).then_inc(root, 1)

        @block.vector
        def _(dve):
            c = Chain(dve, dch)
            dve.wait_ge(t_loaded, 16)
            dve.wait_ge(r_loaded, 16)
            dve.tensor_tensor(prod[:], ropeT[:], L.table[:], ALU.mult).then_inc(prod_ready, 1)
            dve.wait_ge(turned, 1)
            c.mark(dve.tensor_copy(ckv[:, :, T:NKEY], psT[:, 0, :].rearrange("p (k t) -> p k t", k=2)))
            c.mark(dve.tensor_copy(L.kr_hi[:, T:NKEY], psT[:, 1, 0:N_CACHE]))
            c.wait()
            c.mark(dve.tensor_tensor(L.kr_lo[:, T:NKEY], psT[:, 1, 0:N_CACHE], L.kr_hi[:, T:NKEY].bitcast(F32),
                                     ALU.subtract))
            dve.tensor_copy(ko[:], psT[:, 1, 256:512].rearrange("p (a n) -> p a n", a=2)[:, :, 0:ROPE]
                            ).then_inc(out_ready, 1)
            dve.wait_ge(root, 1)
            dve.wait_ge(q_loaded, 16)
            c.link(dve.reciprocal(rstd[:, 0, :], rstd[:, 0, :]))
            for k in range(KQ):
                c.link(dve.scalar_tensor_tensor(qT[:, k, :], qT[:, k, :], L.cols[:, C_GQ + k:C_GQ + k + 1],
                                                rstd[:, 0, :], ALU.mult, ALU.mult))
                c.link(dve.tensor_copy(L.qn_hi[:, k, :], qT[:, k, :]))
                c.mark(dve.tensor_tensor(L.qn_lo[:, k, :], qT[:, k, :], L.qn_hi[:, k, :].bitcast(F32), ALU.subtract))
            dve.wait_ge(root, 2)
            dve.wait_ge(kv_loaded, 16)
            c.link(dve.reciprocal(rstd[:, 1, :], rstd[:, 1, :]))
            for k in range(KKV):
                c.mark(dve.scalar_tensor_tensor(ckv[:, k, 0:T], kvT[:, k, :], L.cols[:, C_GKV + k:C_GKV + k + 1],
                                                rstd[:, 1, :], ALU.mult, ALU.mult))
            c.wait()
            dve.sem_inc(prod_ready, 1)
            c.link(dve.tensor_copy(L.ckv_hi[:], ckv[:]))
            c.mark(dve.tensor_tensor(L.ckv_lo[:], ckv[:], L.ckv_hi[:].bitcast(F32), ALU.subtract))
            dve.wait_ge(fold, 1)
            c.link(dve.tensor_copy(L.kr_hi[:, 0:T], tok(ps3[:])))
            c.mark(dve.tensor_tensor(L.kr_lo[:, 0:T], tok(ps3[:]), L.kr_hi[:, 0:T].bitcast(F32), ALU.subtract))
            dve.wait_ge(turned, 2)
            dve.tensor_copy(co[:], psT[:, 0, :].rearrange("p (a n) -> p a n", a=2)).then_inc(out_ready, 1)
            c.wait()

        @block.tensor
        def _(pe):
            pe.wait_ge(c_loaded, 48)
            pe.wait_ge(r_loaded, 16)
            for k in range(2):
                for a in range(2):
                    pe.transpose(psT[:, 0, (2 * k + a) * P:(2 * k + a + 1) * P], cc[:, a, k * P:(k + 1) * P], L.ident)
            for a in range(2):
                pe.transpose(psT[:, 1, a * P:(a + 1) * P], cr[:, a, :, :], L.ident)
            for a in range(2):
                mm = pe.transpose(psT[:, 1, (2 + a) * P:(3 + a) * P], ropeT[:, N_LAT + a * P:N_LAT + (a + 1) * P],
                                  L.ident)
            mm.then_inc(turned, 1)
            for i, (kn, ps) in enumerate(((KQ, ps3), (KKV, ps3b))):
                pe.wait_ge(sq_done, i + 1)
                for b, (c0, w) in enumerate(BLOCKS):
                    for k in range(kn):
                        mm = pe.matmul(ps[:, b, :w], L.ones[:], sq[:, k, c0:c0 + w], start=(k == 0), stop=(k == kn - 1))
                mm.then_inc(sums, 1)
            pe.wait_ge(prod_ready, 1)
            pe.wait_ge(root, 1)
            for b, (c0, w) in enumerate(BLOCKS):
                mm = pe.matmul(ps3[:, b, :w], L.fold, prod[:, c0:c0 + w], start=True, stop=True)
            mm.then_inc(fold, 1)
            pe.wait_ge(prod_ready, 2)
            pe.wait_ge(dch, 1)
            for a in range(2):
                for k in range(2):
                    mm = pe.transpose(psT[:, 0, (2 * a + k) * P:(2 * a + k + 1) * P],
                                      ckv[:, k, N_LAT + a * P:N_LAT + (a + 1) * P], L.ident)
            mm.then_inc(turned, 1)


def phase_attention(L):
    nc = L.nc
    with ExitStack() as st:
        wq_raw = L.sb(st, "wq_raw", [P, KQ, 256])
        wk_raw = L.sb(st, "wk_raw", [P, KKV, 256])
        wq_hi, wq_lo = (L.sb(st, f"wq_{n}", [P, KQ, 256], F32R) for n in ("hi", "lo"))
        wk_hi, wk_lo = (L.sb(st, f"wk_{n}", [P, KKV, 256], F32R) for n in ("hi", "lo"))
        kn_hi, kn_lo = (L.sb(st, f"kn_{n}", [P, NKEY], F32R) for n in ("hi", "lo"))
        v_hi, v_lo = (L.sb(st, f"v_{n}", [P, NKEY], F32R) for n in ("hi", "lo"))
        q_hi, q_lo = (L.sb(st, f"q_{n}", [P, T], F32R) for n in ("hi", "lo"))
        qr = L.sb(st, "q_rope", [P, T], F32R)
        prod = L.sb(st, "q_prod", [P, T])
        prob = L.sb(st, "prob", [P, 2, T])
        pt_hi, pt_lo = (L.sb(st, f"pt_{n}", [P, 2, T], F32R) for n in ("hi", "lo"))
        mx, nm, sm, rc = (L.sb(st, f"sm_{n}", [P, HEADS * NT]) for n in ("mx", "nm", "sum", "rec"))
        psS = L.ps(st, "psScore", [P, 5, 512])
        psPT = L.ps(st, "psPT", [P, 2, 512])
        psO = L.ps(st, "psO", [P, P])
        (wl, w_hi_r, w_split, proj, drained, hi_done, prod_ready, head_ready, score, m_ready, nm_ready, e_ready,
         p_ready, pt_done, pth_ready, ptl_ready, pv, o_read, dch) = (L.sem("at_" + n) for n in (
             "wl", "w_hi", "w_split", "proj", "drained", "hi_done", "prod_ready", "head_ready", "score", "m_ready",
             "nm_ready", "e_ready", "p_ready", "pt_done", "pth_ready", "ptl_ready", "pv", "o_read", "dch"))
        block = st.enter_context(nc.Block())
        S = flat(psS[:])
        units = [(h, t) for h in range(HEADS) for t in range(NT)]
        key_tiles = lambda t: list(range(NT_LAT, NT)) if t >= NT_LAT else list(range(NT_LAT)) + [NT, NT + 1]
        groups = lambda t: [list(range(g, min(g + 4, len(key_tiles(t))))) for g in range(0, len(key_tiles(t)), 4)]
        n_groups = lambda u: sum(len(groups(units[i][1])) for i in range(u))
        width = lambda t: len(key_tiles(t)) * P

        def pieces(u):
            t, base = units[u][1], T * (u % 2)
            if t >= NT_LAT:
                return [(base, N_LAT, N_PROMPT)]
            if base == 0:
                return [(0, 0, 512), (512, 512, 512), (1024, T, N_CACHE)]
            return [(1536, 0, 512), (2048, 512, 512), (1280, T, N_CACHE)]

        def tile_col(u, i):
            kt = key_tiles(units[u][1])[i]
            for col, k0, w in pieces(u):
                if k0 <= kt * P < k0 + w:
                    return col - T * (u % 2) + kt * P - k0
            raise ValueError(i)

        N_PROJ = 5

        @block.sync
        def _(sp):
            for h in range(HEADS):
                if h >= 1:
                    sp.wait_ge(w_split, h)
                sp.dma_start(wq_raw[:], L.dram["w_uq"][h]).then_inc(wl, 16)
                sp.dma_start(wk_raw[:], L.dram["w_ukv"].rearrange("(k p) n -> p k n", p=P)[:, :, h * 256:(h + 1) * 256]
                             ).then_inc(wl, 16)

        @block.scalar
        def _(act):
            def split(h):
                act.wait_ge(wl, 32 * (h + 1))
                if h >= 1:
                    act.wait_ge(proj, N_PROJ * h)
                act.activation(wq_hi[:], wq_raw[:], ACT.Copy).then_inc(w_hi_r, 1)
                act.activation(wk_hi[:], wk_raw[:], ACT.Copy).then_inc(w_hi_r, 1)

            def head_setup(h):
                act.wait_ge(proj, N_PROJ * h + 2)
                act.activation(kn_hi[:], S[:, 0:NKEY], ACT.Copy).then_inc(hi_done, 1)
                act.wait_ge(proj, N_PROJ * h + 3)
                act.activation(v_hi[:], S[:, 0:NKEY], ACT.Copy).then_inc(hi_done, 1)
                act.wait_ge(proj, N_PROJ * h + 4)
                act.activation(q_hi[:], S[:, 0:T], ACT.Copy).then_inc(hi_done, 1)

            def exp(u):
                w, base = width(units[u][1]), T * (u % 2)
                act.wait_ge(nm_ready, u + 1)
                act.activation(prob[:, u % 2, 0:w], S[:, base:base + w], ACT.Exp, bias=nm[:, u:u + 1], scale=SCALE,
                               accum_out=sm[:, u:u + 1]).then_inc(e_ready, 1)

            def pt(u):
                g0, c0 = n_groups(u), 0
                for i, g in enumerate(groups(units[u][1])):
                    w = len(g) * P
                    act.wait_ge(pt_done, g0 + i + 1)
                    if u >= 2:
                        act.wait_ge(pv, u - 1)
                    act.activation(pt_hi[:, u % 2, c0:c0 + w], psPT[:, (g0 + i) % 2, 0:w], ACT.Copy
                                   ).then_inc(pth_ready, 1)
                    c0 += w

            def out(u):
                h, t = units[u]
                act.wait_ge(pv, u + 1)
                act.activation(L.mixA[:, h, t * P:(t + 1) * P], psO[:], ACT.Copy).then_inc(o_read, 1)

            split(0)
            for h in range(HEADS):
                head_setup(h)
                for t in range(NT):
                    u = h * NT + t
                    if t >= 1:
                        pt(u - 1)
                    exp(u)
                    if t >= 2:
                        out(u - 2)
                pt(u)
                out(u - 1)
                out(u)
                if h + 1 < HEADS:
                    split(h + 1)

        @block.vector
        def _(dve):
            c = Chain(dve, dch)

            def split(h):
                dve.wait_ge(w_hi_r, 2 * h + 2)
                c.mark(dve.tensor_tensor(wq_lo[:], wq_raw[:], wq_hi[:].bitcast(F32), ALU.subtract))
                c.link(dve.tensor_tensor(wk_lo[:], wk_raw[:], wk_hi[:].bitcast(F32), ALU.subtract))
                dve.sem_inc(w_split, 1)

            def head_setup(h):
                dve.wait_ge(proj, N_PROJ * h + 1)
                dve.tensor_tensor(prod[:], S[:, 0:T], L.table[:], ALU.mult).then_inc(prod_ready, 1)
                dve.wait_ge(hi_done, 3 * h + 1)
                dve.tensor_tensor(kn_lo[:], S[:, 0:NKEY], kn_hi[:].bitcast(F32), ALU.subtract).then_inc(drained, 1)
                dve.wait_ge(hi_done, 3 * h + 2)
                dve.tensor_tensor(v_lo[:], S[:, 0:NKEY], v_hi[:].bitcast(F32), ALU.subtract).then_inc(drained, 1)
                dve.wait_ge(hi_done, 3 * h + 3)
                dve.tensor_tensor(q_lo[:], S[:, 0:T], q_hi[:].bitcast(F32), ALU.subtract).then_inc(drained, 1)
                dve.wait_ge(proj, N_PROJ * h + 5)
                c.link(dve.tensor_copy(qr[:], S[:, 0:T]))
                dve.tensor_tensor(qr[64:128, :], S[64:128, 0:T], qr[64:128, :].bitcast(F32), ALU.subtract
                                  ).then_inc(head_ready, 1)

            def maximum(u):
                w, base = width(units[u][1]), T * (u % 2)
                dve.wait_ge(score, u + 1)
                dve.tensor_reduce(mx[:, u:u + 1], S[:, base:base + w], AX_X, ALU.max).then_inc(m_ready, 1)
                dve.wait_ge(m_ready, u + 1)
                dve.tensor_scalar(nm[:, u:u + 1], mx[:, u:u + 1], -SCALE, None, ALU.mult).then_inc(nm_ready, 1)

            def normalise(u):
                w = width(units[u][1])
                dve.wait_ge(e_ready, u + 1)
                c.link(dve.reciprocal(rc[:, u:u + 1], sm[:, u:u + 1]))
                dve.tensor_scalar(prob[:, u % 2, 0:w], prob[:, u % 2, 0:w], rc[:, u:u + 1], None, ALU.mult
                                  ).then_inc(p_ready, 1)

            def pt(u):
                g0, c0 = n_groups(u), 0
                for i, g in enumerate(groups(units[u][1])):
                    w = len(g) * P
                    dve.wait_ge(pth_ready, g0 + i + 1)
                    dve.tensor_tensor(pt_lo[:, u % 2, c0:c0 + w], psPT[:, (g0 + i) % 2, 0:w],
                                      pt_hi[:, u % 2, c0:c0 + w].bitcast(F32), ALU.subtract).then_inc(ptl_ready, 1)
                    c0 += w

            split(0)
            for h in range(HEADS):
                head_setup(h)
                for t in range(NT):
                    u = h * NT + t
                    if t >= 1:
                        pt(u - 1)
                    maximum(u)
                    normalise(u)
                pt(u)
                if h + 1 < HEADS:
                    split(h + 1)

        @block.tensor
        def _(pe):
            def head_setup(h):
                pe.wait_ge(w_split, h + 1)
                if h >= 1:
                    pe.wait_ge(e_ready, h * NT)
                def channel_major(kn, cols, w_hi, w_lo, x_hi, x_lo, blocks):
                    for b, (c0, w) in enumerate(blocks):
                        for k in range(kn):
                            mm = split3(pe, psS[:, b, :w], w_hi[:, k, cols], w_lo[:, k, cols], x_hi[:, k, c0:c0 + w],
                                        x_lo[:, k, c0:c0 + w], k == 0, k == kn - 1)
                    mm.then_inc(proj, 1)

                channel_major(KQ, slice(128, 256), wq_hi, wq_lo, L.qn_hi, L.qn_lo, BLOCKS)
                pe.wait_ge(prod_ready, h + 1)
                channel_major(KKV, slice(0, 128), wk_hi, wk_lo, L.ckv_hi, L.ckv_lo, [(0, 512), (512, 512), (1024, 512)])
                pe.wait_ge(drained, 3 * h + 1)
                for kt in range(NKEY // P):
                    for k in range(KKV):
                        out = S[:, kt * P:(kt + 1) * P]
                        c_hi, c_lo = (x[:, k, kt * P:(kt + 1) * P] for x in (L.ckv_hi, L.ckv_lo))
                        mm = split3(pe, out, c_hi, c_lo, wk_hi[:, k, 128:256], wk_lo[:, k, 128:256], k == 0,
                                    k == KKV - 1)
                mm.then_inc(proj, 1)
                pe.wait_ge(drained, 3 * h + 2)
                channel_major(KQ, slice(0, 128), wq_hi, wq_lo, L.qn_hi, L.qn_lo, BLOCKS)
                pe.wait_ge(drained, 3 * h + 3)
                for b, (c0, w) in enumerate(BLOCKS):
                    mm = pe.matmul(psS[:, b, :w], L.fold, prod[:, c0:c0 + w], start=True, stop=True)
                mm.then_inc(proj, 1)
                pe.wait_ge(head_ready, h + 1)

            def scores(u, part):
                t, shared = units[u][1], pieces(u)[-1:]
                if len(pieces(u)) == 1 and u % 2 == 0:
                    shared = []
                todo = shared if part else pieces(u)[:len(pieces(u)) - len(shared)]
                if u % NT >= 1 + (part == 0):
                    pe.wait_ge(e_ready, u - 1 + part)
                q = slice(t * P, (t + 1) * P)
                for col, k0, w in todo:
                    out, ks = S[:, col:col + w], slice(k0, k0 + w)
                    pe.matmul(out, q_hi[:, q], kn_hi[:, ks], start=True, stop=False)
                    pe.matmul(out, q_hi[:, q], kn_lo[:, ks], start=False, stop=False)
                    pe.matmul(out, q_lo[:, q], kn_hi[:, ks], start=False, stop=False)
                    pe.matmul(out, qr[:, q], L.kr_hi[:, ks], start=False, stop=False)
                    mm = pe.matmul(out, qr[:, q], L.kr_lo[:, ks], start=False, stop=True)
                    if (col, k0, w) == pieces(u)[-1]:
                        mm.then_inc(score, 1)

            def transposes(u):
                g0 = n_groups(u)
                pe.wait_ge(p_ready, u + 1)
                for i, g in enumerate(groups(units[u][1])):
                    if g0 + i >= 2:
                        pe.wait_ge(ptl_ready, g0 + i - 1)
                    for n, kt in enumerate(g):
                        mm = pe.transpose(psPT[:, (g0 + i) % 2, n * P:(n + 1) * P],
                                          prob[:, u % 2, tile_col(u, kt):tile_col(u, kt) + P], L.ident)
                    mm.then_inc(pt_done, 1)

            def values(u):
                kts = key_tiles(units[u][1])
                if u >= 1:
                    pe.wait_ge(o_read, u)
                g0, n = n_groups(u), 0
                for i, g in enumerate(groups(units[u][1])):
                    pe.wait_ge(ptl_ready, g0 + i + 1)
                    for j in g:
                        vs, pc = slice(kts[j] * P, (kts[j] + 1) * P), slice(j * P, (j + 1) * P)
                        mm = split3(pe, psO[:], v_hi[:, vs], v_lo[:, vs], pt_hi[:, u % 2, pc],
                                    pt_lo[:, u % 2, pc], n == 0, n == len(kts) - 1)
                        n += 1
                mm.then_inc(pv, 1)

            for h in range(HEADS):
                head_setup(h)
                for t in range(NT):
                    u = h * NT + t
                    scores(u, 0)
                    if t >= 1:
                        transposes(u - 1)
                    scores(u, 1)
                    if t >= 2:
                        values(u - 2)
                transposes(u)
                values(u - 1)
                values(u)


class GateRows:

    def __init__(self, L, st, tag, part, g_post):
        self.L, self.part, self.g_post = L, part, g_post
        self.rows = L.sb(st, f"{tag}_rows", [P, 2, D])
        self.b = L.sb(st, f"{tag}_b", [P, D])
        self.g = L.sb(st, f"{tag}_g", [P, D])
        self.loaded, self.ready = L.sem(f"{tag}_g_loaded"), L.sem(f"{tag}_g_ready")

    def load(self, eng):
        c = slice(self.part * D, (self.part + 1) * D)
        for g in range(2):
            eng.dma_start(self.rows[:, g, :], self.L.gate_rows[g:g + 1, c].to_broadcast([P, D])
                          ).then_inc(self.loaded, 16)
        eng.dma_start(self.b[:], self.L.dram["b_mod"][:, c].to_broadcast([P, D])).then_inc(self.loaded, 16)
        eng.dma_start(self.g[:], self.L.dram[self.g_post].to_broadcast([P, D])).then_inc(self.loaded, 16)

    def dve(self, dve):
        dve.wait_ge(self.loaded, 64)
        for g in range(2):
            dve.tensor_tensor(self.rows[:, g, :], self.rows[:, g, :], self.b[:], ALU.add).then_inc(self.ready, 1)
            dve.wait_ge(self.ready, 2 * g + 1)
            dve.tensor_tensor(self.rows[:, g, :], self.rows[:, g, :], self.g[:], ALU.mult).then_inc(self.ready, 1)
        dve.wait_ge(self.ready, 4)


def phase_out_proj(L):
    nc = L.nc
    with ExitStack() as st:
        raw = L.sb(st, "wo_raw", [P, 2, D])
        w_hi, w_lo = (L.sb(st, f"wo_{n}", [P, KD, D], F32R) for n in ("hi", "lo"))
        m_hi, m_lo = (L.sb(st, f"mix_{n}", [P, 2, KD, P], F32R) for n in ("hi", "lo"))
        xin = L.sb(st, "op_x", [P, 2, D])
        y = L.sb(st, "op_y", [P, 2, D])
        junk = L.sb(st, "op_sq", [P, D])
        ss, ms, rs, nh = (L.sb(st, f"op_{n}", [P, NT] if n != "nh" else [P, 1]) for n in ("ss", "ms", "rs", "nh"))
        gate = GateRows(L, st, "op", 2, "g_post_mix")
        psY = L.ps(st, "psY", [P, 2, 2, 512])
        w_loaded = [L.sem(f"wo_loaded{i}") for i in range(2)]
        x_loaded = [L.sem(f"op_x_loaded{i}") for i in range(2)]
        y_stored = [L.sem(f"op_y_stored{i}") for i in range(2)]
        (w_hi_r, w_lo_r, m_hi_r, m_lo_r, done, sq, ms_r, rs_r, yt, y_r, pch) = (L.sem("op_" + n) for n in (
            "w_hi", "w_lo", "m_hi", "m_lo", "product", "squared", "ms", "rstd", "scaled", "y", "pool"))
        block = st.enter_context(nc.Block())

        def x_tile(t):
            if t < NT_LAT:
                return L.dram["x_sample"][t * P:(t + 1) * P, :]
            return L.dram["x_prompt"][(t - NT_LAT) * P:(t - NT_LAT + 1) * P, :]

        @block.sync
        def _(sp):
            for k in range(KD):
                if k >= 2:
                    sp.wait_ge(w_lo_r, k - 1)
                sp.dma_start(raw[:, k % 2, :], L.dram["w_out"][k * P:(k + 1) * P, :]).then_inc(w_loaded[k % 2], 16)
            gate.load(sp)
            for t in range(NT):
                if t >= 2:
                    sp.wait_ge(y_r, t - 1)
                sp.dma_start(xin[:, t % 2, :], x_tile(t)).then_inc(x_loaded[t % 2], 16)
                if t >= 1:
                    sp.wait_ge(y_r, t)
                    sp.dma_start(L.y1[t - 1], y[:, (t - 1) % 2, :]).then_inc(y_stored[(t - 1) % 2], 16)
            sp.wait_ge(y_r, NT)
            sp.dma_start(L.y1[NT - 1], y[:, (NT - 1) % 2, :]).then_inc(y_stored[(NT - 1) % 2], 16)
            for i in range(2):
                sp.wait_ge(y_stored[i], 16 * (NT // 2))

        @block.gpsimd
        def _(pool):
            pool.memset(nh[:], -0.5).then_inc(pch, 1)
            pool.wait_ge(pch, 1)
            for t in range(NT):
                pool.wait_ge(ms_r, t + 1)
                pool.tensor_tensor(rs[:, t:t + 1], ms[:, t:t + 1], nh[:], ALU.pow).then_inc(rs_r, 1)

        @block.scalar
        def _(act):
            def mix_hi(t):
                if t >= 2:
                    act.wait_ge(done, t - 1)
                for i, mix in enumerate((L.mixA, L.mixS)):
                    act.activation(m_hi[:, t % 2, 4 * i:4 * i + 4, :], mix[:, :, t * P:(t + 1) * P], ACT.Copy
                                   ).then_inc(m_hi_r, 1)

            mix_hi(0)
            for k in range(KD):
                act.wait_ge(w_loaded[k % 2], 16 * (k // 2 + 1))
                act.activation(w_hi[:, k, :], raw[:, k % 2, :], ACT.Copy).then_inc(w_hi_r, 1)
            for t in range(NT):
                if t + 1 < NT:
                    mix_hi(t + 1)
                act.wait_ge(done, t + 1)
                if t >= 1:
                    act.wait_ge(sq, t)
                act.activation(junk[:], flat(psY[:, t % 2, :, :]), ACT.Square, accum_out=ss[:, t:t + 1]
                               ).then_inc(sq, 1)

        @block.vector
        def _(dve):
            def mix_lo(t):
                dve.wait_ge(m_hi_r, 2 * t + 2)
                for i, mix in enumerate((L.mixA, L.mixS)):
                    dve.tensor_tensor(m_lo[:, t % 2, 4 * i:4 * i + 4, :], mix[:, :, t * P:(t + 1) * P],
                                      m_hi[:, t % 2, 4 * i:4 * i + 4, :].bitcast(F32), ALU.subtract
                                      ).then_inc(m_lo_r, 1)

            mix_lo(0)
            for k in range(KD):
                dve.wait_ge(w_hi_r, k + 1)
                dve.tensor_tensor(w_lo[:, k, :], raw[:, k % 2, :], w_hi[:, k, :].bitcast(F32), ALU.subtract
                                  ).then_inc(w_lo_r, 1)
            gate.dve(dve)
            for t in range(NT):
                if t + 1 < NT:
                    mix_lo(t + 1)
                s, g = t % 2, int(t >= NT_LAT)
                dve.wait_ge(sq, t + 1)
                dve.tensor_scalar(ms[:, t:t + 1], ss[:, t:t + 1], 1.0 / D, EPS, ALU.mult, ALU.add).then_inc(ms_r, 1)
                dve.wait_ge(rs_r, t + 1)
                if t >= 2:
                    dve.wait_ge(y_stored[s], 16 * (t // 2))
                dve.scalar_tensor_tensor(y[:, s, :], flat(psY[:, s, :, :]), rs[:, t:t + 1], gate.rows[:, g, :],
                                         ALU.mult, ALU.mult).then_inc(yt, 1)
                dve.wait_ge(yt, t + 1)
                dve.wait_ge(x_loaded[s], 16 * (t // 2 + 1))
                dve.tensor_tensor(y[:, s, :], y[:, s, :], xin[:, s, :], ALU.add).then_inc(y_r, 1)

        @block.tensor
        def _(pe):
            for t in range(NT):
                pe.wait_ge(m_lo_r, 2 * t + 2)
                if t >= 2:
                    pe.wait_ge(yt, t - 1)
                for half in range(2):
                    cols = slice(half * 512, (half + 1) * 512)
                    for k in range(KD):
                        if t == 0 and half == 0:
                            pe.wait_ge(w_lo_r, k + 1)
                        mm = split3(pe, psY[:, t % 2, half, :], m_hi[:, t % 2, k, :], m_lo[:, t % 2, k, :],
                                    w_hi[:, k, cols], w_lo[:, k, cols], k == 0, k == KD - 1)
                mm.then_inc(done, 1)


def phase_norm2(L):
    nc = L.nc
    with ExitStack() as st:
        norm = NormStage(L, st, "n2", L.h2_hi, L.h2_lo, L.scale2, L.mod[:, 3 * KD:4 * KD, :])
        block = st.enter_context(nc.Block())

        @block.sync
        def _(sp):
            for t in range(NT):
                norm.load(sp, lambda i: L.y1[i], t)

        @block.gpsimd
        def _(pool):
            norm.pool_begin(pool)
            for t in range(NT):
                norm.pool_rstd(pool, t)

        @block.scalar
        def _(act):
            for t in range(NT):
                norm.act_square(act, t)
            norm.act_modulate(act)

        @block.vector
        def _(dve):
            for t in range(NT + 1):
                norm.dve_step(dve, t)
            norm.dve_split(dve)

        @block.tensor
        def _(pe):
            norm.pe_transposes(pe, L.ident)


def phase_ffn(L):
    nc = L.nc
    PAIRS = FT // 2
    GU = [(s, b) for s in range(2) for b in range(len(BLOCKS))]
    NG = len(GU)
    ND = 2 * NT
    with ExitStack() as st:
        raw_gu = L.sb(st, "raw_gu", [P, 2, D])
        raw_d = L.sb(st, "raw_d", [P, D])
        gu_hi, gu_lo = (L.sb(st, f"gu_{n}", [P, 2, 2, D], F32R) for n in ("hi", "lo"))
        d_hi, d_lo = (L.sb(st, f"d_{n}", [P, 2, D], F32R) for n in ("hi", "lo"))
        h_hi, h_lo = (L.sb(st, f"h_{n}", [P, 2, T], F32R) for n in ("hi", "lo"))
        hid = L.sb(st, "hid", [P, 2, 512])
        psG = L.ps(st, "psG", [P, 2, 2, 512])
        psF = L.ps(st, "psF", [P, 4, 512])
        (gu_loaded, d_loaded, gu_hi_r, gu_lo_r, d_hi_r, d_lo_r, gu_used, silu, h_full, h_hi_r, h_lo_r, down,
         flushed) = (L.sem("ff_" + n) for n in (
             "gu_loaded", "d_loaded", "gu_hi", "gu_lo", "d_hi", "d_lo", "gu_used", "silu", "h_full", "h_hi", "h_lo",
             "down", "flushed"))
        block = st.enter_context(nc.Block())

        def over_pairs(eng, body):
            body(0, True, False)
            with eng.Fori(1, PAIRS - 1) as i:
                body(i, False, False)
            body(PAIRS - 1, False, True)

        @block.sync
        def _(sp):
            def load_gu(n, first=False):
                if not first:
                    sp.wait_ge(gu_lo_r, n)
                for i, w in enumerate(("w_gate", "w_up")):
                    sp.dma_start(raw_gu[:, i, :], L.dram[w][bass.ds(n, 1)].rearrange("a p n -> (a p) n")
                                 ).then_inc(gu_loaded, 16)

            def load_d(n, first=False):
                if not first:
                    sp.wait_ge(d_lo_r, n)
                sp.dma_start(raw_d[:], L.dram["w_down"][bass.ds(n, 1)].rearrange("a p n -> (a p) n")
                             ).then_inc(d_loaded, 16)

            load_gu(0, True)
            load_d(0, True)
            load_gu(1)
            load_d(1)
            with sp.Fori(1, PAIRS) as i:
                load_gu(2 * i)
                load_gu(2 * i + 1)
                load_d(2 * i)
                load_d(2 * i + 1)

        @block.scalar
        def _(act):
            def split_gu(n, s, first=False):
                act.wait_ge(gu_loaded, n * 32 + 32)
                if not first:
                    act.wait_ge(gu_used, n * 3 - 3)
                act.activation(gu_hi[:, s, :, :], raw_gu[:], ACT.Copy).then_inc(gu_hi_r, 1)

            def split_d(n, s, i, first=False):
                act.wait_ge(d_loaded, n * 16 + 16)
                if not first:
                    act.wait_ge(down, i * ND)
                act.activation(d_hi[:, s, :], raw_d[:], ACT.Copy).then_inc(d_hi_r, 1)

            def body(i, first, last):
                for n, (s, b) in enumerate(GU):
                    c0, w = BLOCKS[b]
                    act.wait_ge(gu_used, i * NG + (n + 1))
                    if not (first and n < 2):
                        act.wait_ge(h_lo_r, i * NG + (n - 1))
                    act.activation(hid[:, n % 2, :w], psG[:, n % 2, 0, :w], ACT.Silu).then_inc(silu, 1)
                    act.wait_ge(h_full, i * NG + (n + 1))
                    act.activation(h_hi[:, s, c0:c0 + w], hid[:, n % 2, :w], ACT.Copy).then_inc(h_hi_r, 1)
                    if b == 2 and not last:
                        split_gu(i * 2 + (2 + s), s)
                if not last:
                    for s in range(2):
                        split_d(i * 2 + (2 + s), s, i + 1)

            for s in range(2):
                split_gu(s, s, True)
                split_d(s, s, 0, True)
            over_pairs(act, body)

        @block.vector
        def _(dve):
            def split_gu(n, s):
                dve.wait_ge(gu_hi_r, n + 1)
                dve.tensor_tensor(gu_lo[:, s, :, :], raw_gu[:], gu_hi[:, s, :, :].bitcast(F32), ALU.subtract
                                  ).then_inc(gu_lo_r, 1)

            def split_d(n, s):
                dve.wait_ge(d_hi_r, n + 1)
                dve.tensor_tensor(d_lo[:, s, :], raw_d[:], d_hi[:, s, :].bitcast(F32), ALU.subtract
                                  ).then_inc(d_lo_r, 1)

            def body(i, first, last):
                for n, (s, b) in enumerate(GU):
                    c0, w = BLOCKS[b]
                    dve.wait_ge(silu, i * NG + (n + 1))
                    dve.tensor_tensor(hid[:, n % 2, :w], hid[:, n % 2, :w], psG[:, n % 2, 1, :w], ALU.mult
                                      ).then_inc(h_full, 1)
                    dve.wait_ge(h_hi_r, i * NG + (n + 1))
                    dve.tensor_tensor(h_lo[:, s, c0:c0 + w], hid[:, n % 2, :w], h_hi[:, s, c0:c0 + w].bitcast(F32),
                                      ALU.subtract).then_inc(h_lo_r, 1)
                    if b == 2 and not last:
                        split_gu(i * 2 + (2 + s), s)
                for r in range(ND):
                    t, cols = r // 2, slice((r % 2) * 512, (r % 2) * 512 + 512)
                    dve.wait_ge(down, i * ND + (r + 1))
                    if first:
                        dve.tensor_copy(L.facc[:, t, cols], psF[:, r % 4, :]).then_inc(flushed, 1)
                    else:
                        dve.wait_ge(flushed, i * ND + (r - ND + 1))
                        dve.tensor_tensor(L.facc[:, t, cols], L.facc[:, t, cols], psF[:, r % 4, :], ALU.add
                                          ).then_inc(flushed, 1)
                if not last:
                    for s in range(2):
                        split_d(i * 2 + (2 + s), s)

            for s in range(2):
                split_gu(s, s)
                split_d(s, s)
            over_pairs(dve, body)

        @block.tensor
        def _(pe):
            def body(i, first, last):
                for n, (s, b) in enumerate(GU):
                    c0, w = BLOCKS[b]
                    if b == 0:
                        pe.wait_ge(gu_lo_r, i * 2 + (s + 1))
                    if not (first and n < 2):
                        pe.wait_ge(h_full, i * NG + (n - 1))
                    for j in range(2):
                        for k in range(KD):
                            ks = slice(k * P, (k + 1) * P)
                            mm = split3(pe, psG[:, n % 2, j, :w], gu_hi[:, s, j, ks], gu_lo[:, s, j, ks],
                                        L.h2_hi[:, k, c0:c0 + w], L.h2_lo[:, k, c0:c0 + w], k == 0, k == KD - 1)
                    mm.then_inc(gu_used, 1)
                pe.wait_ge(d_lo_r, i * 2 + 2)
                for r in range(ND):
                    t, cols = r // 2, slice((r % 2) * 512, (r % 2) * 512 + 512)
                    if r in (0, 8, 16):
                        pe.wait_ge(h_lo_r, i * NG + (4 + r // 8))
                    if not (first and r < 4):
                        pe.wait_ge(flushed, i * ND + (r - 3))
                    ts = slice(t * P, (t + 1) * P)
                    for s in range(2):
                        mm = split3(pe, psF[:, r % 4, :], h_hi[:, s, ts], h_lo[:, s, ts], d_hi[:, s, cols],
                                    d_lo[:, s, cols], s == 0, s == 1)
                    mm.then_inc(down, 1)

            over_pairs(pe, body)


def phase_final(L):
    nc = L.nc
    with ExitStack() as st:
        yin = L.sb(st, "fi_y", [P, 4, D])
        out = L.sb(st, "fi_out", [P, 3, D])
        junk = L.sb(st, "fi_sq", [P, D])
        ss, ms, rs, nh = (L.sb(st, f"fi_{n}", [P, NT] if n != "nh" else [P, 1]) for n in ("ss", "ms", "rs", "nh"))
        gate = GateRows(L, st, "fi", 5, "g_post_ffn")
        y_loaded = [L.sem(f"fi_y_loaded{i}") for i in range(4)]
        stored = [L.sem(f"fi_stored{i}") for i in range(3)]
        sq, ms_r, rs_r, yt, y_r, pch = (L.sem("fi_" + n) for n in ("sq", "ms", "rs", "yt", "y", "pool"))
        block = st.enter_context(nc.Block())

        @block.sync
        def _(sp):
            gate.load(sp)
            for t in range(4):
                sp.dma_start(yin[:, t, :], L.y1[t]).then_inc(y_loaded[t], 16)
            for t in range(NT):
                sp.wait_ge(y_r, t + 1)
                dst = (L.outs["sample"][0, t * P:(t + 1) * P, :] if t < NT_LAT else
                       L.outs["prompt"][0, (t - NT_LAT) * P:(t - NT_LAT + 1) * P, :])
                sp.dma_start(dst, out[:, t % 3, :]).then_inc(stored[t % 3], 16)
                if t + 4 < NT:
                    sp.dma_start(yin[:, t % 4, :], L.y1[t + 4]).then_inc(y_loaded[t % 4], 16)
            for i in range(3):
                sp.wait_ge(stored[i], 16 * len(range(i, NT, 3)))

        @block.gpsimd
        def _(pool):
            pool.memset(nh[:], -0.5).then_inc(pch, 1)
            pool.wait_ge(pch, 1)
            for t in range(NT):
                pool.wait_ge(ms_r, t + 1)
                pool.tensor_tensor(rs[:, t:t + 1], ms[:, t:t + 1], nh[:], ALU.pow).then_inc(rs_r, 1)

        @block.scalar
        def _(act):
            for t in range(NT):
                if t >= 1:
                    act.wait_ge(sq, t)
                act.activation(junk[:], L.facc[:, t, :], ACT.Square, accum_out=ss[:, t:t + 1]).then_inc(sq, 1)

        @block.vector
        def _(dve):
            gate.dve(dve)
            for t in range(NT + 1):
                if t < NT:
                    dve.wait_ge(sq, t + 1)
                    dve.tensor_scalar(ms[:, t:t + 1], ss[:, t:t + 1], 1.0 / D, EPS, ALU.mult, ALU.add
                                      ).then_inc(ms_r, 1)
                if t == 0:
                    continue
                u = t - 1
                dve.wait_ge(rs_r, u + 1)
                if u >= 3:
                    dve.wait_ge(stored[u % 3], 16 * (u // 3))
                dve.scalar_tensor_tensor(out[:, u % 3, :], L.facc[:, u, :], rs[:, u:u + 1],
                                         gate.rows[:, int(u >= NT_LAT), :], ALU.mult, ALU.mult).then_inc(yt, 1)
                dve.wait_ge(yt, u + 1)
                dve.wait_ge(y_loaded[u % 4], 16 * (u // 4 + 1))
                dve.tensor_tensor(out[:, u % 3, :], out[:, u % 3, :], yin[:, u % 4, :], ALU.add).then_inc(y_r, 1)


def hybrid_layer_kernel(nc, dram, outs):
    with ExitStack() as stack:
        L = Layer(nc, dram, outs)
        sb = L.sb
        L.const = sb(stack, "const", [P, N_CONST])
        L.ident = L.const[:, K_ID:K_ID + P]
        L.fold = L.const[:, K_FOLD:K_FOLD + P]
        L.cols = sb(stack, "cols", [P, N_COLS])
        L.mod = sb(stack, "mod", [P, 6 * KD, 2])
        L.scale1, L.scale2 = (sb(stack, f"scale{i}", [P, KD, 2]) for i in (1, 2))
        L.y1 = nc.dram_tensor("y1_scratch", (NT, P, D), F32, kind="Internal").ap()
        L.staged = nc.dram_tensor("staged_scratch", (N_STAGED, P, T), F32, kind="Internal").ap()
        L.gate_rows = nc.dram_tensor("gate_rows", (2, 6 * D), F32, kind="Internal").ap()
        with ExitStack() as ssm:
            with ExitStack() as proj:
                L.cond_st = sb(proj, "cond_st", [P, KD, P])
                L.hT_hi, L.hT_lo = (sb(proj, f"hT_{n}", [P, KD, T], F32R) for n in ("hi", "lo"))
                phase_norm1(L)
                L.xbcT = sb(ssm, "xbcT", [P, N_XBC, T], side="right")
                L.dtT = sb(ssm, "dtT", [P, T], side="right")
                phase_in_proj(L)
            mixer = ExitStack()
            L.ones = sb(mixer, "ones", [P, P])
            L.mixS = sb(mixer, "mixS", [P, 4, T])
            with ExitStack() as decay:
                L.feat = sb(decay, "feat", [P, T])
                L.u2 = sb(decay, "u2", [64, T], F32R)
                L.sel, L.negsel = (sb(decay, n, [64, 16, P], F32R) for n in ("sel", "negsel"))
                L.maskb = sb(decay, "maskb", [P, 2, 4, P], BF16)
                L.identb = sb(decay, "identb", [P, P], BF16)
                L.cdrow = sb(decay, "cdrow", [P, NT, 16])
                phase_dt(L)
                phase_ssm(L)
        L.reuse_semaphores()
        with mixer:
            L.mixA = sb(mixer, "mixA", [P, HEADS, T])
            with ExitStack() as attn:
                L.table = sb(attn, "rope_table", [P, T])
                L.qn_hi, L.qn_lo = (sb(attn, f"qn_{n}", [P, KQ, T], F32R) for n in ("hi", "lo"))
                L.ckv_hi, L.ckv_lo = (sb(attn, f"ckv_{n}", [P, KKV, NKEY], F32R) for n in ("hi", "lo"))
                L.kr_hi, L.kr_lo = (sb(attn, f"kr_{n}", [P, NKEY], F32R) for n in ("hi", "lo"))
                phase_attn_prep(L)
                phase_attention(L)
            phase_out_proj(L)
        with ExitStack() as ffn:
            L.facc = sb(ffn, "facc", [P, NT, D])
            with ExitStack() as h:
                L.h2_hi, L.h2_lo = (sb(h, f"h2_{n}", [P, KD, T], F32R) for n in ("hi", "lo"))
                phase_norm2(L)
                phase_ffn(L)
            phase_final(L)


_OUTS = [("prompt", (1, N_PROMPT, D)), ("sample", (1, N_LAT, D)), ("ckv", (1, 1, N_PROMPT, KV_LORA)),
         ("krope", (1, 1, N_PROMPT, ROPE)), ("ssm", (1, 1, 2, SH, SP_, DS))]


def shape_constants(np):
    const = np.zeros((P, N_CONST), np.float32)
    i, j = np.arange(P)[:, None], np.arange(P)[None, :]
    const[:, K_ID:K_ID + P] = i == j
    const[:, K_MASK:K_MASK + P] = np.where(j >= i, 0.0, -1e30)
    const[:, K_MASK + P:K_MASK + 2 * P] = np.where(j <= i, 0.0, -1e30)
    h = np.arange(16)[None, :]
    const[:, K_SEL:K_SEL + 16] = (i == h) | (i == 32 + h)
    const[:, K_FOLD:K_FOLD + P] = (i % 64) == (j % 64)
    forward = (np.arange(P) % 16) < SH
    const[:, K_SA] = np.where(forward, 1.0, -1.0)
    const[:, K_SB] = np.where(forward, 0.0, 1.0)
    const[:, K_MT] = ~forward
    const[:, K_MD] = forward
    quarter = ROPE // 4
    inv = (np.float32(10000.0) ** (-np.arange(quarter, dtype=np.float32) / np.float32(quarter))).astype(np.float32)
    pos = np.arange(N_LAT)
    table = np.zeros((P, T), np.float32)
    table[0:ROPE, N_LAT:] = 1.0
    for half, where in enumerate((pos // 64, pos % 64)):
        ang = inv[:, None] * where[None, :].astype(np.float32)
        for part, sign in ((0, -1.0), (1, 1.0)):
            r = half * 2 * quarter + part * quarter
            table[r:r + quarter, 0:N_LAT] = np.cos(ang)
            table[ROPE + r:ROPE + r + quarter, 0:N_LAT] = sign * np.sin(ang)
    return const, table


def kernel(**inputs):
    import numpy as np
    import concourse.bacc as bacc
    from concourse.bass_utils import run_bass_kernel_spmd

    a = {k: np.asarray(v) for k, v in inputs.items()}
    const, table = shape_constants(np)
    swap = np.concatenate([np.arange(16, 32), np.arange(0, 16), np.arange(48, 64), np.arange(32, 48)])

    def col(v):
        return v.reshape(-1, P).T

    def k_tiles(w):
        return w.reshape(-1, P, w.shape[1]).transpose(1, 0, 2)

    w_in = a["w_in"][0]
    o_kv, o_r = Q_LORA, Q_LORA + KV_LORA
    o_z = o_r + ROPE
    o_x = o_z + SW
    o_dt = o_x + N_XBC * P
    tiles = [w_in[:, o_x + P * i:o_x + P * (i + 1)] for i in range(N_XBC)]
    tiles.append(np.tile(w_in[:, o_dt:o_dt + 16], (1, 8)))
    tiles += [w_in[:, o_z + P * i:o_z + P * (i + 1)] for i in range(N_Z)]
    tiles += [w_in[:, P * i:P * (i + 1)] for i in range(KQ)]
    tiles += [w_in[:, o_kv + P * i:o_kv + P * (i + 1)] for i in range(KKV)]
    rope = w_in[:, o_r:o_z]
    tiles.append(np.concatenate([rope, rope[:, swap]], axis=1))
    w_uq = a["w_uq"][0].reshape(Q_LORA, HEADS, NOPE + ROPE).transpose(1, 0, 2)
    w_uq = np.concatenate([w_uq, w_uq[:, :, NOPE + swap]], axis=2)

    def f_tiles(w):
        return w.reshape(KD, P, FT, P).transpose(2, 1, 0, 3).reshape(FT, P, D)

    dram_arrays = {
        "x_sample": a["x_sample"][0], "x_prompt": a["x_prompt"][0],
        "cond": np.stack([a["c"][0].reshape(KD, P), a["c_ctx"].reshape(KD, P)]).transpose(2, 1, 0).reshape(P, 2 * KD),
        "const": const, "rope_table": table,
        "cols": np.concatenate([
            col(a["g_pre_mix"][0]), col(a["g_pre_ffn"][0]), col(a["b_mod"][0]), col(a["g_q"][0]), col(a["g_kv"][0]),
            col(a["conv_w"][0][0]), col(a["conv_w"][0][1]), col(a["conv_w"][0][2]), col(a["conv_b"][0]),
            col(a["g_ssm_out"][0]), np.tile(a["dt_bias"].reshape(16), 8)[:, None],
            np.tile(a["a_log"].reshape(16), 8)[:, None]], axis=1),
        "b_mod": a["b_mod"], "g_post_mix": a["g_post_mix"], "g_post_ffn": a["g_post_ffn"], "d_skip": a["d_skip"],
        "w_mod": a["w_mod"][0], "w_in": np.stack([k_tiles(w) for w in tiles]),
        "w_uq": np.stack([k_tiles(w) for w in w_uq]), "w_ukv": a["w_ukv"][0], "w_out": a["w_out"][0],
        "w_gate": f_tiles(a["w_gate"][0]), "w_up": f_tiles(a["w_up"][0]), "w_down": a["w_down"][0].reshape(FT, P, D),
        "cache_ckv": a["cache_ckv"], "cache_krope": a["cache_krope"], "state_ssm": a["state_ssm"],
    }
    nc = bacc.Bacc("TRN2", target_bir_lowering=False, num_devices=1)
    arrays, dram = {}, {}
    for name, v in dram_arrays.items():
        arrays[f"in_{name}"] = np.ascontiguousarray(v)
        dram[name] = nc.dram_tensor(f"in_{name}", v.shape, F32, kind="ExternalInput").ap()
    outs = {n: nc.dram_tensor(f"out_{n}", shape, F32, kind="ExternalOutput").ap() for n, shape in _OUTS}
    hybrid_layer_kernel(nc, dram, outs)
    r = run_bass_kernel_spmd(nc, [arrays], core_ids=[0])
    return tuple(r.results[0][f"out_{n}"] for n, _ in _OUTS)
```

```python
from contextlib import ExitStack

import concourse.bass as bass
from concourse import mybir

P = 128
F32 = mybir.dt.float32
F32R = mybir.dt.float32r
BF16 = mybir.dt.bfloat16
ALU = mybir.AluOpType
ACT = mybir.ActivationFunctionType
AX_X = mybir.AxisListType.X

D = 1024
KD = D // P
N_LAT, N_PROMPT, N_CACHE = 1024, 256, 256
T = N_LAT + N_PROMPT
NT = T // P
NT_LAT = N_LAT // P
BLOCKS = [(0, 512), (512, 512), (1024, 256)]
EPS = 1e-6
HEADS, NOPE, ROPE, VD = 4, 128, 64, 128
Q_LORA, KV_LORA = 384, 256
KQ, KKV = Q_LORA // P, KV_LORA // P
SCALE = float(NOPE + ROPE) ** -0.5
NKEY = T + N_CACHE
SH, SP_, DS = 8, 64, 128
SW = SH * SP_
D_FF = 2816
FT = D_FF // P
N_XBC, N_Z = 8, 4
TILE_KINDS = ["xbc"] * N_XBC + ["dt"] + ["z"] * N_Z + ["q"] * KQ + ["kv"] * KKV + ["rope"]
N_TILES = len(TILE_KINDS)
N_STAGED = N_Z + KQ + KKV + 1
FIRST = {k: TILE_KINDS.index(k) for k in ("xbc", "dt", "z", "q", "kv", "rope")}
MOD_W = 256
MOD_EARLY = 2 * D // MOD_W
MOD_ALL = 6 * D // MOD_W

C_GPRE, C_GFFN, C_BMOD, C_GQ, C_GKV, C_CW, C_CB, C_GS = 0, 8, 16, 64, 67, 69, 93, 101
N_COLS = 105
K_ID, K_MASK, K_SEL, K_FOLD, K_TRI, K_SA, K_SB, K_MT, K_MD = 0, 128, 384, 400, 528, 656, 672, 688, 704
N_CONST = 720


class Chain:

    def __init__(self, eng, sem):
        self.eng, self.sem, self.n = eng, sem, 0

    def mark(self, ins):
        ins.then_inc(self.sem, 1)
        self.n += 1

    def wait(self, back=0):
        self.eng.wait_ge(self.sem, self.n - back)

    def link(self, ins):
        self.mark(ins)
        self.wait()


class Layer:

    def __init__(self, nc, dram, outs):
        self.nc, self.dram, self.outs, self.sems = nc, dram, outs, []

    def sb(self, stack, name, shape, dt=F32, side="left"):
        return stack.enter_context(self.nc.sbuf_tensor(name, shape, dt, side=side))

    def ps(self, stack, name, shape):
        return stack.enter_context(self.nc.psum_tensor(name, shape, F32))

    def sem(self, name):
        self.sems.append(self.nc.alloc_semaphore(name=name))
        return self.sems[-1]

    def reuse_semaphores(self):
        for s in self.sems:
            self.nc.sync.sem_clear(s)
        for s in self.sems:
            self.nc.release_semaphore(s)
        self.sems = []
        self.nc.all_engine_barrier()


def flat(ap):
    return ap.rearrange("p a b -> p (a b)")


def across(ap, n):
    p, a = ap.shape
    return ap.unsqueeze(2).to_broadcast([p, a, n])


class Turn:

    def __init__(self, L, tag, xn, psX, full, hT_hi, hT_lo, scale_col, shift_col):
        self.L, self.xn, self.psX, self.full = L, xn, psX, full
        self.hi, self.lo, self.a, self.s = hT_hi, hT_lo, scale_col, shift_col
        self.slots = full.shape[1]
        self.transposed, self.modulated, self.rounded, self.h_ready = (
            L.sem(f"{tag}_{n}") for n in ("transposed", "modulated", "rounded", "h_ready"))
        self.steps = [(b, k) for b in range(len(BLOCKS)) for k in range(KD)]

    def pe(self, pe, first, last, xn_ready=None):
        for n in range(first, last):
            b, k = self.steps[n]
            t0, w = BLOCKS[b][0] // P, BLOCKS[b][1] // P
            if xn_ready is not None:
                pe.wait_ge(xn_ready, t0 + w)
            if n >= 4:
                pe.wait_ge(self.modulated, n - 3)
            for i in range(w):
                mm = pe.transpose(self.psX[:, n % 4, i * P:(i + 1) * P], self.xn[:, t0 + i, k * P:(k + 1) * P],
                                  self.L.ident)
            mm.then_inc(self.transposed, 1)

    def act(self, act, first, last):
        for n in range(first, last):
            b, k = self.steps[n]
            w, g = BLOCKS[b][1], int(BLOCKS[b][0] >= N_LAT)
            act.wait_ge(self.transposed, n + 1)
            if n >= self.slots:
                act.wait_ge(self.h_ready, n + 1 - self.slots)
            act.activation(self.full[:, n % self.slots, :w], self.psX[:, n % 4, :w], ACT.Identity,
                           bias=self.s[:, k, g:g + 1], scale=self.a[:, k, g:g + 1]).then_inc(self.modulated, 1)

    def dve(self, dve, first, last):
        for n in range(first, last):
            b, k = self.steps[n]
            c0, w = BLOCKS[b]
            dve.wait_ge(self.modulated, n + 1)
            dve.tensor_copy(self.hi[:, k, c0:c0 + w], self.full[:, n % self.slots, :w]).then_inc(self.rounded, 1)
            dve.wait_ge(self.rounded, n + 1)
            dve.tensor_tensor(self.lo[:, k, c0:c0 + w], self.full[:, n % self.slots, :w],
                              self.hi[:, k, c0:c0 + w].bitcast(F32), ALU.subtract).then_inc(self.h_ready, 1)


class NormStage:

    def __init__(self, L, st, tag):
        self.xin = L.sb(st, f"{tag}_xin", [P, 4, D])
        self.xn = L.sb(st, f"{tag}_xn", [P, NT, D])
        self.ssq = L.sb(st, f"{tag}_ssq", [P, NT])
        self.ms = L.sb(st, f"{tag}_ms", [P, NT])
        self.rstd = L.sb(st, f"{tag}_rstd", [P, NT])
        self.neghalf = L.sb(st, f"{tag}_nh", [P, 1])
        self.x_loaded = [L.sem(f"{tag}_x_loaded{i}") for i in range(4)]
        self.squared, self.meansq, self.rstd_ready, self.xn_ready, self.const = (
            L.sem(f"{tag}_{n}") for n in ("squared", "meansq", "rstd_ready", "xn_ready", "const"))

    def load(self, eng, tiles, t):
        if t >= 4:
            eng.wait_ge(self.xn_ready, t - 3)
        eng.dma_start(self.xin[:, t % 4, :], tiles(t)).then_inc(self.x_loaded[t % 4], 16)

    def act_square(self, act, t):
        act.wait_ge(self.x_loaded[t % 4], 16 * (t // 4 + 1))
        act.activation(self.xn[:, t, :], self.xin[:, t % 4, :], ACT.Square,
                       accum_out=self.ssq[:, t:t + 1]).then_inc(self.squared, 1)

    def pool_begin(self, pool):
        pool.memset(self.neghalf[:], -0.5).then_inc(self.const, 1)
        pool.wait_ge(self.const, 1)

    def pool_rstd(self, pool, t):
        pool.wait_ge(self.meansq, t + 1)
        pool.tensor_tensor(self.rstd[:, t:t + 1], self.ms[:, t:t + 1], self.neghalf[:],
                           ALU.pow).then_inc(self.rstd_ready, 1)

    def dve_step(self, dve, t):
        if t < NT:
            dve.wait_ge(self.squared, t + 1)
            dve.tensor_scalar(self.ms[:, t:t + 1], self.ssq[:, t:t + 1], 1.0 / D, EPS, ALU.mult,
                              ALU.add).then_inc(self.meansq, 1)
        if t >= 1:
            u = t - 1
            dve.wait_ge(self.rstd_ready, u + 1)
            dve.tensor_scalar(self.xn[:, u, :], self.xin[:, u % 4, :], self.rstd[:, u:u + 1], None,
                              ALU.mult).then_inc(self.xn_ready, 1)


class ModStage:
    def __init__(self, L, st, tag, first, last, banks, depth):
        self.L, self.first, self.last, self.banks, self.depth = L, first, last, banks, depth
        self.ring = L.sb(st, f"{tag}_wring", [P, depth, KD, MOD_W])
        self.row = L.sb(st, f"{tag}_row", [P, 2, MOD_W])
        self.psM = L.ps(st, f"{tag}_psM", [P, banks, 512])
        self.psC = L.ps(st, f"{tag}_psC", [P, 2, P])
        self.loaded = [L.sem(f"{tag}_w_loaded{i}") for i in range(depth)]
        self.row_out = [L.sem(f"{tag}_row_out{i}") for i in range(2)]
        self.product, self.row_ready, self.turned, self.col_ready = (
            L.sem(f"{tag}_{n}") for n in ("product", "row_ready", "turned", "col_ready"))

    @staticmethod
    def is_gate(j):
        return (j * MOD_W // D) % 3 == 2

    def n_turned(self, j):
        return sum(not self.is_gate(i) for i in range(self.first, j))

    def n_rows(self, j, slot):
        return sum(self.is_gate(i) for i in range(self.first + slot, j, 2))

    def load(self, eng, j):
        i = j - self.first
        r = i % self.depth
        if i >= self.depth:
            eng.wait_ge(self.product, i + 1 - self.depth)
        eng.dma_start(self.ring[:, r, :, :],
                      self.L.dram["w_mod"].rearrange("(k p) n -> p k n", p=P)[:, :, j * MOD_W:(j + 1) * MOD_W]
                      ).then_inc(self.loaded[r], 16)

    def pe_product(self, pe, j):
        i = j - self.first
        r = i % self.depth
        pe.wait_ge(self.loaded[r], 16 * (i // self.depth + 1))
        if i >= self.banks:
            pe.wait_ge(self.row_ready, i + 1 - self.banks)
        for k in range(KD):
            mm = pe.matmul(self.psM[:, i % self.banks, :MOD_W], self.L.cond_st[:, k, :], self.ring[:, r, k, :],
                           start=(k == 0), stop=(k == KD - 1))
        mm.then_inc(self.product, 1)

    def dve_row(self, dve, j):
        i = j - self.first
        dve.wait_ge(self.product, i + 1)
        if i >= 2:
            if self.is_gate(j - 2):
                dve.wait_ge(self.row_out[i % 2], 32 * self.n_rows(j - 1, i % 2))
            else:
                dve.wait_ge(self.turned, self.n_turned(j - 1))
        dve.tensor_copy(self.row[:, i % 2, :], self.psM[:, i % self.banks, :MOD_W]).then_inc(self.row_ready, 1)

    def pe_turn(self, pe, j, ident):
        i, c = j - self.first, self.n_turned(j)
        pe.wait_ge(self.row_ready, i + 1)
        if c >= 1:
            pe.wait_ge(self.col_ready, c)
        for s in range(2):
            mm = pe.transpose(self.psC[:, s, :], self.row[:, i % 2, s * P:(s + 1) * P], ident)
        mm.then_inc(self.turned, 1)

    def dve_col(self, dve, j):
        c = self.n_turned(j)
        dve.wait_ge(self.turned, c + 1)
        dve.tensor_tensor(self.L.mod[:, 2 * j:2 * j + 2, :], self.psC[:, :, 0:P:P // 2],
                          across(self.L.cols[:, C_BMOD + 2 * j:C_BMOD + 2 * j + 2], 2),
                          ALU.add).then_inc(self.col_ready, 1)

    def store_gate(self, eng, j):
        i = j - self.first
        eng.wait_ge(self.row_ready, i + 1)
        for g in range(2):
            eng.dma_start(self.L.gate_rows[g:g + 1, j * MOD_W:(j + 1) * MOD_W],
                          self.row[g * (P // 2):g * (P // 2) + 1, i % 2, :]).then_inc(self.row_out[i % 2], 16)


def phase_norm1(L):
    nc = L.nc
    with ExitStack() as st:
        norm = NormStage(L, st, "n1")
        full = L.sb(st, "n1_full", [P, 3, 512])
        psX = L.ps(st, "n1_psX", [P, 4, 512])
        turn = Turn(L, "n1", norm.xn, psX, full, L.hT_hi, L.hT_lo, L.scale1, L.mod[:, 0:KD, :])
        mod = ModStage(L, st, "m1", 0, MOD_EARLY, 2, 4)
        cond = L.sb(st, "cond", [P, KD * 2])
        scond = L.sb(st, "scond", [P, KD * 2])
        c_ld, k_ld, silu, dch = (L.sem(n) for n in ("cond_loaded", "const_loaded", "cond_silu", "n1_dve"))
        block = st.enter_context(nc.Block())

        def x_tile(t):
            if t < NT_LAT:
                return L.dram["x_sample"][t * P:(t + 1) * P, :]
            return L.dram["x_prompt"][(t - NT_LAT) * P:(t - NT_LAT + 1) * P, :]

        @block.sync
        def _(sp):
            sp.dma_start(cond[:], L.dram["cond"]).then_inc(c_ld, 16)
            sp.dma_start(L.const[:], L.dram["const"]).then_inc(k_ld, 16)
            sp.dma_start(L.cols[:], L.dram["cols"]).then_inc(k_ld, 16)
            for j in range(NT):
                norm.load(sp, x_tile, j)
                if j < MOD_EARLY:
                    mod.load(sp, j)

        @block.gpsimd
        def _(pool):
            norm.pool_begin(pool)
            for t in range(NT):
                norm.pool_rstd(pool, t)

        @block.scalar
        def _(act):
            act.wait_ge(c_ld, 16)
            act.activation(scond[:], cond[:], ACT.Silu).then_inc(silu, 1)
            for t in range(NT):
                norm.act_square(act, t)
            act.wait_ge(dch, 2)
            turn.act(act, 0, len(turn.steps))

        @block.vector
        def _(dve):
            dve.wait_ge(silu, 1)
            dve.tensor_copy(L.cond_st[:].rearrange("p k (g r) -> p (k g) r", g=2),
                            across(scond[:], P // 2)).then_inc(dch, 1)
            dve.wait_ge(k_ld, 32)
            for i in range(NT + 1):
                if i < MOD_EARLY:
                    mod.dve_row(dve, i)
                norm.dve_step(dve, i)
                if i < MOD_EARLY:
                    mod.dve_col(dve, i)
            dve.wait_ge(mod.col_ready, MOD_EARLY)
            dve.scalar_tensor_tensor(L.scale1[:], L.mod[:, KD:2 * KD, :], 1.0,
                                     across(L.cols[:, C_GPRE:C_GPRE + KD], 2), ALU.add,
                                     ALU.mult).then_inc(dch, 1)
            turn.dve(dve, 0, len(turn.steps))

        @block.tensor
        def _(pe):
            pe.wait_ge(dch, 1)
            pe.wait_ge(k_ld, 32)
            for j in range(MOD_EARLY):
                mod.pe_product(pe, j)
                mod.pe_turn(pe, j, L.ident)
            turn.pe(pe, 0, len(turn.steps), norm.xn_ready)


def split3(pe, out, w_hi, w_lo, x_hi, x_lo, first, last):
    pe.matmul(out, w_hi, x_hi, start=first, stop=False)
    pe.matmul(out, w_hi, x_lo, start=False, stop=False)
    return pe.matmul(out, w_lo, x_hi, start=False, stop=last)


def phase_in_proj(L):
    nc = L.nc
    with ExitStack() as st:
        raw = L.sb(st, "win_raw", [P, 2, KD, P])
        w_hi = L.sb(st, "win_hi", [P, 2, KD, P], F32R)
        w_lo = L.sb(st, "win_lo", [P, 2, KD, P], F32R)
        conv = L.sb(st, "conv_acc", [P, T])
        stage = L.sb(st, "stage", [P, 2, T])
        mod = ModStage(L, st, "m2", MOD_EARLY, MOD_ALL, 1, 2)
        psP = L.ps(st, "psP", [P, 2, 3, 512])
        loaded = [L.sem(f"win_loaded{i}") for i in range(2)]
        stored = [L.sem(f"stage_stored{i}") for i in range(2)]
        hi_ready, lo_ready, used, drained, conv_ready, conv_read, dch, mod_done = (
            L.sem(n) for n in ("win_hi_ready", "win_lo_ready", "win_used", "proj_drained", "conv_ready",
                               "conv_read", "ip_dve", "mod2_scale"))
        block = st.enter_context(nc.Block())
        last_mod = MOD_ALL - MOD_EARLY

        @block.sync
        def _(sp):
            def load(ct):
                if ct >= 2:
                    sp.wait_ge(lo_ready, ct - 1)
                sp.dma_start(raw[:, ct % 2, :, :], L.dram["w_in"][ct]).then_inc(loaded[ct % 2], 16)

            load(0)
            load(1)
            for ct in range(N_TILES):
                if ct < last_mod:
                    mod.load(sp, MOD_EARLY + ct)
                if ct + 2 < N_TILES:
                    load(ct + 2)

        @block.gpsimd
        def _(pool):
            for ct in range(N_TILES):
                if ct < last_mod and mod.is_gate(MOD_EARLY + ct):
                    mod.store_gate(pool, MOD_EARLY + ct)
                if ct >= FIRST["z"]:
                    i = ct - FIRST["z"]
                    pool.wait_ge(drained, i + 2)
                    pool.dma_start(L.staged[i], stage[:, i % 2, :]).then_inc(stored[i % 2], 16)
            for i in range(2):
                pool.wait_ge(stored[i], 16 * (N_STAGED // 2))
            for i in range(2):
                pool.wait_ge(mod.row_out[i], 32 * mod.n_rows(MOD_ALL, i))

        @block.scalar
        def _(act):
            def split(ct):
                act.wait_ge(loaded[ct % 2], 16 * (ct // 2 + 1))
                if ct >= 2:
                    act.wait_ge(used, ct - 1)
                act.activation(w_hi[:, ct % 2, :, :], raw[:, ct % 2, :, :], ACT.Copy).then_inc(hi_ready, 1)

            split(0)
            for ct, kind in enumerate(TILE_KINDS):
                if ct + 1 < N_TILES:
                    split(ct + 1)
                i = ct - FIRST[kind]
                src = flat(psP[:, ct % 2, :, :])[:, 0:T]
                if kind == "xbc":
                    act.wait_ge(conv_ready, ct + 1)
                    act.activation(L.xbcT[:, i, :], conv[:], ACT.Silu,
                                   bias=L.cols[:, C_CB + i:C_CB + i + 1]).then_inc(conv_read, 1)
                    continue
                act.wait_ge(used, ct + 1)
                if kind == "dt":
                    act.activation(L.dtT[:], src, ACT.Copy).then_inc(drained, 1)
                    continue
                i = ct - FIRST["z"]
                if i >= 2:
                    act.wait_ge(stored[i % 2], 16 * (i // 2))
                act.activation(stage[:, i % 2, :], src, ACT.Silu if kind == "z" else ACT.Copy).then_inc(drained, 1)

        @block.vector
        def _(dve):
            chain = Chain(dve, dch)

            def split(ct):
                dve.wait_ge(hi_ready, ct + 1)
                dve.tensor_tensor(w_lo[:, ct % 2, :, :], raw[:, ct % 2, :, :],
                                  w_hi[:, ct % 2, :, :].bitcast(F32), ALU.subtract).then_inc(lo_ready, 1)

            split(0)
            for ct, kind in enumerate(TILE_KINDS):
                if ct + 1 < N_TILES:
                    split(ct + 1)
                if kind == "xbc":
                    src = flat(psP[:, ct % 2, :, :])
                    tap = [L.cols[:, C_CW + 8 * n + ct:C_CW + 8 * n + ct + 1] for n in range(3)]
                    dve.wait_ge(used, ct + 1)
                    if ct >= 1:
                        dve.wait_ge(conv_read, ct)
                    chain.link(dve.tensor_scalar(conv[:], src[:, 0:T], tap[1], None, ALU.mult))
                    for a, b in ((0, N_LAT), (N_LAT, T)):
                        chain.mark(dve.scalar_tensor_tensor(conv[:, a + 1:b], src[:, a:b - 1], tap[0],
                                                            conv[:, a + 1:b], ALU.mult, ALU.add))
                    chain.wait()
                    for a, b in ((0, N_LAT), (N_LAT, T)):
                        chain.mark(dve.scalar_tensor_tensor(conv[:, a:b - 1], src[:, a + 1:b], tap[2],
                                                            conv[:, a:b - 1], ALU.mult, ALU.add))
                    chain.wait()
                    dve.sem_inc(conv_ready, 1)
                if ct < last_mod:
                    mod.dve_row(dve, MOD_EARLY + ct)
                if 1 <= ct <= last_mod and not mod.is_gate(MOD_EARLY + ct - 1):
                    mod.dve_col(dve, MOD_EARLY + ct - 1)
            dve.wait_ge(mod.col_ready, mod.n_turned(MOD_ALL))
            dve.scalar_tensor_tensor(L.scale2[:], L.mod[:, 4 * KD:5 * KD, :], 1.0,
                                     across(L.cols[:, C_GFFN:C_GFFN + KD], 2), ALU.add,
                                     ALU.mult).then_inc(mod_done, 1)
            dve.wait_ge(mod_done, 1)

        @block.tensor
        def _(pe):
            for ct in range(N_TILES):
                s = ct % 2
                pe.wait_ge(lo_ready, ct + 1)
                if ct >= 2 and ct - 2 < N_XBC:
                    pe.wait_ge(conv_ready, ct - 1)
                elif ct >= 2:
                    pe.wait_ge(drained, ct - 1 - N_XBC)
                for b, (c0, w) in enumerate(BLOCKS):
                    for k in range(KD):
                        mm = split3(pe, psP[:, s, b, :w], w_hi[:, s, k, :], w_lo[:, s, k, :],
                                    L.hT_hi[:, k, c0:c0 + w], L.hT_lo[:, k, c0:c0 + w], k == 0, k == KD - 1)
                mm.then_inc(used, 1)
                if 1 <= ct <= last_mod and not mod.is_gate(MOD_EARLY + ct - 1):
                    mod.pe_turn(pe, MOD_EARLY + ct - 1, L.ident)
                if ct < last_mod:
                    mod.pe_product(pe, MOD_EARLY + ct)


def phase_ssm(L):
    nc = L.nc
    with ExitStack() as st:
        xs = L.sb(st, "xs", [P, NT, SW])
        bt = L.sb(st, "bt", [P, NT, 2, DS])
        mix_out = L.sb(st, "ssm_mix", [P, NT, SW])
        zt = mix_out
        zc = L.sb(st, "zc", [P, 2, 4, P])
        sb_in = L.sb(st, "sb_in", [P, NT, SW])
        sf = L.sb(st, "sf", [P, 2, SW])
        xw = L.sb(st, "xw", [P, 2, SW])
        tmp, off_b, yv, yn, decayed = (L.sb(st, n, [P, SW]) for n in ("s_tmp", "off_b", "yv", "yn", "decayed"))
        st_in = L.sb(st, "st_in", [P, 2, 4, DS])
        fin = L.sb(st, "fin", [P, 2, SW])
        seg = L.sb(st, "seg", [P, 16, P])
        cb = L.sb(st, "cb", [P, 2, P])
        wt = L.sb(st, "wt", [P, SH, P])
        dskip = L.sb(st, "dskip", [P, 4])
        ddiag = L.sb(st, "ddiag", [P, 4, P])
        rows = L.sb(st, "dt_rows", [P, 2, 16])
        feats = [L.sb(st, f"dt_{n}", [P, NT, 16]) for n in (
            "v", "e", "w", "lw", "c", "dt", "da", "u", "up", "eoff", "wgt", "t", "cdrow")]
        v, e, w, lw, cc, dt, da, u, up, eoff, wgt, t3, cdrow = feats
        rnd = L.sb(st, "dt_rnd", [P, NT, 16], F32R)
        pack = L.sb(st, "dt_pack", [P, 2, NT, 64])
        u2, up2 = (L.sb(st, n, [64, T], F32R) for n in ("u2", "up2"))
        sel, negsel = (L.sb(st, n, [64, 16, P], F32R) for n in ("sel", "negsel"))
        maskb = L.sb(st, "maskb", [P, 2, 4, P], BF16)
        identb = L.sb(st, "identb", [P, P], BF16)
        ss, ms, rs, nh = (L.sb(st, f"y_{n}", [P, NT] if n != "nh" else [P, 1]) for n in ("ss", "ms", "rs", "nh"))
        A = [L.ps(st, f"psA{i}", [P, 512]) for i in range(4)]
        Q = L.ps(st, "psQ", [P, 4, 512])
        z_loaded = [L.sem(f"ss_z{i}") for i in range(2)]
        (mix_stored, st_loaded, st_turned, row_loaded, dt_turned, dt_pe, dt_act, dt_dve, dch, packed, u_turned, u_read, x_turned, x_copied,
         xw_ready, s_mm, s_ready, cb_done, cb_read, seg_done, exp_done, off_done, off_read, w_ready, diag_done,
         y_ready, squared, rstd_ready, yn_ready, y_turned, mix_ready, sf_ready, dec_ready, fin_mm, fin_cp, fin_out,
         consts, pch) = (L.sem("ss_" + n) for n in (
             "mix_stored", "st_loaded", "st_turned", "row_loaded", "dt_turned", "dt_pe", "dt_act", "dt_dve", "dch", "packed", "u_turned", "u_read",
             "x_turned", "x_copied", "xw_ready", "s_mm", "s_ready", "cb_done", "cb_read", "seg_done", "exp_done",
             "off_done", "off_read", "w_ready", "diag_done", "y_ready", "squared", "rstd", "yn_ready", "y_turned",
             "mix_ready", "sf_ready", "dec_ready", "fin_mm", "fin_cp", "fin_out", "consts", "pch"))
        block = st.enter_context(nc.Block())
        down = list(range(NT_LAT - 1, -1, -1)) + list(range(NT - 1, NT_LAT - 1, -1))
        heads = lambda ap: ap.rearrange("p (h q) -> p h q", q=SP_)
        chunk = lambda c: slice(c * P, (c + 1) * P)
        krow = lambda c: L.const[:, c:c + 16].unsqueeze(1).to_broadcast([P, NT, 16])
        row = lambda i: rows[:, i, :].unsqueeze(1).to_broadcast([P, NT, 16])
        U_GROUPS = [(which, c0, min(4, NT - c0)) for which in range(2) for c0 in range(0, NT, 4)]

        @block.sync
        def _(sp):
            sp.dma_start(rows[:, 0, :], L.dram["dt_bias"].to_broadcast([P, 16])).then_inc(row_loaded, 16)
            sp.dma_start(rows[:, 1, :], L.dram["a_log"].to_broadcast([P, 16])).then_inc(row_loaded, 16)
            for d in range(2):
                sp.dma_start(st_in[:, d, :, :], L.dram["state_ssm"][0, 0, d].rearrange("(a h) p n -> (h p) a n", a=4)
                             ).then_inc(st_loaded, 16)
            for g in range(2):
                sp.dma_start(dskip[64 * g:64 * g + 64, :],
                             L.dram["d_skip"][g:g + 1, :].to_broadcast([64, 4])
                             ).then_inc(st_loaded, 16)
            for i, c in enumerate(down):
                if i >= 2:
                    sp.wait_ge(x_turned, i - 1)
                sp.dma_start(zc[:, i % 2, :, :], L.staged[0:N_Z].rearrange("a p t -> p a t")[:, :, chunk(c)]
                             ).then_inc(z_loaded[i % 2], 16)
            for c in range(NT):
                sp.wait_ge(mix_ready, c + 1)
                sp.dma_start(L.mixS[c], mix_out[:, c, :]).then_inc(mix_stored, 16)
            sp.wait_ge(mix_stored, 16 * NT)
            sp.wait_ge(fin_cp, 2)
            for d in range(2):
                sp.dma_start(L.outs["ssm"][0, 0, d].rearrange("(a h) p n -> (h p) a n", a=4), st_in[:, d, :, :]
                             ).then_inc(fin_out, 16)
            sp.wait_ge(fin_out, 32)

        @block.gpsimd
        def _(pool):
            p = Chain(pool, pch)
            pool.memset(L.ones[:], 1.0).then_inc(consts, 1)
            p.mark(pool.memset(nh[:], -0.5))
            pool.memset(pack[:], 0.0).then_inc(consts, 1)
            pool.tensor_copy(sel[:], across(L.const[0:64, K_SEL:K_SEL + 16], P)).then_inc(consts, 1)
            pool.tensor_scalar(negsel[:], across(L.const[0:64, K_SEL:K_SEL + 16], P), -1.0, None, ALU.mult
                               ).then_inc(consts, 1)
            for d in range(2):
                pool.tensor_copy(maskb[:, d, :, :], L.const[:, K_MASK + d * P:K_MASK + (d + 1) * P]
                                 .unsqueeze(1).to_broadcast([P, 4, P])).then_inc(consts, 1)
            pool.tensor_copy(identb[:], L.ident).then_inc(consts, 1)
            pool.wait_ge(st_loaded, 64)
            pool.tensor_tensor(ddiag[:], L.ident.unsqueeze(1).to_broadcast([P, 4, P]), across(dskip[:], P), ALU.mult
                               ).then_inc(consts, 1)
            p.wait()

            def decay(c):
                if c == NT_LAT - 1:
                    return
                pool.wait_ge(sf_ready, c + 1)
                if c == 0:
                    pool.wait_ge(dt_act, 5)
                pool.tensor_tensor(heads(decayed[:]), heads(sf[:, c % 2, :]), across(cdrow[:, c, 0:8], SP_), ALU.mult
                                   ).then_inc(dec_ready, 1)

            def rstd(c):
                pool.wait_ge(squared, c + 1)
                p.link(pool.tensor_scalar(ms[:, c:c + 1], ss[:, c:c + 1], 1.0 / SW, EPS, ALU.mult, ALU.add))
                pool.tensor_tensor(rs[:, c:c + 1], ms[:, c:c + 1], nh[:], ALU.pow).then_inc(rstd_ready, 1)

            for c in range(NT):
                if c >= 1:
                    rstd(c - 1)
                decay(c)
            rstd(NT - 1)

        @block.scalar
        def _(act):
            def copies(i):
                c = down[i]
                act.wait_ge(x_turned, i + 1)
                act.activation(xs[:, c, :], A[i % 2][:], ACT.Copy).then_inc(x_copied, 1)
                act.activation(flat(bt[:, c, :, :]), A[2 + i % 2][:, 0:2 * DS], ACT.Copy).then_inc(x_copied, 1)
                act.activation(zt[:, c, :], Q[:, 2 + i % 2, :], ACT.Copy).then_inc(x_copied, 1)

            act.wait_ge(row_loaded, 32)
            act.activation(rows[:, 1, :], rows[:, 1, :], ACT.Exp).then_inc(dt_act, 1)
            act.wait_ge(dt_dve, 1)
            act.activation(e[:], e[:], ACT.Exp).then_inc(dt_act, 1)
            act.wait_ge(dt_dve, 2)
            act.activation(lw[:], w[:], ACT.Ln).then_inc(dt_act, 1)
            act.wait_ge(dt_dve, 3)
            act.activation(w[:], w[:], ACT.Ln).then_inc(dt_act, 1)
            copies(0)
            copies(1)
            act.wait_ge(dt_pe, 1)
            act.activation(flat(cdrow[:]), Q[:, 0, 0:NT * 16], ACT.Exp).then_inc(dt_act, 1)
            act.wait_ge(dt_dve, 5)
            act.activation(eoff[:], eoff[:], ACT.Exp).then_inc(dt_act, 1)
            act.activation(wgt[:], wgt[:], ACT.Exp).then_inc(dt_act, 1)
            for i in range(2, NT):
                copies(i)

            def finish(c):
                act.wait_ge(y_ready, c + 1)
                if c >= 1:
                    act.wait_ge(y_turned, c)
                act.activation(yn[:], yv[:], ACT.Square, accum_out=ss[:, c:c + 1]).then_inc(squared, 1)
                act.wait_ge(rstd_ready, c + 1)
                act.wait_ge(squared, c + 1)
                act.activation(yn[:], yv[:], ACT.Copy, scale=rs[:, c:c + 1]).then_inc(yn_ready, 1)

            for c in range(NT):
                act.wait_ge(cb_done, c + 1)
                if c >= 1:
                    act.wait_ge(w_ready, c)
                act.activation(flat(cb[:]), A[0][:, 0:2 * P], ACT.Copy).then_inc(cb_read, 1)
                act.wait_ge(seg_done, c + 1)
                act.activation(flat(seg[:]), flat(Q[:]), ACT.Exp).then_inc(exp_done, 1)
                if c >= 1:
                    finish(c - 1)
            finish(NT - 1)

        @block.vector
        def _(dve):
            f = Chain(dve, dch)
            dve.wait_ge(row_loaded, 32)
            dve.wait_ge(dt_turned, 1)
            f.link(dve.tensor_tensor(v[:], Q[:, 0, 0:NT * 16].rearrange("p (c h) -> p c h", h=16), row(0), ALU.add))
            dve.scalar_tensor_tensor(e[:], v[:], -1.0, v[:], ALU.mult, ALU.min).then_inc(dt_dve, 1)
            dve.wait_ge(dt_act, 2)
            dve.tensor_scalar(w[:], e[:], 1.0, None, ALU.add).then_inc(dt_dve, 1)
            dve.wait_ge(dt_dve, 2)
            f.mark(dve.scalar_tensor_tensor(cc[:], w[:], 1.0, e[:], ALU.subtract, ALU.subtract))
            f.link(dve.tensor_scalar(t3[:], w[:], 0.5, -1.5, ALU.mult, ALU.add))
            f.link(dve.tensor_tensor(cc[:], cc[:], t3[:], ALU.mult))
            dve.wait_ge(dt_act, 3)
            f.link(dve.tensor_tensor(lw[:], lw[:], cc[:], ALU.add))
            f.link(dve.scalar_tensor_tensor(dt[:], v[:], 0.0, lw[:], ALU.max, ALU.add))
            dve.tensor_scalar(w[:], dt[:], 2.0 ** -60, None, ALU.max).then_inc(dt_dve, 1)
            dve.scalar_tensor_tensor(da[:], dt[:], -1.0, row(1), ALU.mult, ALU.mult).then_inc(dt_dve, 1)
            dve.wait_ge(st_turned, 1)
            f.mark(dve.tensor_copy(sb_in[:, down[0], :], A[2][:]))
            f.link(dve.tensor_copy(sf[:, 0, :], A[3][:]))
            dve.sem_inc(sf_ready, 1)
            f.mark(dve.memset(sb_in[:, NT - 1, :], 0.0))
            dve.wait_ge(dt_pe, 2)
            cum = Q[:, 1, 0:NT * 16].rearrange("p (c h) -> p c h", h=16)
            tot = Q[:, 0, 0:NT * 16].rearrange("p (c h) -> p c h", h=16)
            f.mark(dve.tensor_tensor(u[:], cum, krow(K_SA), ALU.mult))
            f.link(dve.tensor_tensor(t3[:], da[:], krow(K_SB), ALU.mult))
            f.link(dve.tensor_tensor(u[:], u[:], t3[:], ALU.add))
            dve.wait_ge(dt_act, 5)
            f.mark(dve.tensor_tensor(eoff[:], tot, krow(K_MT), ALU.mult))
            f.link(dve.tensor_tensor(wgt[:], tot, krow(K_MD), ALU.mult))
            f.mark(dve.tensor_tensor(eoff[:], eoff[:], u[:], ALU.add))
            dve.tensor_tensor(wgt[:], wgt[:], u[:], ALU.subtract).then_inc(dt_dve, 1)
            f.link(dve.tensor_tensor(w[:], w[:], v[:], ALU.min))
            f.link(dve.tensor_tensor(up[:], u[:], w[:], ALU.subtract))
            dve.wait_ge(consts, 2)
            for i, x in enumerate((u, up)):
                f.link(dve.tensor_copy(rnd[:], x[:]))
                f.link(dve.tensor_copy(pack[:, i, :, 0:16], rnd[:].bitcast(F32)))
                dve.tensor_tensor(pack[:, i, :, 32:48], x[:], rnd[:].bitcast(F32), ALU.subtract).then_inc(packed, 1)
                dve.wait_ge(packed, i + 1)
            dve.wait_ge(dt_act, 7)
            f.mark(dve.tensor_tensor(wgt[:], wgt[:], dt[:], ALU.mult))
            for n, (which, c0, k) in enumerate(U_GROUPS):
                dve.wait_ge(u_turned, n + 1)
                dst = (u2, up2)[which]
                dve.tensor_copy(dst[:, c0 * P:(c0 + k) * P], Q[0:64, n % 2, 0:k * P]).then_inc(u_read, 1)
            f.wait()

            def weigh(n, c, slot, first):
                dve.tensor_tensor(heads(xw[:, slot, :]), heads(xs[:, c, :]), across(wgt[:, c, first:first + 8], SP_),
                                  ALU.mult).then_inc(xw_ready, 1)

            for i, c in enumerate(down):
                dve.wait_ge(x_copied, 3 * i + 3)
                if i >= 2:
                    dve.wait_ge(s_mm, i - 1)
                weigh(i, c, i % 2, 8)
                dve.wait_ge(s_mm, i + 1)
                if c != 0:
                    f.link(dve.tensor_tensor(heads(tmp[:]), heads(sb_in[:, c, :]), across(cdrow[:, c, 8:16], SP_),
                                             ALU.mult))
                    dst = fin[:, 1, :] if c == NT_LAT else sb_in[:, c - 1, :]
                    f.link(dve.tensor_tensor(dst, tmp[:], Q[:, i % 2, :], ALU.add))
                dve.sem_inc(s_ready, 1)

            def mix(c):
                dve.wait_ge(y_turned, c + 1)
                dve.tensor_tensor(mix_out[:, c, :].rearrange("p (a t) -> p a t", a=4), A[0][:].rearrange("p (a t) -> p a t", a=4),
                                  across(L.cols[:, C_GS:C_GS + 4], P), ALU.mult).then_inc(mix_ready, 1)

            for c in range(NT):
                dve.wait_ge(s_mm, NT + c)
                weigh(NT + c, c, 0, 0)
                dve.wait_ge(exp_done, c + 1)
                if c >= 1:
                    dve.wait_ge(diag_done, c)
                f.link(dve.tensor_tensor(wt[:], seg[:, 0:SH, :], seg[:, SH:2 * SH, :], ALU.add))
                dve.wait_ge(cb_read, c + 1)
                dve.tensor_tensor(wt[:].rearrange("p (g r) l -> p g r l", g=2),
                                  wt[:].rearrange("p (g r) l -> p g r l", g=2),
                                  cb[:].unsqueeze(2).to_broadcast([P, 2, 4, P]), ALU.mult).then_inc(w_ready, 1)
                dve.wait_ge(off_done, c + 1)
                if c >= 1:
                    dve.wait_ge(yn_ready, c)
                f.mark(dve.tensor_tensor(heads(yv[:]), heads(A[1][:]), across(eoff[:, c, 0:8], SP_), ALU.mult))
                f.link(dve.tensor_tensor(heads(off_b[:]), heads(A[2][:]), across(eoff[:, c, 8:16], SP_), ALU.mult))
                dve.sem_inc(off_read, 1)
                f.link(dve.tensor_tensor(yv[:], yv[:], off_b[:], ALU.add))
                if c >= 1:
                    mix(c - 1)
                dve.wait_ge(s_mm, NT + c + 1)
                if c == NT_LAT - 1:
                    f.link(dve.memset(sf[:, 1 - c % 2, :], 0.0))
                else:
                    dve.wait_ge(dec_ready, c + 1 - (c >= NT_LAT))
                    dst = fin[:, 0, :] if c == NT - 1 else sf[:, 1 - c % 2, :]
                    f.link(dve.tensor_tensor(dst, decayed[:], A[0][:], ALU.add))
                dve.sem_inc(sf_ready, 1)
                dve.wait_ge(diag_done, c + 1)
                f.link(dve.tensor_tensor(yv[:], yv[:], A[3][:], ALU.add))
                dve.tensor_tensor(yv[:], yv[:], zt[:, c, :], ALU.mult).then_inc(y_ready, 1)
            mix(NT - 1)
            for d in range(2):
                dve.wait_ge(fin_mm, d + 1)
                dve.tensor_copy(st_in[:, d, :, :], A[1 + d][:].rearrange("p (a n) -> p a n", a=4)).then_inc(fin_cp, 1)

        @block.tensor
        def _(pe):
            for c in range(NT):
                mm = pe.transpose(Q[:, 0, c * 16:(c + 1) * 16], L.dtT[0:16, chunk(c)], L.const[0:16, 0:16])
            mm.then_inc(dt_turned, 1)
            pe.wait_ge(st_loaded, 64)
            for a in range(4):
                pe.transpose(A[2][:, chunk(a)], st_in[:, 1, a, :], L.ident)
            for a in range(4):
                mm = pe.transpose(A[3][:, chunk(a)], st_in[:, 0, a, :], L.ident)
            mm.then_inc(st_turned, 1)
            pe.wait_ge(dt_dve, 4)
            pe.wait_ge(consts, 1)
            pe.matmul(Q[:, 0, 0:NT * 16], L.ones[:], flat(da[:]), start=True, stop=True).then_inc(dt_pe, 1)
            pe.matmul(Q[:, 1, 0:NT * 16], L.const[:, K_TRI:K_TRI + P], flat(da[:]), start=True, stop=True
                      ).then_inc(dt_pe, 1)

            def turn(i):
                c = down[i]
                if i >= 2:
                    pe.wait_ge(x_copied, 3 * i - 3)
                else:
                    pe.wait_ge(sf_ready, 1)
                for a in range(4):
                    pe.transpose(A[i % 2][:, chunk(a)], L.xbcT[:, a, chunk(c)], L.ident)
                for g in range(2):
                    pe.transpose(A[2 + i % 2][:, chunk(g)], L.xbcT[:, 4 + g, chunk(c)], L.ident)
                pe.wait_ge(z_loaded[i % 2], 16 * (i // 2 + 1))
                for a in range(4):
                    mm = pe.transpose(Q[:, 2 + i % 2, chunk(a)], zc[:, i % 2, a, :], L.ident)
                mm.then_inc(x_turned, 1)

            turn(0)
            turn(1)
            for n, (which, c0, k) in enumerate(U_GROUPS):
                if n == 0:
                    pe.wait_ge(dt_dve, 5)
                pe.wait_ge(packed, which + 1)
                if n >= 2:
                    pe.wait_ge(u_read, n - 1)
                for j in range(k):
                    mm = pe.transpose(Q[0:64, n % 2, chunk(j)], pack[:, which, c0 + j, :], L.ident)
                mm.then_inc(u_turned, 1)

            def contribution(n, c, slot, dst):
                pe.wait_ge(xw_ready, n + 1)
                for g in range(2):
                    mm = pe.matmul(dst[:, g * 256:(g + 1) * 256], bt[:, c, g, :], xw[:, slot, g * 256:(g + 1) * 256],
                                   start=True, stop=True)
                mm.then_inc(s_mm, 1)

            for i, c in enumerate(down):
                if 2 <= i + 1 < NT:
                    turn(i + 1)
                if i == 0:
                    pe.wait_ge(u_read, len(U_GROUPS))
                if i >= 2:
                    pe.wait_ge(s_ready, i - 1)
                contribution(i, c, i % 2, Q[:, i % 2, :])

            def segments(c):
                pe.wait_ge(exp_done, c) if c else None
                for q in range(4):
                    pe.matmul(Q[:, q, :], up2[:, chunk(c)], flat(negsel[:, 4 * q:4 * q + 4, :]), start=True,
                              stop=False)
                    pe.matmul(Q[:, q, :], identb[:], flat(maskb[:, q // 2, :, :]), start=False, stop=False)
                    for h in range(4):
                        mm = pe.matmul(Q[:, q, chunk(h)], sel[:, 4 * q + h, :], u2[:, chunk(c)], start=False,
                                       stop=(h == 3))
                mm.then_inc(seg_done, 1)

            def y_turn(c):
                pe.wait_ge(yn_ready, c + 1)
                for a in range(4):
                    mm = pe.transpose(A[0][:, chunk(a)], yn[:, chunk(a)], L.ident)
                mm.then_inc(y_turned, 1)

            pe.wait_ge(consts, 8)
            pe.wait_ge(s_ready, NT)
            pe.wait_ge(x_copied, 3 * NT)
            for c in range(NT):
                if c == 0:
                    segments(0)
                if c >= 1:
                    pe.wait_ge(sf_ready, c + 1)
                for g in range(2):
                    mm = pe.matmul(A[0][:, chunk(g)], L.xbcT[:, 4 + g, chunk(c)], L.xbcT[:, 6 + g, chunk(c)],
                                   start=True, stop=True)
                mm.then_inc(cb_done, 1)
                if c >= 1:
                    pe.wait_ge(off_read, c)
                for d, state in ((0, sf[:, c % 2, :]), (1, sb_in[:, c, :])):
                    for g in range(2):
                        mm = pe.matmul(A[1 + d][:, g * 256:(g + 1) * 256], L.xbcT[:, 6 + g, chunk(c)],
                                       state[:, g * 256:(g + 1) * 256], start=True, stop=True)
                mm.then_inc(off_done, 1)
                if c >= 1:
                    pe.wait_ge(y_ready, c)
                for a in range(4):
                    pe.matmul(A[3][:, chunk(a)], L.xbcT[:, a, chunk(c)], ddiag[:, a, :], start=(a == 0), stop=False)
                if c + 1 < NT:
                    segments(c + 1)
                pe.wait_ge(w_ready, c + 1)
                for h in range(SH):
                    mm = pe.matmul(A[3][:, h * SP_:(h + 1) * SP_], wt[:, h, :], xs[:, c, h * SP_:(h + 1) * SP_],
                                   start=False, stop=(h == SH - 1))
                mm.then_inc(diag_done, 1)
                pe.wait_ge(cb_read, c + 1)
                if c >= 1:
                    y_turn(c - 1)
                    pe.wait_ge(mix_ready, c)
                contribution(NT + c, c, 0, A[0])
            pe.wait_ge(sf_ready, NT + 1)
            y_turn(NT - 1)
            for d in range(2):
                for a in range(4):
                    mm = pe.transpose(A[1 + d][:, chunk(a)], fin[:, d, chunk(a)], L.ident)
                mm.then_inc(fin_mm, 1)


def phase_attn_prep(L):
    nc = L.nc
    with ExitStack() as st:
        qT = L.sb(st, "qT", [P, KQ, T])
        kvT = L.sb(st, "kvT", [P, KKV, T])
        ropeT = L.sb(st, "ropeT", [P, T])
        sq = L.sb(st, "sq", [P, KQ, T])
        rstd = L.sb(st, "bc_rstd", [P, 2, T])
        ckv = L.sb(st, "ckv", [P, KKV, NKEY])
        prod = L.sb(st, "rope_prod", [P, T])
        cc = L.sb(st, "cache_in", [P, 2, KV_LORA])
        cr = L.sb(st, "cachek_in", [P, 2, 2, ROPE])
        co = L.sb(st, "ckv_out", [P, 2, KV_LORA])
        ko = L.sb(st, "krope_out", [P, 2, ROPE])
        eps = L.sb(st, "eps", [P, 1])
        ps3 = L.ps(st, "ps3", [P, 3, 512])
        ps3b = L.ps(st, "ps3b", [P, 3, 512])
        psT = L.ps(st, "psT", [P, 2, 512])
        (c_loaded, t_loaded, q_loaded, kv_loaded, r_loaded, sq_done, sums, ms_ready, root, dch, turned, prod_ready, fold, ro_ready, out_ready,
         out_done, ones_rd) = (L.sem("ap_" + n) for n in (
             "c_loaded", "t_loaded", "q_loaded", "kv_loaded", "r_loaded", "sq_done", "sums", "ms_ready", "root", "dch", "turned", "prod_ready", "fold",
             "ro_ready", "out_ready", "out_done", "eps_ready"))
        block = st.enter_context(nc.Block())
        tok = lambda ap: flat(ap)[:, 0:T]

        @block.sync
        def _(sp):
            sp.dma_start(qT[:], L.staged[N_Z:N_Z + KQ].rearrange("a p t -> p a t")).then_inc(q_loaded, 16)
            sp.dma_start(kvT[:], L.staged[N_Z + KQ:N_Z + KQ + KKV].rearrange("a p t -> p a t")).then_inc(kv_loaded, 16)
            sp.dma_start(ropeT[:], L.staged[N_STAGED - 1]).then_inc(r_loaded, 16)
            sp.dma_start(L.table[:], L.dram["rope_table"]).then_inc(t_loaded, 16)
            sp.dma_start(cc[:], L.dram["cache_ckv"][0, 0].rearrange("(a p) n -> p a n", p=P)).then_inc(c_loaded, 16)
            for r in range(2):
                sp.dma_start(cr[:, :, r, :], L.dram["cache_krope"][0, 0].rearrange("(a p) n -> p a n", p=P)
                             ).then_inc(c_loaded, 16)
            sp.wait_ge(out_ready, 2)
            sp.dma_start(L.outs["ckv"][0, 0].rearrange("(a p) n -> p a n", p=P), co[:]).then_inc(out_done, 16)
            sp.dma_start(L.outs["krope"][0, 0].rearrange("(a p) n -> p a n", p=P), ko[:]).then_inc(out_done, 16)
            sp.wait_ge(out_done, 32)

        @block.gpsimd
        def _(pool):
            pool.memset(eps[:], EPS).then_inc(ones_rd, 1)

        @block.scalar
        def _(act):
            act.wait_ge(q_loaded, 16)
            act.activation(sq[:], qT[:], ACT.Square).then_inc(sq_done, 1)
            act.wait_ge(sums, 1)
            act.wait_ge(kv_loaded, 16)
            act.activation(sq[:, 0:KKV, :], kvT[:], ACT.Square).then_inc(sq_done, 1)
            act.wait_ge(ones_rd, 1)
            act.activation(rstd[:, 0, :], tok(ps3[:]), ACT.Sqrt, bias=eps[:], scale=1.0 / Q_LORA).then_inc(root, 1)
            act.wait_ge(sums, 2)
            act.activation(rstd[:, 1, :], tok(ps3b[:]), ACT.Sqrt, bias=eps[:], scale=1.0 / KV_LORA).then_inc(root, 1)

        @block.vector
        def _(dve):
            c = Chain(dve, dch)
            dve.wait_ge(t_loaded, 16)
            dve.wait_ge(r_loaded, 16)
            dve.tensor_tensor(prod[:], ropeT[:], L.table[:], ALU.mult).then_inc(prod_ready, 1)
            dve.wait_ge(turned, 1)
            c.mark(dve.tensor_copy(ckv[:, :, T:NKEY], psT[:, 0, :].rearrange("p (k t) -> p k t", k=2)))
            c.mark(dve.tensor_copy(L.kr_hi[:, T:NKEY], psT[:, 1, 0:N_CACHE]))
            c.wait()
            c.mark(dve.tensor_tensor(L.kr_lo[:, T:NKEY], psT[:, 1, 0:N_CACHE], L.kr_hi[:, T:NKEY].bitcast(F32),
                                     ALU.subtract))
            dve.tensor_copy(ko[:], psT[:, 1, 256:512].rearrange("p (a n) -> p a n", a=2)[:, :, 0:ROPE]
                            ).then_inc(out_ready, 1)
            dve.wait_ge(root, 1)
            dve.wait_ge(q_loaded, 16)
            c.link(dve.reciprocal(rstd[:, 0, :], rstd[:, 0, :]))
            for k in range(KQ):
                c.link(dve.scalar_tensor_tensor(qT[:, k, :], qT[:, k, :], L.cols[:, C_GQ + k:C_GQ + k + 1],
                                                rstd[:, 0, :], ALU.mult, ALU.mult))
                c.link(dve.tensor_copy(L.qn_hi[:, k, :], qT[:, k, :]))
                c.mark(dve.tensor_tensor(L.qn_lo[:, k, :], qT[:, k, :], L.qn_hi[:, k, :].bitcast(F32), ALU.subtract))
            dve.wait_ge(root, 2)
            dve.wait_ge(kv_loaded, 16)
            c.link(dve.reciprocal(rstd[:, 1, :], rstd[:, 1, :]))
            for k in range(KKV):
                c.mark(dve.scalar_tensor_tensor(ckv[:, k, 0:T], kvT[:, k, :], L.cols[:, C_GKV + k:C_GKV + k + 1],
                                                rstd[:, 1, :], ALU.mult, ALU.mult))
            c.wait()
            dve.sem_inc(prod_ready, 1)
            c.link(dve.tensor_copy(L.ckv_hi[:], ckv[:]))
            c.mark(dve.tensor_tensor(L.ckv_lo[:], ckv[:], L.ckv_hi[:].bitcast(F32), ALU.subtract))
            dve.wait_ge(fold, 1)
            c.link(dve.tensor_copy(L.kr_hi[:, 0:T], tok(ps3[:])))
            c.mark(dve.tensor_tensor(L.kr_lo[:, 0:T], tok(ps3[:]), L.kr_hi[:, 0:T].bitcast(F32), ALU.subtract))
            dve.wait_ge(turned, 2)
            dve.tensor_copy(co[:], psT[:, 0, :].rearrange("p (a n) -> p a n", a=2)).then_inc(out_ready, 1)
            c.wait()

        @block.tensor
        def _(pe):
            pe.wait_ge(c_loaded, 48)
            pe.wait_ge(r_loaded, 16)
            for k in range(2):
                for a in range(2):
                    pe.transpose(psT[:, 0, (2 * k + a) * P:(2 * k + a + 1) * P], cc[:, a, k * P:(k + 1) * P], L.ident)
            for a in range(2):
                pe.transpose(psT[:, 1, a * P:(a + 1) * P], cr[:, a, :, :], L.ident)
            for a in range(2):
                mm = pe.transpose(psT[:, 1, (2 + a) * P:(3 + a) * P], ropeT[:, N_LAT + a * P:N_LAT + (a + 1) * P],
                                  L.ident)
            mm.then_inc(turned, 1)
            for i, (kn, ps) in enumerate(((KQ, ps3), (KKV, ps3b))):
                pe.wait_ge(sq_done, i + 1)
                for b, (c0, w) in enumerate(BLOCKS):
                    for k in range(kn):
                        mm = pe.matmul(ps[:, b, :w], L.ones[:], sq[:, k, c0:c0 + w], start=(k == 0), stop=(k == kn - 1))
                mm.then_inc(sums, 1)
            pe.wait_ge(prod_ready, 1)
            pe.wait_ge(root, 1)
            for b, (c0, w) in enumerate(BLOCKS):
                mm = pe.matmul(ps3[:, b, :w], L.fold, prod[:, c0:c0 + w], start=True, stop=True)
            mm.then_inc(fold, 1)
            pe.wait_ge(prod_ready, 2)
            pe.wait_ge(dch, 1)
            for a in range(2):
                for k in range(2):
                    mm = pe.transpose(psT[:, 0, (2 * a + k) * P:(2 * a + k + 1) * P],
                                      ckv[:, k, N_LAT + a * P:N_LAT + (a + 1) * P], L.ident)
            mm.then_inc(turned, 1)


def phase_attention(L):
    nc = L.nc
    with ExitStack() as st:
        wq_raw = L.sb(st, "wq_raw", [P, KQ, 256])
        wk_raw = L.sb(st, "wk_raw", [P, KKV, P])
        wv_raw = L.sb(st, "wv_raw", [P, KKV, 256])
        wq_hi, wq_lo = (L.sb(st, f"wq_{n}", [P, KQ, 256], F32R) for n in ("hi", "lo"))
        wk_hi, wk_lo = (L.sb(st, f"wk_{n}", [P, KKV, P], F32R) for n in ("hi", "lo"))
        wv_hi, wv_lo = (L.sb(st, f"wv_{n}", [P, KKV, 256], F32R) for n in ("hi", "lo"))
        kn_hi, kn_lo = (L.sb(st, f"kn_{n}", [P, NKEY], F32R) for n in ("hi", "lo"))
        v_hi, v_lo = (L.sb(st, f"v_{n}", [P, NKEY // P, 2, VD], F32R) for n in ("hi", "lo"))
        q_hi, q_lo = (L.sb(st, f"q_{n}", [P, T], F32R) for n in ("hi", "lo"))
        qr = L.sb(st, "q_rope", [P, T], F32R)
        prod = L.sb(st, "q_prod", [P, T])
        prob = L.sb(st, "prob", [P, 3, T])
        pt_hi, pt_lo = (L.sb(st, f"pt_{n}", [P, NT, 2 * P], F32R) for n in ("hi", "lo"))
        mx, nm, sm, rc = (L.sb(st, f"sm_{n}", [P, HEADS * NT]) for n in ("mx", "nm", "sum", "rec"))
        psS = L.ps(st, "psScore", [P, 5, 512])
        psPT = L.ps(st, "psPT", [P, 2, 4, P])
        psO = L.ps(st, "psO", [P, 2 * P])
        (wl, wvl, w_hi_r, w_split, proj, drained, hi_done, score, m_ready, nm_ready, e_ready,
         p_ready, pt_done, pth_ready, ptl_ready, pv, o_read, dch) = (L.sem("at_" + n) for n in (
             "wl", "wvl", "w_hi", "w_split", "proj", "drained", "hi_done", "score", "m_ready",
             "nm_ready", "e_ready", "p_ready", "pt_done", "pth_ready", "ptl_ready", "pv", "o_read", "dch"))
        block = st.enter_context(nc.Block())
        S = flat(psS[:])
        units = [(h, t) for h in range(HEADS) for t in range(NT)]
        key_tiles = lambda t: list(range(NT_LAT, NT)) if t >= NT_LAT else list(range(NT_LAT)) + [NT, NT + 1]
        groups = lambda t: [list(range(g, min(g + 4, len(key_tiles(t))))) for g in range(0, len(key_tiles(t)), 4)]
        n_groups = lambda u: sum(len(groups(units[i][1])) for i in range(u))
        width = lambda t: len(key_tiles(t)) * P

        def pieces(u):
            t, base = units[u][1], T * (u % 2)
            if t >= NT_LAT:
                return [(base, N_LAT, N_PROMPT)]
            if base == 0:
                return [(0, 0, 512), (512, 512, 512), (1024, T, N_CACHE)]
            return [(1536, 0, 512), (2048, 512, 512), (1280, T, N_CACHE)]

        def tile_col(u, i):
            kt = key_tiles(units[u][1])[i]
            for col, k0, w in pieces(u):
                if k0 <= kt * P < k0 + w:
                    return col - T * (u % 2) + kt * P - k0
            raise ValueError(i)

        RING = [3, 4, 1, 0, 2]
        KEY_BLOCKS = [(0, 512), (512, 512), (1024, 512)]
        stage = {"qrope": BLOCKS, "k": KEY_BLOCKS, "fold": BLOCKS, "q": BLOCKS, "v": [(2 * i, 2) for i in range(6)]}
        order = ["qrope", "k", "fold", "q", "v"]

        def projections(h):
            kinds = order if h % 2 == 0 else order[:-1]
            return [(kind, b) for kind in kinds for b in range(len(stage[kind]))]

        n_proj = lambda h: sum(len(projections(i)) for i in range(h))
        n_high = lambda h: n_proj(h) - 3 * h

        def of_kind(h, kind):
            return [(b, n_proj(h) + i, i) for i, (k, b) in enumerate(projections(h)) if k == kind]

        def high_index(h, i):
            return n_high(h) + i - 3

        def operand(kind, b):
            c0, w = stage[kind][b]
            if kind == "v":
                return v_hi[:, c0:c0 + 2, :, :], v_lo[:, c0:c0 + 2, :, :], 512
            if kind == "fold":
                return qr[:, c0:c0 + w], qr[64:128, c0:c0 + w], w
            hi, lo = (kn_hi, kn_lo) if kind == "k" else (q_hi, q_lo)
            return hi[:, c0:c0 + w], lo[:, c0:c0 + w], w

        @block.sync
        def _(sp):
            for h in range(HEADS):
                if h >= 1:
                    sp.wait_ge(w_split, h)
                sp.dma_start(wq_raw[:], L.dram["w_uq"][h]).then_inc(wl, 16)
                sp.dma_start(wk_raw[:], L.dram["w_uk"][h]).then_inc(wl, 16)
                if h % 2 == 0:
                    sp.dma_start(wv_raw[:], L.dram["w_uv"][h // 2]).then_inc(wvl, 16)

        @block.scalar
        def _(act):
            def split(h):
                act.wait_ge(wl, 32 * (h + 1))
                if h >= 1:
                    act.wait_ge(proj, n_proj(h))
                act.activation(wq_hi[:], wq_raw[:], ACT.Copy).then_inc(w_hi_r, 1)
                act.activation(wk_hi[:], wk_raw[:], ACT.Copy).then_inc(w_hi_r, 1)
                if h % 2 == 0:
                    act.wait_ge(wvl, 16 * (h // 2 + 1))
                    act.activation(wv_hi[:], wv_raw[:], ACT.Copy).then_inc(w_hi_r, 1)

            def high(h, kind):
                for b, n, i in of_kind(h, kind):
                    hi, _, w = operand(kind, b)
                    src = psS[:, RING[i % 5], :w]
                    act.wait_ge(proj, n + 1)
                    if kind == "v":
                        src = src.rearrange("p (a h v) -> p a h v", a=2, h=2)
                    act.activation(hi, src, ACT.Copy).then_inc(hi_done, 1)

            def exp(u):
                w, base = width(units[u][1]), T * (u % 2)
                act.wait_ge(nm_ready, u + 1)
                act.activation(prob[:, u % 3, 0:w], S[:, base:base + w], ACT.Exp, bias=nm[:, u:u + 1], scale=SCALE,
                               accum_out=sm[:, u:u + 1]).then_inc(e_ready, 1)

            def pt(u):
                g0, r = n_groups(u), (u % 2) * P
                if u >= 2:
                    act.wait_ge(pv, u // 2)
                for i, g in enumerate(groups(units[u][1])):
                    act.wait_ge(pt_done, g0 + i + 1)
                    act.activation(pt_hi[:, g[0]:g[-1] + 1, r:r + P], psPT[:, (g0 + i) % 2, 0:len(g), :], ACT.Copy
                                   ).then_inc(pth_ready, 1)

            def out(pair):
                h, t = units[2 * pair]
                act.wait_ge(pv, pair + 1)
                act.activation(L.mixA[:, h, t * P:(t + 2) * P], psO[:], ACT.Copy).then_inc(o_read, 1)

            split(0)
            for kind in order[1:]:
                high(0, kind)
            for h in range(HEADS):
                for t in range(NT):
                    u = h * NT + t
                    if t % 2 == 0 and t >= 4:
                        out(u // 2 - 2)
                    if t >= 2:
                        pt(u - 2)
                    exp(u)
                    if t == 5 and h + 1 < HEADS:
                        split(h + 1)
                out(u // 2 - 1)
                pt(u - 1)
                if h + 1 < HEADS:
                    high(h + 1, "k")
                pt(u)
                if h + 1 < HEADS:
                    high(h + 1, "fold")
                out(u // 2)
                if h + 1 < HEADS:
                    high(h + 1, "q")
                    high(h + 1, "v")

        @block.vector
        def _(dve):
            c = Chain(dve, dch)

            def split(h):
                dve.wait_ge(w_hi_r, 2 * h + 2 + (h + 1) // 2)
                c.mark(dve.tensor_tensor(wq_lo[:], wq_raw[:], wq_hi[:].bitcast(F32), ALU.subtract))
                c.mark(dve.tensor_tensor(wk_lo[:], wk_raw[:], wk_hi[:].bitcast(F32), ALU.subtract))
                if h % 2 == 0:
                    dve.wait_ge(w_hi_r, 2 * h + 3 + h // 2)
                    c.mark(dve.tensor_tensor(wv_lo[:], wv_raw[:], wv_hi[:].bitcast(F32), ALU.subtract))
                c.wait()
                dve.sem_inc(w_split, 1)

            def rotate(h):
                for b, n, i in of_kind(h, "qrope"):
                    c0, w = BLOCKS[b]
                    dve.wait_ge(proj, n + 1)
                    dve.tensor_tensor(prod[:, c0:c0 + w], psS[:, RING[i % 5], :w], L.table[:, c0:c0 + w], ALU.mult
                                      ).then_inc(drained, 1)

            def low(h, kind):
                for b, n, i in of_kind(h, kind):
                    hi, lo, w = operand(kind, b)
                    src = psS[:, RING[i % 5], :w]
                    dve.wait_ge(hi_done, high_index(h, i) + 1)
                    if kind == "v":
                        src = src.rearrange("p (a h v) -> p a h v", a=2, h=2)
                    if kind == "fold":
                        src, hi = src[64:128, :], lo
                    dve.tensor_tensor(lo, src, hi.bitcast(F32), ALU.subtract).then_inc(drained, 1)

            def maximum(u):
                w, base = width(units[u][1]), T * (u % 2)
                dve.wait_ge(score, u + 1)
                dve.tensor_reduce(mx[:, u:u + 1], S[:, base:base + w], AX_X, ALU.max).then_inc(m_ready, 1)
                dve.wait_ge(m_ready, u + 1)
                dve.tensor_scalar(nm[:, u:u + 1], mx[:, u:u + 1], -SCALE, None, ALU.mult).then_inc(nm_ready, 1)

            def normalise(u):
                w = width(units[u][1])
                dve.wait_ge(e_ready, u + 1)
                c.link(dve.reciprocal(rc[:, u:u + 1], sm[:, u:u + 1]))
                dve.tensor_scalar(prob[:, u % 3, 0:w], prob[:, u % 3, 0:w], rc[:, u:u + 1], None, ALU.mult
                                  ).then_inc(p_ready, 1)

            def pt(u, part):
                g0, r = n_groups(u), (u % 2) * P
                for i, g in enumerate(groups(units[u][1])):
                    if (i >= 2) == bool(part):
                        dve.wait_ge(pth_ready, g0 + i + 1)
                        dve.tensor_tensor(pt_lo[:, g[0]:g[-1] + 1, r:r + P], psPT[:, (g0 + i) % 2, 0:len(g), :],
                                          pt_hi[:, g[0]:g[-1] + 1, r:r + P].bitcast(F32), ALU.subtract
                                          ).then_inc(ptl_ready, 1)

            split(0)
            rotate(0)
            for kind in order[1:]:
                low(0, kind)
            for h in range(HEADS):
                for t in range(NT):
                    u = h * NT + t
                    if t >= 2:
                        pt(u - 2, 0)
                    maximum(u)
                    if t >= 2:
                        pt(u - 2, 1)
                    if t >= 1:
                        normalise(u - 1)
                    if t == 5 and h + 1 < HEADS:
                        split(h + 1)
                if h + 1 < HEADS:
                    rotate(h + 1)
                normalise(u)
                for part in range(2):
                    pt(u - 1, part)
                if h + 1 < HEADS:
                    low(h + 1, "k")
                for part in range(2):
                    pt(u, part)
                if h + 1 < HEADS:
                    for kind in order[2:]:
                        low(h + 1, kind)

        @block.tensor
        def _(pe):
            def project(h, kind):
                for b, n, i in of_kind(h, kind):
                    if i == 0:
                        pe.wait_ge(w_split, h + 1)
                    if i >= 5:
                        pe.wait_ge(drained, n - 4)
                    elif h >= 1:
                        pe.wait_ge(e_ready, h * NT - (0 if i == 4 else 1 if i == 3 else 2))
                    c0, w = stage[kind][b]
                    bank = psS[:, RING[i % 5], :]
                    if kind == "fold":
                        pe.wait_ge(drained, n_proj(h) + b + 1)
                        mm = pe.matmul(bank[:, :w], L.fold, prod[:, c0:c0 + w], start=True, stop=True)
                    elif kind == "v":
                        for j in range(2):
                            ks = slice((c0 + j) * P, (c0 + j + 1) * P)
                            for k in range(KKV):
                                mm = split3(pe, bank[:, j * 256:(j + 1) * 256], L.ckv_hi[:, k, ks], L.ckv_lo[:, k, ks],
                                            wv_hi[:, k, :], wv_lo[:, k, :], k == 0, k == KKV - 1)
                    else:
                        w_hi, w_lo, x_hi, x_lo, kn = ((wk_hi, wk_lo, L.ckv_hi, L.ckv_lo, KKV) if kind == "k" else
                                                      (wq_hi, wq_lo, L.qn_hi, L.qn_lo, KQ))
                        cols = slice(128, 256) if kind == "qrope" else slice(0, 128)
                        for k in range(kn):
                            mm = split3(pe, bank[:, :w], w_hi[:, k, cols], w_lo[:, k, cols], x_hi[:, k, c0:c0 + w],
                                        x_lo[:, k, c0:c0 + w], k == 0, k == kn - 1)
                    mm.then_inc(proj, 1)

            def scores(u, part):
                t, shared = units[u][1], pieces(u)[-1:]
                if len(pieces(u)) == 1 and u % 2 == 0:
                    shared = []
                todo = shared if part else pieces(u)[:len(pieces(u)) - len(shared)]
                if u % NT == 0 and part == 0:
                    pe.wait_ge(drained, n_proj(units[u][0] + 1))
                elif u % NT >= 1 + (part == 0):
                    pe.wait_ge(e_ready, u - 1 + part)
                q = slice(t * P, (t + 1) * P)
                for col, k0, w in todo:
                    out, ks = S[:, col:col + w], slice(k0, k0 + w)
                    pe.matmul(out, q_hi[:, q], kn_hi[:, ks], start=True, stop=False)
                    pe.matmul(out, q_hi[:, q], kn_lo[:, ks], start=False, stop=False)
                    pe.matmul(out, q_lo[:, q], kn_hi[:, ks], start=False, stop=False)
                    pe.matmul(out, qr[:, q], L.kr_hi[:, ks], start=False, stop=False)
                    mm = pe.matmul(out, qr[:, q], L.kr_lo[:, ks], start=False, stop=True)
                    if (col, k0, w) == pieces(u)[-1]:
                        mm.then_inc(score, 1)

            def transposes(u, part):
                g0 = n_groups(u)
                pe.wait_ge(p_ready, u + 1)
                for i, g in enumerate(groups(units[u][1])):
                    if (i >= 2) != bool(part):
                        continue
                    if g0 + i >= 2:
                        pe.wait_ge(ptl_ready, g0 + i - 1)
                    for n, kt in enumerate(g):
                        mm = pe.transpose(psPT[:, (g0 + i) % 2, n, :],
                                          prob[:, u % 3, tile_col(u, kt):tile_col(u, kt) + P], L.ident)
                    mm.then_inc(pt_done, 1)

            def values(pair):
                h, t = units[2 * pair]
                kts = key_tiles(t)
                if pair >= 1:
                    pe.wait_ge(o_read, pair)
                pe.wait_ge(ptl_ready, n_groups(2 * pair + 2))
                for n, kt in enumerate(kts):
                    mm = split3(pe, psO[:], v_hi[:, kt, h % 2, :], v_lo[:, kt, h % 2, :], pt_hi[:, n, :],
                                pt_lo[:, n, :], n == 0, n == len(kts) - 1)
                mm.then_inc(pv, 1)

            for kind in order:
                project(0, kind)
            for h in range(HEADS):
                for t in range(NT):
                    u = h * NT + t
                    scores(u, 0)
                    if t % 2 == 0 and t >= 4:
                        values(u // 2 - 2)
                    if t >= 2:
                        transposes(u - 2, 0)
                    scores(u, 1)
                    if t >= 2:
                        transposes(u - 2, 1)
                if h + 1 < HEADS:
                    project(h + 1, "qrope")
                values(u // 2 - 1)
                for part in range(2):
                    transposes(u - 1, part)
                if h + 1 < HEADS:
                    project(h + 1, "k")
                for part in range(2):
                    transposes(u, part)
                if h + 1 < HEADS:
                    project(h + 1, "fold")
                values(u // 2)
                if h + 1 < HEADS:
                    project(h + 1, "q")
                    if (h + 1) % 2 == 0:
                        project(h + 1, "v")


class GateRows:

    def __init__(self, L, st, tag, part, g_post):
        self.L, self.part, self.g_post = L, part, g_post
        self.rows = L.sb(st, f"{tag}_rows", [P, 2, D])
        self.b = L.sb(st, f"{tag}_b", [P, D])
        self.g = L.sb(st, f"{tag}_g", [P, D])
        self.loaded, self.ready = L.sem(f"{tag}_g_loaded"), L.sem(f"{tag}_g_ready")

    def load(self, eng):
        c = slice(self.part * D, (self.part + 1) * D)
        for g in range(2):
            eng.dma_start(self.rows[:, g, :], self.L.gate_rows[g:g + 1, c].to_broadcast([P, D])
                          ).then_inc(self.loaded, 16)
        eng.dma_start(self.b[:], self.L.dram["b_mod"][:, c].to_broadcast([P, D])).then_inc(self.loaded, 16)
        eng.dma_start(self.g[:], self.L.dram[self.g_post].to_broadcast([P, D])).then_inc(self.loaded, 16)

    def dve(self, dve):
        dve.wait_ge(self.loaded, 64)
        for g in range(2):
            dve.tensor_tensor(self.rows[:, g, :], self.rows[:, g, :], self.b[:], ALU.add).then_inc(self.ready, 1)
            dve.wait_ge(self.ready, 2 * g + 1)
            dve.tensor_tensor(self.rows[:, g, :], self.rows[:, g, :], self.g[:], ALU.mult).then_inc(self.ready, 1)
        dve.wait_ge(self.ready, 4)


def phase_out_proj(L):
    nc = L.nc
    with ExitStack() as st:
        raw = L.sb(st, "wo_raw", [P, 4, D])
        w_hi, w_lo = (L.sb(st, f"wo_{n}", [P, KD, D], F32R) for n in ("hi", "lo"))
        m_hi, m_lo = (L.sb(st, f"mix_{n}", [P, 2, KD, P], F32R) for n in ("hi", "lo"))
        mixS = L.sb(st, "op_mixS", [P, 2, 4, P])
        xin = L.sb(st, "op_x", [P, 2, D])
        y = L.sb(st, "op_y", [P, 2, D])
        junk = L.sb(st, "op_sq", [P, D])
        ss, ms, rs, nh = (L.sb(st, f"op_{n}", [P, NT] if n != "nh" else [P, 1]) for n in ("ss", "ms", "rs", "nh"))
        ss2, ms2, rs2 = (L.sb(st, f"op_{n}2", [P, NT]) for n in ("ss", "ms", "rs"))
        gate = GateRows(L, st, "op", 2, "g_post_mix")
        psY = L.ps(st, "psY", [P, 2, 2, 512])
        w_loaded = [L.sem(f"wo_loaded{i}") for i in range(4)]
        x_loaded = [L.sem(f"op_x_loaded{i}") for i in range(2)]
        s_loaded = [L.sem(f"op_s_loaded{i}") for i in range(2)]
        y_stored = [L.sem(f"op_y_stored{i}") for i in range(2)]
        (sq2, ms2_r, rs2_r, xn_r, w_hi_r, w_lo_r, m_hi_r, m_lo_r, done, sq, ms_r, rs_r, yt, y_r, pch) = (L.sem("op_" + n) for n in (
            "y_squared", "y_ms", "y_rstd", "xn", "w_hi", "w_lo", "m_hi", "m_lo", "product", "squared", "ms", "rstd", "scaled", "y", "pool"))
        block = st.enter_context(nc.Block())

        def x_tile(t):
            if t < NT_LAT:
                return L.dram["x_sample"][t * P:(t + 1) * P, :]
            return L.dram["x_prompt"][(t - NT_LAT) * P:(t - NT_LAT + 1) * P, :]

        def mixes(t):
            return L.mixA[:, :, t * P:(t + 1) * P], mixS[:, t % 2, :, :]

        @block.sync
        def _(sp):
            def load_mix(t):
                if t >= 2:
                    sp.wait_ge(m_lo_r, 2 * t - 2)
                sp.dma_start(flat(mixS[:, t % 2, :, :]), L.mixS[t]).then_inc(s_loaded[t % 2], 16)

            load_mix(0)
            load_mix(1)
            for k in range(KD):
                if k >= 4:
                    sp.wait_ge(w_lo_r, k - 3)
                sp.dma_start(raw[:, k % 4, :], L.dram["w_out"][k * P:(k + 1) * P, :]).then_inc(w_loaded[k % 4], 16)
            gate.load(sp)
            for t in range(NT):
                if t >= 2:
                    sp.wait_ge(y_r, t - 1)
                sp.dma_start(xin[:, t % 2, :], x_tile(t)).then_inc(x_loaded[t % 2], 16)
                if t + 2 < NT:
                    load_mix(t + 2)
                if t >= 1:
                    sp.wait_ge(y_r, t)
                    sp.dma_start(L.y1[t - 1], y[:, (t - 1) % 2, :]).then_inc(y_stored[(t - 1) % 2], 16)
            sp.wait_ge(y_r, NT)
            sp.dma_start(L.y1[NT - 1], y[:, (NT - 1) % 2, :]).then_inc(y_stored[(NT - 1) % 2], 16)
            for i in range(2):
                sp.wait_ge(y_stored[i], 16 * (NT // 2))

        @block.gpsimd
        def _(pool):
            pool.memset(nh[:], -0.5).then_inc(pch, 1)
            pool.wait_ge(pch, 1)
            for t in range(NT):
                pool.wait_ge(ms_r, t + 1)
                pool.tensor_tensor(rs[:, t:t + 1], ms[:, t:t + 1], nh[:], ALU.pow).then_inc(rs_r, 1)
                pool.wait_ge(ms2_r, t + 1)
                pool.tensor_tensor(rs2[:, t:t + 1], ms2[:, t:t + 1], nh[:], ALU.pow).then_inc(rs2_r, 1)

        @block.scalar
        def _(act):
            def mix_hi(t):
                if t >= 2:
                    act.wait_ge(done, t - 1)
                act.wait_ge(s_loaded[t % 2], 16 * (t // 2 + 1))
                for i, mix in enumerate(mixes(t)):
                    act.activation(m_hi[:, t % 2, 4 * i:4 * i + 4, :], mix, ACT.Copy
                                   ).then_inc(m_hi_r, 1)

            mix_hi(0)
            for k in range(KD):
                act.wait_ge(w_loaded[k % 4], 16 * (k // 4 + 1))
                act.activation(w_hi[:, k, :], raw[:, k % 4, :], ACT.Copy).then_inc(w_hi_r, 1)
            for t in range(NT):
                if t + 1 < NT:
                    mix_hi(t + 1)
                act.wait_ge(done, t + 1)
                if t >= 1:
                    act.wait_ge(sq2, t)
                act.activation(junk[:], flat(psY[:, t % 2, :, :]), ACT.Square, accum_out=ss[:, t:t + 1]
                               ).then_inc(sq, 1)
                act.wait_ge(y_r, t + 1)
                act.wait_ge(sq, t + 1)
                act.activation(L.facc[:, t, :], y[:, t % 2, :], ACT.Square, accum_out=ss2[:, t:t + 1]
                               ).then_inc(sq2, 1)

        @block.vector
        def _(dve):
            def mix_lo(t):
                dve.wait_ge(m_hi_r, 2 * t + 2)
                for i, mix in enumerate(mixes(t)):
                    dve.tensor_tensor(m_lo[:, t % 2, 4 * i:4 * i + 4, :], mix,
                                      m_hi[:, t % 2, 4 * i:4 * i + 4, :].bitcast(F32), ALU.subtract
                                      ).then_inc(m_lo_r, 1)

            mix_lo(0)
            for k in range(KD):
                dve.wait_ge(w_hi_r, k + 1)
                dve.tensor_tensor(w_lo[:, k, :], raw[:, k % 4, :], w_hi[:, k, :].bitcast(F32), ALU.subtract
                                  ).then_inc(w_lo_r, 1)
            gate.dve(dve)
            for t in range(NT):
                if t + 1 < NT:
                    mix_lo(t + 1)
                s, g = t % 2, int(t >= NT_LAT)
                dve.wait_ge(sq, t + 1)
                dve.tensor_scalar(ms[:, t:t + 1], ss[:, t:t + 1], 1.0 / D, EPS, ALU.mult, ALU.add).then_inc(ms_r, 1)
                dve.wait_ge(rs_r, t + 1)
                if t >= 2:
                    dve.wait_ge(y_stored[s], 16 * (t // 2))
                    dve.wait_ge(xn_r, t - 1)
                dve.scalar_tensor_tensor(y[:, s, :], flat(psY[:, s, :, :]), rs[:, t:t + 1], gate.rows[:, g, :],
                                         ALU.mult, ALU.mult).then_inc(yt, 1)
                dve.wait_ge(yt, t + 1)
                dve.wait_ge(x_loaded[s], 16 * (t // 2 + 1))
                dve.tensor_tensor(y[:, s, :], y[:, s, :], xin[:, s, :], ALU.add).then_inc(y_r, 1)
                dve.wait_ge(sq2, t + 1)
                dve.tensor_scalar(ms2[:, t:t + 1], ss2[:, t:t + 1], 1.0 / D, EPS, ALU.mult, ALU.add
                                  ).then_inc(ms2_r, 1)
                dve.wait_ge(rs2_r, t + 1)
                dve.tensor_scalar(L.facc[:, t, :], y[:, s, :], rs2[:, t:t + 1], None, ALU.mult).then_inc(xn_r, 1)

        @block.tensor
        def _(pe):
            for t in range(NT):
                pe.wait_ge(m_lo_r, 2 * t + 2)
                if t >= 2:
                    pe.wait_ge(yt, t - 1)
                for half in range(2):
                    cols = slice(half * 512, (half + 1) * 512)
                    for k in range(KD):
                        if t == 0 and half == 0:
                            pe.wait_ge(w_lo_r, k + 1)
                        mm = split3(pe, psY[:, t % 2, half, :], m_hi[:, t % 2, k, :], m_lo[:, t % 2, k, :],
                                    w_hi[:, k, cols], w_lo[:, k, cols], k == 0, k == KD - 1)
                mm.then_inc(done, 1)


def phase_ffn(L):
    nc = L.nc
    PAIRS = FT // 2
    GU = [(s, b) for s in range(2) for b in range(len(BLOCKS))]
    NG = len(GU)
    ND = 2 * NT
    with ExitStack() as st:
        raw_gu = L.sb(st, "raw_gu", [P, 2, D])
        raw_d = L.sb(st, "raw_d", [P, D])
        gu_hi, gu_lo = (L.sb(st, f"gu_{n}", [P, 2, 2, D], F32R) for n in ("hi", "lo"))
        d_hi, d_lo, h_hi, h_lo = L.d_hi, L.d_lo, L.h_hi, L.h_lo
        hid = L.sb(st, "hid", [P, 2, 512])
        psG = L.ps(st, "psG", [P, 2, 2, 512])
        psF = L.ps(st, "psF", [P, 4, 512])
        (gu_loaded, d_loaded, gu_hi_r, gu_lo_r, d_hi_r, d_lo_r, gu_used, silu, h_full, h_hi_r, h_lo_r, down,
         flushed) = (L.sem("ff_" + n) for n in (
             "gu_loaded", "d_loaded", "gu_hi", "gu_lo", "d_hi", "d_lo", "gu_used", "silu", "h_full", "h_hi", "h_lo",
             "down", "flushed"))
        turn = Turn(L, "n2", L.facc, psF, raw_d[:].rearrange("p (a n) -> p a n", a=2), L.h2_hi, L.h2_lo, L.scale2,
                    L.mod[:, 3 * KD:4 * KD, :])
        block = st.enter_context(nc.Block())

        def over_pairs(eng, body):
            body(0, True, False)
            with eng.Fori(1, PAIRS - 1) as i:
                body(i, False, False)
            body(PAIRS - 1, False, True)

        @block.sync
        def _(sp):
            def load_gu(n, first=False):
                if not first:
                    sp.wait_ge(gu_lo_r, n)
                for i, w in enumerate(("w_gate", "w_up")):
                    sp.dma_start(raw_gu[:, i, :], L.dram[w][bass.ds(n, 1)].rearrange("a p n -> (a p) n")
                                 ).then_inc(gu_loaded, 16)

            def load_d(n, first=False):
                if not first:
                    sp.wait_ge(d_lo_r, n)
                sp.dma_start(raw_d[:], L.dram["w_down"][bass.ds(n, 1)].rearrange("a p n -> (a p) n")
                             ).then_inc(d_loaded, 16)

            load_gu(0, True)
            load_gu(1)
            sp.wait_ge(turn.h_ready, len(turn.steps))
            load_d(0, True)
            load_d(1)
            with sp.Fori(1, PAIRS) as i:
                load_gu(2 * i)
                load_gu(2 * i + 1)
                load_d(2 * i)
                load_d(2 * i + 1)

        @block.scalar
        def _(act):
            def split_gu(n, s, first=False):
                act.wait_ge(gu_loaded, n * 32 + 32)
                if not first:
                    act.wait_ge(gu_used, n * 3 - 3)
                act.activation(gu_hi[:, s, :, :], raw_gu[:], ACT.Copy).then_inc(gu_hi_r, 1)

            def split_d(n, s, i, first=False):
                act.wait_ge(d_loaded, n * 16 + 16)
                if not first:
                    act.wait_ge(down, i * ND)
                act.activation(d_hi[:, s, :], raw_d[:], ACT.Copy).then_inc(d_hi_r, 1)

            def body(i, first, last):
                for n, (s, b) in enumerate(GU):
                    c0, w = BLOCKS[b]
                    act.wait_ge(gu_used, i * NG + (n + 1))
                    if not (first and n < 2):
                        act.wait_ge(h_lo_r, i * NG + (n - 1))
                    act.activation(hid[:, n % 2, :w], psG[:, n % 2, 0, :w], ACT.Silu).then_inc(silu, 1)
                    act.wait_ge(h_full, i * NG + (n + 1))
                    act.activation(h_hi[:, s, c0:c0 + w], hid[:, n % 2, :w], ACT.Copy).then_inc(h_hi_r, 1)
                    if first and n == 0:
                        turn.act(act, 16, 24)
                    if first and n in (1, 3):
                        split_d(n // 2, n // 2, 0, True)
                    if b == 2 and not last:
                        split_gu(i * 2 + (2 + s), s)
                if not last:
                    for s in range(2):
                        split_d(i * 2 + (2 + s), s, i + 1)

            for s in range(2):
                turn.act(act, 8 * s, 8 * s + 8)
                split_gu(s, s, True)
            over_pairs(act, body)

        @block.vector
        def _(dve):
            def split_gu(n, s):
                dve.wait_ge(gu_hi_r, n + 1)
                dve.tensor_tensor(gu_lo[:, s, :, :], raw_gu[:], gu_hi[:, s, :, :].bitcast(F32), ALU.subtract
                                  ).then_inc(gu_lo_r, 1)

            def split_d(n, s):
                dve.wait_ge(d_hi_r, n + 1)
                dve.tensor_tensor(d_lo[:, s, :], raw_d[:], d_hi[:, s, :].bitcast(F32), ALU.subtract
                                  ).then_inc(d_lo_r, 1)

            def body(i, first, last):
                for n, (s, b) in enumerate(GU):
                    c0, w = BLOCKS[b]
                    dve.wait_ge(silu, i * NG + (n + 1))
                    dve.tensor_tensor(hid[:, n % 2, :w], hid[:, n % 2, :w], psG[:, n % 2, 1, :w], ALU.mult
                                      ).then_inc(h_full, 1)
                    dve.wait_ge(h_hi_r, i * NG + (n + 1))
                    dve.tensor_tensor(h_lo[:, s, c0:c0 + w], hid[:, n % 2, :w], h_hi[:, s, c0:c0 + w].bitcast(F32),
                                      ALU.subtract).then_inc(h_lo_r, 1)
                    if first and n == 0:
                        turn.dve(dve, 16, 24)
                    if first and n in (1, 3):
                        split_d(n // 2, n // 2)
                    if b == 2 and not last:
                        split_gu(i * 2 + (2 + s), s)
                for r in range(0 if last else ND):
                    t, cols = r // 2, slice((r % 2) * 512, (r % 2) * 512 + 512)
                    dve.wait_ge(down, i * ND + (r + 1))
                    if first:
                        dve.tensor_copy(L.facc[:, t, cols], psF[:, r % 4, :]).then_inc(flushed, 1)
                    else:
                        dve.wait_ge(flushed, i * ND + (r - ND + 1))
                        dve.tensor_tensor(L.facc[:, t, cols], L.facc[:, t, cols], psF[:, r % 4, :], ALU.add
                                          ).then_inc(flushed, 1)
                if not last:
                    for s in range(2):
                        split_d(i * 2 + (2 + s), s)

            for s in range(2):
                turn.dve(dve, 8 * s, 8 * s + 8)
                split_gu(s, s)
            over_pairs(dve, body)

        @block.tensor
        def _(pe):
            def body(i, first, last):
                for n, (s, b) in enumerate(GU):
                    c0, w = BLOCKS[b]
                    if b == 0:
                        pe.wait_ge(gu_lo_r, i * 2 + (s + 1))
                    if not (first and n < 2):
                        pe.wait_ge(h_full, i * NG + (n - 1))
                    if first and s == 0:
                        pe.wait_ge(turn.h_ready, 8 * b + 8)
                    for j in range(2):
                        if first and n == 0:
                            turn.pe(pe, 8 + 4 * j, 12 + 4 * j)
                        if first and n == 1:
                            turn.pe(pe, 16 + 4 * j, 20 + 4 * j)
                        for k in range(KD):
                            ks = slice(k * P, (k + 1) * P)
                            mm = split3(pe, psG[:, n % 2, j, :w], gu_hi[:, s, j, ks], gu_lo[:, s, j, ks],
                                        L.h2_hi[:, k, c0:c0 + w], L.h2_lo[:, k, c0:c0 + w], k == 0, k == KD - 1)
                    mm.then_inc(gu_used, 1)
                if last:
                    return
                pe.wait_ge(d_lo_r, i * 2 + 2)
                for r in range(ND):
                    t, cols = r // 2, slice((r % 2) * 512, (r % 2) * 512 + 512)
                    if r in (0, 8, 16):
                        pe.wait_ge(h_lo_r, i * NG + (4 + r // 8))
                    if not (first and r < 4):
                        pe.wait_ge(flushed, i * ND + (r - 3))
                    ts = slice(t * P, (t + 1) * P)
                    for s in range(2):
                        mm = split3(pe, psF[:, r % 4, :], h_hi[:, s, ts], h_lo[:, s, ts], d_hi[:, s, cols],
                                    d_lo[:, s, cols], s == 0, s == 1)
                    mm.then_inc(down, 1)

            turn.pe(pe, 0, 8)
            over_pairs(pe, body)


def phase_final(L):
    nc = L.nc
    with ExitStack() as st:
        yin = L.sb(st, "fi_y", [P, 4, D])
        out = L.sb(st, "fi_out", [P, 3, D])
        junk = L.sb(st, "fi_sq", [P, D])
        ss, ms, rs, nh = (L.sb(st, f"fi_{n}", [P, NT] if n != "nh" else [P, 1]) for n in ("ss", "ms", "rs", "nh"))
        psF = L.ps(st, "fi_psF", [P, 4, 512])
        gate = GateRows(L, st, "fi", 5, "g_post_ffn")
        y_loaded = [L.sem(f"fi_y_loaded{i}") for i in range(4)]
        stored = [L.sem(f"fi_stored{i}") for i in range(3)]
        down, flushed = L.sem("fi_down"), L.sem("fi_flushed")
        sq, ms_r, rs_r, yt, y_r, pch = (L.sem("fi_" + n) for n in ("sq", "ms", "rs", "yt", "y", "pool"))
        block = st.enter_context(nc.Block())

        @block.sync
        def _(sp):
            gate.load(sp)
            for t in range(4):
                sp.dma_start(yin[:, t, :], L.y1[t]).then_inc(y_loaded[t], 16)
            for t in range(NT):
                sp.wait_ge(y_r, t + 1)
                dst = (L.outs["sample"][0, t * P:(t + 1) * P, :] if t < NT_LAT else
                       L.outs["prompt"][0, (t - NT_LAT) * P:(t - NT_LAT + 1) * P, :])
                sp.dma_start(dst, out[:, t % 3, :]).then_inc(stored[t % 3], 16)
                if t + 4 < NT:
                    sp.dma_start(yin[:, t % 4, :], L.y1[t + 4]).then_inc(y_loaded[t % 4], 16)
            for i in range(3):
                sp.wait_ge(stored[i], 16 * len(range(i, NT, 3)))

        @block.gpsimd
        def _(pool):
            pool.memset(nh[:], -0.5).then_inc(pch, 1)
            pool.wait_ge(pch, 1)
            for t in range(NT):
                pool.wait_ge(ms_r, t + 1)
                pool.tensor_tensor(rs[:, t:t + 1], ms[:, t:t + 1], nh[:], ALU.pow).then_inc(rs_r, 1)

        @block.scalar
        def _(act):
            for t in range(NT):
                act.wait_ge(flushed, t + 1)
                if t >= 1:
                    act.wait_ge(sq, t)
                act.activation(junk[:], L.facc[:, t, :], ACT.Square, accum_out=ss[:, t:t + 1]).then_inc(sq, 1)

        @block.vector
        def _(dve):
            gate.dve(dve)
            for t in range(NT + 2):
                if t < NT:
                    b = 2 * (t % 2)
                    dve.wait_ge(down, t + 1)
                    dve.tensor_tensor(L.facc[:, t, :], L.facc[:, t, :], flat(psF[:, b:b + 2, :]), ALU.add
                                      ).then_inc(flushed, 1)
                if 1 <= t <= NT:
                    dve.wait_ge(sq, t)
                    dve.tensor_scalar(ms[:, t - 1:t], ss[:, t - 1:t], 1.0 / D, EPS, ALU.mult, ALU.add
                                      ).then_inc(ms_r, 1)
                if t < 2:
                    continue
                u = t - 2
                dve.wait_ge(rs_r, u + 1)
                if u >= 3:
                    dve.wait_ge(stored[u % 3], 16 * (u // 3))
                dve.scalar_tensor_tensor(out[:, u % 3, :], L.facc[:, u, :], rs[:, u:u + 1],
                                         gate.rows[:, int(u >= NT_LAT), :], ALU.mult, ALU.mult).then_inc(yt, 1)
                dve.wait_ge(yt, u + 1)
                dve.wait_ge(y_loaded[u % 4], 16 * (u // 4 + 1))
                dve.tensor_tensor(out[:, u % 3, :], out[:, u % 3, :], yin[:, u % 4, :], ALU.add).then_inc(y_r, 1)

        @block.tensor
        def _(pe):
            for t in range(NT):
                if t >= 2:
                    pe.wait_ge(flushed, t - 1)
                ts = slice(t * P, (t + 1) * P)
                for half in range(2):
                    cols = slice(half * 512, half * 512 + 512)
                    for s in range(2):
                        mm = split3(pe, psF[:, 2 * (t % 2) + half, :], L.h_hi[:, s, ts], L.h_lo[:, s, ts],
                                    L.d_hi[:, s, cols], L.d_lo[:, s, cols], s == 0, s == 1)
                mm.then_inc(down, 1)


def hybrid_layer_kernel(nc, dram, outs):
    with ExitStack() as stack:
        L = Layer(nc, dram, outs)
        sb = L.sb
        L.const = sb(stack, "const", [P, N_CONST])
        L.ident = L.const[:, K_ID:K_ID + P]
        L.fold = L.const[:, K_FOLD:K_FOLD + P]
        L.cols = sb(stack, "cols", [P, N_COLS])
        L.mod = sb(stack, "mod", [P, 6 * KD, 2])
        L.scale1, L.scale2 = (sb(stack, f"scale{i}", [P, KD, 2]) for i in (1, 2))
        L.y1 = nc.dram_tensor("y1_scratch", (NT, P, D), F32, kind="Internal").ap()
        L.mixS = nc.dram_tensor("ssm_mix_scratch", (NT, P, SW), F32, kind="Internal").ap()
        L.staged = nc.dram_tensor("staged_scratch", (N_STAGED, P, T), F32, kind="Internal").ap()
        L.gate_rows = nc.dram_tensor("gate_rows", (2, 6 * D), F32, kind="Internal").ap()
        with ExitStack() as ssm:
            with ExitStack() as proj:
                L.cond_st = sb(proj, "cond_st", [P, KD, P])
                L.hT_hi, L.hT_lo = (sb(proj, f"hT_{n}", [P, KD, T], F32R) for n in ("hi", "lo"))
                phase_norm1(L)
                L.xbcT = sb(ssm, "xbcT", [P, N_XBC, T], side="right")
                L.dtT = sb(ssm, "dtT", [P, T], side="right")
                phase_in_proj(L)
            mixer = ExitStack()
            L.ones = sb(mixer, "ones", [P, P])
            phase_ssm(L)
        L.reuse_semaphores()
        with mixer:
            L.mixA = sb(mixer, "mixA", [P, HEADS, T])
            with ExitStack() as attn:
                L.table = sb(attn, "rope_table", [P, T])
                L.qn_hi, L.qn_lo = (sb(attn, f"qn_{n}", [P, KQ, T], F32R) for n in ("hi", "lo"))
                L.ckv_hi, L.ckv_lo = (sb(attn, f"ckv_{n}", [P, KKV, NKEY], F32R) for n in ("hi", "lo"))
                L.kr_hi, L.kr_lo = (sb(attn, f"kr_{n}", [P, NKEY], F32R) for n in ("hi", "lo"))
                phase_attn_prep(L)
                phase_attention(L)
            ffn = ExitStack()
            L.facc = sb(ffn, "facc", [P, NT, D], side="right")
            phase_out_proj(L)
        with ffn:
            L.d_hi, L.d_lo = (sb(ffn, f"d_{n}", [P, 2, D], F32R) for n in ("hi", "lo"))
            L.h_hi, L.h_lo = (sb(ffn, f"h_{n}", [P, 2, T], F32R) for n in ("hi", "lo"))
            with ExitStack() as h:
                L.h2_hi, L.h2_lo = (sb(h, f"h2_{n}", [P, KD, T], F32R) for n in ("hi", "lo"))
                phase_ffn(L)
            phase_final(L)


_OUTS = [("prompt", (1, N_PROMPT, D)), ("sample", (1, N_LAT, D)), ("ckv", (1, 1, N_PROMPT, KV_LORA)),
         ("krope", (1, 1, N_PROMPT, ROPE)), ("ssm", (1, 1, 2, SH, SP_, DS))]


def shape_constants(np):
    const = np.zeros((P, N_CONST), np.float32)
    i, j = np.arange(P)[:, None], np.arange(P)[None, :]
    const[:, K_ID:K_ID + P] = i == j
    const[:, K_MASK:K_MASK + P] = np.where(j >= i, 0.0, -1e30)
    const[:, K_MASK + P:K_MASK + 2 * P] = np.where(j <= i, 0.0, -1e30)
    h = np.arange(16)[None, :]
    const[:, K_SEL:K_SEL + 16] = (i == h) | (i == 32 + h)
    const[:, K_FOLD:K_FOLD + P] = (i % 64) == (j % 64)
    const[:, K_TRI:K_TRI + P] = i <= j
    forward = np.arange(16) < SH
    const[:, K_SA:K_SA + 16] = np.where(forward, 1.0, -1.0)
    const[:, K_SB:K_SB + 16] = np.where(forward, 0.0, 1.0)
    const[:, K_MT:K_MT + 16] = ~forward
    const[:, K_MD:K_MD + 16] = forward
    quarter = ROPE // 4
    inv = (np.float32(10000.0) ** (-np.arange(quarter, dtype=np.float32) / np.float32(quarter))).astype(np.float32)
    pos = np.arange(N_LAT)
    table = np.zeros((P, T), np.float32)
    table[0:ROPE, N_LAT:] = 1.0
    for half, where in enumerate((pos // 64, pos % 64)):
        ang = inv[:, None] * where[None, :].astype(np.float32)
        for part, sign in ((0, -1.0), (1, 1.0)):
            r = half * 2 * quarter + part * quarter
            table[r:r + quarter, 0:N_LAT] = np.cos(ang)
            table[ROPE + r:ROPE + r + quarter, 0:N_LAT] = sign * np.sin(ang)
    return const, table


def kernel(**inputs):
    import numpy as np
    import concourse.bacc as bacc
    from concourse.bass_utils import run_bass_kernel_spmd

    a = {k: np.asarray(v) for k, v in inputs.items()}
    const, table = shape_constants(np)
    swap = np.concatenate([np.arange(16, 32), np.arange(0, 16), np.arange(48, 64), np.arange(32, 48)])

    def col(v):
        return v.reshape(-1, P).T

    def k_tiles(w):
        return w.reshape(-1, P, w.shape[1]).transpose(1, 0, 2)

    w_in = a["w_in"][0]
    o_kv, o_r = Q_LORA, Q_LORA + KV_LORA
    o_z = o_r + ROPE
    o_x = o_z + SW
    o_dt = o_x + N_XBC * P
    tiles = [w_in[:, o_x + P * i:o_x + P * (i + 1)] for i in range(N_XBC)]
    tiles.append(np.tile(w_in[:, o_dt:o_dt + 16], (1, 8)))
    tiles += [w_in[:, o_z + P * i:o_z + P * (i + 1)] for i in range(N_Z)]
    tiles += [w_in[:, P * i:P * (i + 1)] for i in range(KQ)]
    tiles += [w_in[:, o_kv + P * i:o_kv + P * (i + 1)] for i in range(KKV)]
    rope = w_in[:, o_r:o_z]
    tiles.append(np.concatenate([rope, rope[:, swap]], axis=1))
    w_uq = a["w_uq"][0].reshape(Q_LORA, HEADS, NOPE + ROPE).transpose(1, 0, 2)
    w_uq = np.concatenate([w_uq, w_uq[:, :, NOPE + swap]], axis=2)

    w_ukv = a["w_ukv"][0].reshape(KV_LORA, HEADS, NOPE + VD)

    def f_tiles(w):
        return w.reshape(KD, P, FT, P).transpose(2, 1, 0, 3).reshape(FT, P, D)

    dram_arrays = {
        "x_sample": a["x_sample"][0], "x_prompt": a["x_prompt"][0],
        "cond": np.stack([a["c"][0].reshape(KD, P), a["c_ctx"].reshape(KD, P)]).transpose(2, 1, 0).reshape(P, 2 * KD),
        "const": const, "rope_table": table,
        "cols": np.concatenate([
            col(a["g_pre_mix"][0]), col(a["g_pre_ffn"][0]), col(a["b_mod"][0]), col(a["g_q"][0]), col(a["g_kv"][0]),
            col(a["conv_w"][0][0]), col(a["conv_w"][0][1]), col(a["conv_w"][0][2]), col(a["conv_b"][0]),
            col(a["g_ssm_out"][0])], axis=1),
        "b_mod": a["b_mod"], "g_post_mix": a["g_post_mix"], "g_post_ffn": a["g_post_ffn"], "d_skip": a["d_skip"][0].reshape(4, 2).T,
        "dt_bias": a["dt_bias"].reshape(1, 16), "a_log": a["a_log"].reshape(1, 16),
        "w_mod": a["w_mod"][0], "w_in": np.stack([k_tiles(w) for w in tiles]),
        "w_uq": np.stack([k_tiles(w) for w in w_uq]), "w_uk": np.stack([k_tiles(w_ukv[:, h, :NOPE]) for h in range(HEADS)]),
        "w_uv": np.stack([k_tiles(w_ukv[:, h:h + 2, NOPE:].reshape(KV_LORA, 2 * VD)) for h in range(0, HEADS, 2)]), "w_out": a["w_out"][0],
        "w_gate": f_tiles(a["w_gate"][0]), "w_up": f_tiles(a["w_up"][0]), "w_down": a["w_down"][0].reshape(FT, P, D),
        "cache_ckv": a["cache_ckv"], "cache_krope": a["cache_krope"], "state_ssm": a["state_ssm"],
    }
    nc = bacc.Bacc("TRN2", target_bir_lowering=False, num_devices=1)
    arrays, dram = {}, {}
    for name, v in dram_arrays.items():
        arrays[f"in_{name}"] = np.ascontiguousarray(v)
        dram[name] = nc.dram_tensor(f"in_{name}", v.shape, F32, kind="ExternalInput").ap()
    outs = {n: nc.dram_tensor(f"out_{n}", shape, F32, kind="ExternalOutput").ap() for n, shape in _OUTS}
    hybrid_layer_kernel(nc, dram, outs)
    r = run_bass_kernel_spmd(nc, [arrays], core_ids=[0])
    return tuple(r.results[0][f"out_{n}"] for n, _ in _OUTS)
```

```python
from contextlib import ExitStack

import concourse.bass as bass
from concourse import mybir

P = 128
F32 = mybir.dt.float32
F32R = mybir.dt.float32r
BF16 = mybir.dt.bfloat16
ALU = mybir.AluOpType
ACT = mybir.ActivationFunctionType
AX_X = mybir.AxisListType.X

D = 1024
KD = D // P
N_LAT, N_PROMPT, N_CACHE = 1024, 256, 256
T = N_LAT + N_PROMPT
NT = T // P
NT_LAT = N_LAT // P
BLOCKS = [(0, 512), (512, 512), (1024, 256)]
EPS = 1e-6
HEADS, NOPE, ROPE, VD = 4, 128, 64, 128
Q_LORA, KV_LORA = 384, 256
KQ, KKV = Q_LORA // P, KV_LORA // P
SCALE = float(NOPE + ROPE) ** -0.5
NKEY = T + N_CACHE
SH, SP_, DS = 8, 64, 128
SW = SH * SP_
D_FF = 2816
FT = D_FF // P
N_XBC, N_Z = 8, 4
SEQUENCE = ([("rope", 0), ("kv", 0), ("fold", 0), ("kv", 1), ("cache", 0), ("q", 0), ("sumkv", 0), ("q", 1), ("q", 2),
             ("out", 0), ("xbc", 6), ("sumq", 0), ("xbc", 7)] + [("xbc", i) for i in range(6)] +
            [("z", i) for i in range(N_Z)] + [("dt", 0)])
TILES = [e for e in SEQUENCE if e[0] in ("rope", "kv", "q", "xbc", "dt", "z")]
MOD_W = 256
MOD_EARLY = 2 * D // MOD_W
MOD_ALL = 6 * D // MOD_W

C_GPRE, C_GFFN, C_BMOD, C_GQ, C_GKV, C_CW, C_CB, C_GS, C_DB, C_AL, C_DS = 0, 8, 16, 64, 67, 69, 93, 101, 105, 121, 137
N_COLS = 141
K_ID, K_MASK, K_SEL, K_FOLD, K_TRI, K_SA, K_SB, K_MT, K_MD, K_SUM = 0, 128, 384, 400, 528, 656, 672, 672, 688, 704
N_CONST = 706


class Chain:

    def __init__(self, eng, sem):
        self.eng, self.sem, self.n = eng, sem, 0

    def mark(self, ins):
        ins.then_inc(self.sem, 1)
        self.n += 1

    def wait(self, back=0):
        self.eng.wait_ge(self.sem, self.n - back)

    def link(self, ins):
        self.mark(ins)
        self.wait()


class Layer:

    def __init__(self, nc, dram, outs):
        self.nc, self.dram, self.outs, self.sems, self.old = nc, dram, outs, [], []

    def sb(self, stack, name, shape, dt=F32, side="left"):
        return stack.enter_context(self.nc.sbuf_tensor(name, shape, dt, side=side))

    def ps(self, stack, name, shape):
        return stack.enter_context(self.nc.psum_tensor(name, shape, F32))

    def sem(self, name):
        self.sems.append(self.nc.alloc_semaphore(name=name))
        return self.sems[-1]

    def own_sem(self, name):
        return self.nc.alloc_semaphore(name=name)

    def next_phase(self):
        for s in self.old:
            self.nc.release_semaphore(s)
        self.old, self.sems = self.sems, []

    def clear_old(self):
        for s in self.old:
            self.nc.sync.sem_clear(s)


def flat(ap):
    return ap.rearrange("p a b -> p (a b)")


def across(ap, n):
    p, a = ap.shape
    return ap.unsqueeze(2).to_broadcast([p, a, n])


class Turn:

    def __init__(self, L, tag, xn, psX, full, hT_hi, hT_lo, scale_col, shift_col):
        self.L, self.xn, self.psX, self.full = L, xn, psX, full
        self.hi, self.lo, self.a, self.s = hT_hi, hT_lo, scale_col, shift_col
        self.slots, self.banks = full.shape[1], psX.shape[1]
        self.transposed, self.modulated, self.rounded, self.h_ready = (
            L.sem(f"{tag}_{n}") for n in ("transposed", "modulated", "rounded", "h_ready"))
        self.steps = [(b, k) for b in range(len(BLOCKS)) for k in range(KD)]

    def pe(self, pe, first, last):
        for n in range(first, last):
            b, k = self.steps[n]
            t0, w = BLOCKS[b][0] // P, BLOCKS[b][1] // P
            if n >= self.banks:
                pe.wait_ge(self.modulated, n + 1 - self.banks)
            for i in range(w):
                mm = pe.transpose(self.psX[:, n % self.banks, i * P:(i + 1) * P], self.xn[:, t0 + i, k * P:(k + 1) * P],
                                  self.L.ident)
            mm.then_inc(self.transposed, 1)

    def act(self, act, first, last):
        for n in range(first, last):
            b, k = self.steps[n]
            w, g = BLOCKS[b][1], int(BLOCKS[b][0] >= N_LAT)
            act.wait_ge(self.transposed, n + 1)
            if n >= self.slots:
                act.wait_ge(self.h_ready, n + 1 - self.slots)
            act.activation(self.full[:, n % self.slots, :w], self.psX[:, n % self.banks, :w], ACT.Identity,
                           bias=self.s[:, k, g:g + 1], scale=self.a[:, k, g:g + 1]).then_inc(self.modulated, 1)

    def dve(self, dve, first, last):
        for n in range(first, last):
            b, k = self.steps[n]
            c0, w = BLOCKS[b]
            dve.wait_ge(self.modulated, n + 1)
            dve.tensor_copy(self.hi[:, k, c0:c0 + w], self.full[:, n % self.slots, :w]).then_inc(self.rounded, 1)
            dve.wait_ge(self.rounded, n + 1)
            dve.tensor_tensor(self.lo[:, k, c0:c0 + w], self.full[:, n % self.slots, :w],
                              self.hi[:, k, c0:c0 + w].bitcast(F32), ALU.subtract).then_inc(self.h_ready, 1)


class NormStage:

    def __init__(self, L, st, tag, xn):
        self.xn = xn
        self.xin = L.sb(st, f"{tag}_xin", [P, 4, D])
        self.ssq = L.sb(st, f"{tag}_ssq", [P, NT])
        self.ms = L.sb(st, f"{tag}_ms", [P, NT])
        self.rstd = L.sb(st, f"{tag}_rstd", [P, NT])
        self.neghalf = L.sb(st, f"{tag}_nh", [P, 1])
        self.x_loaded = [L.sem(f"{tag}_x_loaded{i}") for i in range(4)]
        self.squared, self.meansq, self.rstd_ready, self.xn_ready, self.const = (
            L.sem(f"{tag}_{n}") for n in ("squared", "meansq", "rstd_ready", "xn_ready", "const"))

    def load(self, eng, tiles, t):
        if t >= 4:
            eng.wait_ge(self.xn_ready, t - 3)
        eng.dma_start(self.xin[:, t % 4, :], tiles(t)).then_inc(self.x_loaded[t % 4], 16)

    def act_square(self, act, t):
        act.wait_ge(self.x_loaded[t % 4], 16 * (t // 4 + 1))
        act.activation(self.xn[:, t, :], self.xin[:, t % 4, :], ACT.Square,
                       accum_out=self.ssq[:, t:t + 1]).then_inc(self.squared, 1)

    def pool_begin(self, pool):
        pool.memset(self.neghalf[:], -0.5).then_inc(self.const, 1)
        pool.wait_ge(self.const, 1)

    def pool_rstd(self, pool, t):
        pool.wait_ge(self.meansq, t + 1)
        pool.tensor_tensor(self.rstd[:, t:t + 1], self.ms[:, t:t + 1], self.neghalf[:],
                           ALU.pow).then_inc(self.rstd_ready, 1)

    def dve_step(self, dve, t):
        if t < NT:
            dve.wait_ge(self.squared, t + 1)
            dve.tensor_scalar(self.ms[:, t:t + 1], self.ssq[:, t:t + 1], 1.0 / D, EPS, ALU.mult,
                              ALU.add).then_inc(self.meansq, 1)
        if t >= 1:
            u = t - 1
            dve.wait_ge(self.rstd_ready, u + 1)
            dve.tensor_scalar(self.xn[:, u, :], self.xin[:, u % 4, :], self.rstd[:, u:u + 1], None,
                              ALU.mult).then_inc(self.xn_ready, 1)


class ModStage:

    def __init__(self, L, st, tag, first, last, banks, depth, slots):
        self.L, self.first, self.last, self.banks, self.depth, self.slots = L, first, last, banks, depth, slots
        self.ring = L.sb(st, f"{tag}_wring", [P, depth, KD, MOD_W])
        self.hi, self.lo = (L.sb(st, f"{tag}_w_{n}", [P, slots, KD, MOD_W], F32R) for n in ("hi", "lo"))
        self.row = L.sb(st, f"{tag}_row", [P, MOD_W])
        self.gate = L.sb(st, f"{tag}_gate", [2, 2, MOD_W])
        self.psM = L.ps(st, f"{tag}_psM", [P, banks, 512])
        self.psC = L.ps(st, f"{tag}_psC", [P, MOD_W])
        self.loaded = [L.sem(f"{tag}_w_loaded{i}") for i in range(depth)]
        self.row_out = [L.own_sem(f"{tag}_row_out{i}") for i in range(2)]
        self.hi_ready, self.lo_ready, self.product, self.row_ready, self.turned, self.col_ready = (
            L.sem(f"{tag}_{n}") for n in ("w_hi", "w_lo", "product", "row_ready", "turned", "col_ready"))

    @staticmethod
    def is_gate(j):
        return (j * MOD_W // D) % 3 == 2

    def n_gates(self, j):
        return sum(self.is_gate(i) for i in range(self.first, j))

    def load(self, eng, j):
        i = j - self.first
        r = i % self.depth
        if i >= self.depth:
            eng.wait_ge(self.lo_ready, i + 1 - self.depth)
        eng.dma_start(self.ring[:, r, :, :],
                      self.L.dram["w_mod"].rearrange("(k p) n -> p k n", p=P)[:, :, j * MOD_W:(j + 1) * MOD_W]
                      ).then_inc(self.loaded[r], 16)

    def act_hi(self, act, j):
        i = j - self.first
        r = i % self.depth
        act.wait_ge(self.loaded[r], 16 * (i // self.depth + 1))
        if i >= self.slots:
            act.wait_ge(self.product, i + 1 - self.slots)
        act.activation(self.hi[:, i % self.slots, :, :], self.ring[:, r, :, :], ACT.Copy).then_inc(self.hi_ready, 1)

    def dve_lo(self, dve, j):
        i = j - self.first
        dve.wait_ge(self.hi_ready, i + 1)
        dve.tensor_tensor(self.lo[:, i % self.slots, :, :], self.ring[:, i % self.depth, :, :],
                          self.hi[:, i % self.slots, :, :].bitcast(F32), ALU.subtract).then_inc(self.lo_ready, 1)

    def pe_product(self, pe, j):
        i = j - self.first
        pe.wait_ge(self.lo_ready, i + 1)
        if i >= self.banks:
            pe.wait_ge(self.row_ready, i + 1 - self.banks)
        for k in range(KD):
            for w in (self.hi, self.lo):
                mm = pe.matmul(self.psM[:, i % self.banks, :MOD_W], self.L.cond_st[:, k, :],
                               w[:, i % self.slots, k, :], start=(k == 0 and w is self.hi),
                               stop=(k == KD - 1 and w is self.lo))
        mm.then_inc(self.product, 1)

    def dve_row(self, dve, j):
        i = j - self.first
        dve.wait_ge(self.product, i + 1)
        if i >= 1:
            dve.wait_ge(self.turned, i)
        dve.tensor_copy(self.row[:], self.psM[:, i % self.banks, :MOD_W]).then_inc(self.row_ready, 1)

    def pe_turn(self, pe, j):
        i = j - self.first
        pe.wait_ge(self.row_ready, i + 1)
        if i >= 1:
            pe.wait_ge(self.col_ready, i)
        total = self.L.const[:, K_SUM:K_SUM + 2]
        if self.is_gate(j):
            mm = pe.matmul(self.psC[0:2, :], total, self.row[:], start=True, stop=True)
        else:
            for s in range(2):
                mm = pe.matmul(self.psC[:, 2 * s:2 * s + 2], self.row[:, s * P:(s + 1) * P], total, start=True,
                               stop=True)
        mm.then_inc(self.turned, 1)

    def dve_col(self, dve, j):
        i = j - self.first
        dve.wait_ge(self.turned, i + 1)
        if self.is_gate(j):
            n = self.n_gates(j)
            if n >= 2:
                dve.wait_ge(self.row_out[n % 2], 16 * (n // 2))
            dve.tensor_copy(self.gate[:, n % 2, :], self.psC[0:2, :]).then_inc(self.col_ready, 1)
        else:
            dve.tensor_tensor(self.L.mod[:, 2 * j:2 * j + 2, :], self.psC[:, 0:4].rearrange("p (s g) -> p s g", s=2),
                              across(self.L.cols[:, C_BMOD + 2 * j:C_BMOD + 2 * j + 2], 2),
                              ALU.add).then_inc(self.col_ready, 1)

    def store_gate(self, eng, j):
        i, n = j - self.first, self.n_gates(j)
        eng.wait_ge(self.col_ready, i + 1)
        eng.dma_start(self.L.gate_rows[:, j * MOD_W:(j + 1) * MOD_W], self.gate[:, n % 2, :]
                      ).then_inc(self.row_out[n % 2], 16)


def phase_norm1(L):
    nc = L.nc
    with ExitStack() as st:
        norm = NormStage(L, st, "n1", L.xn)
        mod = ModStage(L, st, "m1", 0, MOD_EARLY, 2, 4, 2)
        cond = L.sb(st, "cond", [P, KD * 2])
        scond = L.sb(st, "scond", [P, KD * 2])
        c_hi, c_lo = (L.sb(st, f"cond_{n}", [P, KD * 2], F32R) for n in ("hi", "lo"))
        c_ld, k_ld, silu, dch = (L.sem(n) for n in ("cond_loaded", "const_loaded", "cond_silu", "n1_dve"))
        block = st.enter_context(nc.Block())

        def x_tile(t):
            if t < NT_LAT:
                return L.dram["x_sample"][t * P:(t + 1) * P, :]
            return L.dram["x_prompt"][(t - NT_LAT) * P:(t - NT_LAT + 1) * P, :]

        @block.sync
        def _(sp):
            sp.dma_start(cond[:], L.dram["cond"]).then_inc(c_ld, 16)
            for j in range(NT):
                if j < MOD_EARLY:
                    mod.load(sp, j)
                norm.load(sp, x_tile, j)
                if j == 0:
                    sp.dma_start(L.cols[:], L.dram["cols"]).then_inc(k_ld, 16)
                    sp.dma_start(L.const[:], L.dram["const"]).then_inc(k_ld, 16)

        @block.gpsimd
        def _(pool):
            norm.pool_begin(pool)
            for t in range(NT):
                norm.pool_rstd(pool, t)

        @block.scalar
        def _(act):
            act.wait_ge(c_ld, 16)
            act.activation(scond[:], cond[:], ACT.Silu).then_inc(silu, 1)
            for t in range(NT):
                if t < MOD_EARLY:
                    mod.act_hi(act, t)
                norm.act_square(act, t)

        @block.vector
        def _(dve):
            c = Chain(dve, dch)
            dve.wait_ge(silu, 1)
            c.link(dve.tensor_copy(c_hi[:], scond[:]))
            c.link(dve.tensor_tensor(c_lo[:], scond[:], c_hi[:].bitcast(F32), ALU.subtract))
            parts = L.cond_st[:].rearrange("p k (g h r) -> p (k g) h r", g=2, h=2)
            c.mark(dve.tensor_copy(parts[:, :, 0, :], across(c_hi[:].bitcast(F32), P // 4)))
            c.mark(dve.tensor_copy(parts[:, :, 1, :], across(c_lo[:].bitcast(F32), P // 4)))
            for i in range(NT + 1):
                if i < MOD_EARLY:
                    mod.dve_lo(dve, i)
                norm.dve_step(dve, i)
                if 1 <= i <= MOD_EARLY:
                    mod.dve_row(dve, i - 1)
                if 2 <= i < MOD_EARLY + 2:
                    if i == 2:
                        dve.wait_ge(k_ld, 32)
                    mod.dve_col(dve, i - 2)
            dve.wait_ge(mod.col_ready, MOD_EARLY)
            c.link(dve.scalar_tensor_tensor(L.scale1[:], L.mod[:, KD:2 * KD, :], 1.0,
                                            across(L.cols[:, C_GPRE:C_GPRE + KD], 2), ALU.add, ALU.mult))

        @block.tensor
        def _(pe):
            pe.wait_ge(dch, 4)
            for j in range(MOD_EARLY + 1):
                if j < MOD_EARLY:
                    mod.pe_product(pe, j)
                if j == 1:
                    pe.wait_ge(k_ld, 32)
                if j >= 1:
                    mod.pe_turn(pe, j - 1)


def split3(pe, out, w_hi, w_lo, x_hi, x_lo, first, last):
    pe.matmul(out, w_hi, x_hi, start=first, stop=False)
    pe.matmul(out, w_hi, x_lo, start=False, stop=False)
    return pe.matmul(out, w_lo, x_hi, start=False, stop=last)


def phase_in_proj(L):
    nc = L.nc
    L.next_phase()
    with ExitStack() as st:
        raw = L.sb(st, "win_raw", [P, 2, KD, P])
        w_hi = L.sb(st, "win_hi", [P, 2, KD, P], F32R)
        w_lo = L.sb(st, "win_lo", [P, 2, KD, P], F32R)
        conv = L.sb(st, "conv_acc", [P, T])
        cc = L.sb(st, "cache_in", [P, 2, KV_LORA])
        cr = L.sb(st, "cachek_in", [P, 2, 2, ROPE])
        cst = L.sb(st, "cache_turned", [P, 3, N_CACHE])
        rope_p = L.sb(st, "rope_prompt", [P, N_PROMPT])
        co, ko = cc, cr[:, :, 0, :]
        eps = L.sb(st, "eps", [P, 1])
        mod = ModStage(L, st, "m2", MOD_EARLY, MOD_ALL, 1, 2, 1)
        stage = [conv[:], flat(mod.ring[:, 1, :, :])[:, 0:T]]
        psP = L.ps(st, "psP", [P, 2, 3, 512])
        turn = Turn(L, "n1", L.xn, psP[:, 1, :, :], conv[:, 0:1024].rearrange("p (a n) -> p a n", a=2), L.hT_hi,
                    L.hT_lo, L.scale1, L.mod[:, 0:KD, :])
        loaded = [L.sem(f"win_loaded{i}") for i in range(2)]
        stored = [L.own_sem(f"stage_stored{i}") for i in range(2)]
        (hi_ready, lo_ready, used, act_read, dve_read, conv_ready, conv_read, dch, ach, mod_done, c_loaded, t_loaded,
         ip_consts, squares, summed, kvn_ready, qn_ready, out_copied) = (L.sem("ip_" + n) for n in (
             "win_hi", "win_lo", "used", "act_read", "dve_read", "conv_ready", "conv_read", "dve", "act", "mod_scale",
             "c_loaded", "t_loaded", "consts", "squares", "summed", "kvn_ready", "qn_ready", "out_copied"))
        kv_stored, kr_stored, q_stored, cache_stored, out_stored = (L.own_sem("ip_" + n) for n in (
            "kv_stored", "kr_stored", "q_stored", "cache_stored", "out_stored"))
        block = st.enter_context(nc.Block())
        last_mod = MOD_ALL - MOD_EARLY
        table = L.dtT
        place = {e: m for m, e in enumerate(SEQUENCE)}
        tiles = [m for m, e in enumerate(SEQUENCE) if e in TILES]
        number = {m: ct for ct, m in enumerate(tiles)}
        by_dve = lambda e: e[0] in ("rope", "out", "xbc")
        reads = lambda m, dve: sum(by_dve(e) == dve for e in SEQUENCE[:m + 1])
        xbc_order = [e[1] for e in SEQUENCE if e[0] == "xbc"]
        splits = {}
        for ct in range(1, len(tiles)):
            m = tiles[ct - 1]
            if SEQUENCE[m - 1][0] in ("sumkv", "sumq"):
                m -= 1
            splits[m] = ct

        def until(eng, m):
            eng.wait_ge(used, m + 1)

        def bank(m):
            return psP[:, m % 2, :, :]

        @block.sync
        def _(sp):
            def load(ct):
                if ct >= 2:
                    sp.wait_ge(lo_ready, ct - 1)
                sp.dma_start(raw[:, ct % 2, :, :], L.dram["w_in"][ct]).then_inc(loaded[ct % 2], 16)

            load(0)
            mod.load(sp, MOD_EARLY)
            load(1)
            sp.dma_start(table[:], L.dram["rope_table"]).then_inc(t_loaded, 16)
            sp.dma_start(cc[:], L.dram["cache_ckv"][0, 0].rearrange("(a p) n -> p a n", p=P)).then_inc(c_loaded, 16)
            for r in range(2):
                sp.dma_start(cr[:, :, r, :], L.dram["cache_krope"][0, 0].rearrange("(a p) n -> p a n", p=P)
                             ).then_inc(c_loaded, 16)
            for ct in range(len(tiles)):
                if ct + 1 < last_mod:
                    mod.load(sp, MOD_EARLY + ct + 1)
                if ct + 2 < len(tiles):
                    load(ct + 2)
            L.clear_old()

        @block.gpsimd
        def _(pool):
            pool.memset(L.ones[:], 1.0).then_inc(ip_consts, 1)
            pool.memset(eps[:], EPS).then_inc(ip_consts, 1)
            for m, (kind, i) in enumerate(SEQUENCE):
                j = MOD_EARLY + number.get(m, 0) - 1
                if m in number and MOD_EARLY <= j < MOD_ALL and mod.is_gate(j):
                    mod.store_gate(pool, j)
                if kind == "cache":
                    pool.wait_ge(act_read, reads(m, False))
                    pool.dma_start(L.kv_s.rearrange("a p t -> p a t")[:, :, T:NKEY], cst[:, 0:2, :]
                                   ).then_inc(cache_stored, 16)
                    pool.dma_start(L.kr_s[:, T:NKEY], cst[:, 2, :]).then_inc(cache_stored, 16)
                if kind == "sumkv":
                    pool.wait_ge(kvn_ready, 2)
                    pool.dma_start(L.kv_s.rearrange("a p t -> p a t")[:, :, 0:T], L.xbcT[:, 6:8, :]
                                   ).then_inc(kv_stored, 16)
                if kind == "out":
                    pool.wait_ge(out_copied, 2)
                    pool.dma_start(L.outs["ckv"][0, 0].rearrange("(a p) n -> p a n", p=P), co[:]
                                   ).then_inc(out_stored, 16)
                    pool.dma_start(L.outs["krope"][0, 0].rearrange("(a p) n -> p a n", p=P), ko[:]
                                   ).then_inc(out_stored, 16)
                if kind == "sumq":
                    pool.wait_ge(qn_ready, KQ)
                    pool.dma_start(L.q_s.rearrange("a p t -> p a t"), L.xbcT[:, 3:6, :]).then_inc(q_stored, 16)
                if kind == "fold":
                    pool.wait_ge(act_read, reads(m, False))
                    pool.dma_start(L.kr_s[:, 0:T], L.xbcT[:, 2, :]).then_inc(kr_stored, 16)
                if kind == "z":
                    pool.wait_ge(act_read, reads(m, False))
                    pool.dma_start(L.staged[i], stage[i % 2]).then_inc(stored[i % 2], 16)
            for i in range(2):
                pool.wait_ge(stored[i], 16 * (N_Z // 2))
            for sem, n in ((kv_stored, 1), (q_stored, 1), (kr_stored, 1), (cache_stored, 2), (out_stored, 2)):
                pool.wait_ge(sem, 16 * n)
            for i in range(2):
                pool.wait_ge(mod.row_out[i], 16 * (mod.n_gates(MOD_ALL) // 2))

        @block.scalar
        def _(act):
            chain = Chain(act, ach)

            def split(ct):
                act.wait_ge(loaded[ct % 2], 16 * (ct // 2 + 1))
                if ct >= 2:
                    until(act, tiles[ct - 2])
                act.activation(w_hi[:, ct % 2, :, :], raw[:, ct % 2, :, :], ACT.Copy).then_inc(hi_ready, 1)

            def square(src, dst):
                act.activation(L.xbcT[:, dst, :], L.xbcT[:, src, :], ACT.Square).then_inc(squares, 1)

            turn.act(act, 0, 4)
            split(0)
            turn.act(act, 4, 24)
            act.wait_ge(ip_consts, 2)
            for m, (kind, i) in enumerate(SEQUENCE):
                if m in splits:
                    split(splits[m])
                if m in number and number[m] < last_mod:
                    mod.act_hi(act, MOD_EARLY + number[m])
                src = flat(bank(m))[:, 0:T]
                if kind == "xbc":
                    n = xbc_order.index(i)
                    act.wait_ge(conv_ready, n + 1)
                    if i >= 6:
                        act.wait_ge(kv_stored, 16)
                        until(act, place["out", 0])
                    elif i == 0:
                        until(act, place["sumq", 0])
                    elif i == 2:
                        act.wait_ge(qn_ready, KQ)
                    elif i == 3:
                        act.wait_ge(q_stored, 16)
                    act.activation(L.xbcT[:, i, :], conv[:], ACT.Silu,
                                   bias=L.cols[:, C_CB + i:C_CB + i + 1]).then_inc(conv_read, 1)
                    continue
                if by_dve((kind, i)):
                    continue
                until(act, m)
                if kind == "kv":
                    chain.link(act.activation(L.xbcT[:, 6 + i, :], src, ACT.Copy))
                    act.sem_inc(act_read, 1)
                    square(6 + i, i)
                elif kind == "q":
                    chain.link(act.activation(L.xbcT[:, 3 + i, :], src, ACT.Copy))
                    act.sem_inc(act_read, 1)
                    if i >= 1:
                        act.wait_ge(summed, i)
                        square(3 + i, 1)
                elif kind in ("sumkv", "sumq"):
                    if kind == "sumkv":
                        act.wait_ge(kr_stored, 16)
                    else:
                        act.wait_ge(kvn_ready, 2)
                    act.activation(L.xbcT[:, 2, :], src, ACT.Sqrt, bias=eps[:],
                                   scale=1.0 / (KV_LORA if kind == "sumkv" else Q_LORA)).then_inc(act_read, 1)
                    if kind == "sumkv":
                        square(3, 0)
                elif kind == "cache":
                    chain.link(act.activation(flat(cst[:, 0:2, :]), bank(m)[:, 0, :], ACT.Copy))
                    chain.link(act.activation(cst[:, 2, :], bank(m)[:, 1, 0:N_CACHE], ACT.Copy))
                    act.sem_inc(act_read, 1)
                elif kind in ("dt", "fold"):
                    act.activation(L.dtT[:] if kind == "dt" else L.xbcT[:, 2, :], src, ACT.Copy).then_inc(act_read, 1)
                else:
                    if i == 0:
                        act.wait_ge(conv_read, N_XBC)
                    elif i == 1:
                        act.wait_ge(mod.lo_ready, last_mod)
                    else:
                        act.wait_ge(stored[i % 2], 16 * (i // 2))
                    act.activation(stage[i % 2], src, ACT.Silu).then_inc(act_read, 1)

        @block.vector
        def _(dve):
            chain = Chain(dve, dch)

            def split(ct):
                dve.wait_ge(hi_ready, ct + 1)
                dve.tensor_tensor(w_lo[:, ct % 2, :, :], raw[:, ct % 2, :, :],
                                  w_hi[:, ct % 2, :, :].bitcast(F32), ALU.subtract).then_inc(lo_ready, 1)

            def add_squares(n):
                dve.wait_ge(squares, n)
                dve.tensor_tensor(L.xbcT[:, 0, :], L.xbcT[:, 0, :], L.xbcT[:, 1, :], ALU.add).then_inc(summed, 1)

            def invert(m):
                dve.wait_ge(act_read, reads(m, False))
                chain.link(dve.reciprocal(L.xbcT[:, 2, :], L.xbcT[:, 2, :]))

            def normalise(n, slot, gains, done):
                for k in range(n):
                    dve.scalar_tensor_tensor(L.xbcT[:, slot + k, :], L.xbcT[:, slot + k, :],
                                             L.cols[:, gains + k:gains + k + 1], L.xbcT[:, 2, :], ALU.mult, ALU.mult
                                             ).then_inc(done, 1)

            turn.dve(dve, 0, 8)
            split(0)
            turn.dve(dve, 8, 24)
            dve.wait_ge(turn.h_ready, 24)
            for m, (kind, i) in enumerate(SEQUENCE):
                if m in splits:
                    split(splits[m])
                if m in number and number[m] < last_mod:
                    mod.dve_lo(dve, MOD_EARLY + number[m])
                src = flat(bank(m))
                if kind == "rope":
                    dve.wait_ge(t_loaded, 16)
                    until(dve, m)
                    chain.link(dve.tensor_copy(rope_p[:], src[:, N_LAT:T]))
                    chain.link(dve.tensor_tensor(conv[:], src[:, 0:T], table[:], ALU.mult))
                    dve.sem_inc(dve_read, 1)
                elif kind == "kv" and i == 1:
                    add_squares(2)
                elif kind == "sumkv":
                    invert(m)
                    normalise(KKV, 6, C_GKV, kvn_ready)
                elif kind == "q" and i >= 1:
                    add_squares(3 + i)
                elif kind == "sumq":
                    invert(m)
                elif kind == "out":
                    until(dve, m)
                    dve.tensor_copy(co[:], bank(m)[:, 0, :].rearrange("p (a n) -> p a n", a=2)).then_inc(out_copied, 1)
                    dve.tensor_copy(ko[:], bank(m)[:, 1, 0:256].rearrange("p (a n) -> p a n", a=2)[:, :, 0:ROPE]
                                    ).then_inc(out_copied, 1)
                    dve.wait_ge(out_copied, 2)
                    dve.sem_inc(dve_read, 1)
                elif kind == "xbc":
                    tap = [L.cols[:, C_CW + 8 * n + i:C_CW + 8 * n + i + 1] for n in range(3)]
                    until(dve, m)
                    n = xbc_order.index(i)
                    if n >= 1:
                        dve.wait_ge(conv_read, n)
                    chain.link(dve.tensor_scalar(conv[:], src[:, 0:T], tap[1], None, ALU.mult))
                    for a, b in ((0, N_LAT), (N_LAT, T)):
                        chain.mark(dve.scalar_tensor_tensor(conv[:, a + 1:b], src[:, a:b - 1], tap[0],
                                                            conv[:, a + 1:b], ALU.mult, ALU.add))
                    chain.wait()
                    for a, b in ((0, N_LAT), (N_LAT, T)):
                        chain.mark(dve.scalar_tensor_tensor(conv[:, a:b - 1], src[:, a + 1:b], tap[2],
                                                            conv[:, a:b - 1], ALU.mult, ALU.add))
                    chain.wait()
                    dve.sem_inc(conv_ready, 1)
                    dve.sem_inc(dve_read, 1)
                    if SEQUENCE[m - 1][0] == "sumq":
                        normalise(KQ, 3, C_GQ, qn_ready)
                ct = number.get(m)
                if ct is None:
                    continue
                if ct < last_mod:
                    mod.dve_row(dve, MOD_EARLY + ct)
                if 1 <= ct <= last_mod:
                    mod.dve_col(dve, MOD_EARLY + ct - 1)
            dve.wait_ge(mod.col_ready, last_mod)
            dve.scalar_tensor_tensor(L.scale2[:], L.mod[:, 4 * KD:5 * KD, :], 1.0,
                                     across(L.cols[:, C_GFFN:C_GFFN + KD], 2), ALU.add,
                                     ALU.mult).then_inc(mod_done, 1)
            dve.wait_ge(mod_done, 1)

        @block.tensor
        def _(pe):
            turn.pe(pe, 0, 8)
            for m, (kind, i) in enumerate(SEQUENCE):
                if m == 1:
                    pe.wait_ge(turn.modulated, 24)
                if m >= 2:
                    dve = by_dve(SEQUENCE[m - 2])
                    pe.wait_ge(dve_read if dve else act_read, reads(m - 2, dve))
                out = bank(m)
                ct = number.get(m)
                if kind == "fold":
                    for b, (c0, w) in enumerate(BLOCKS):
                        mm = pe.matmul(out[:, b, :w], L.fold, conv[:, c0:c0 + w], start=True, stop=True)
                elif kind == "cache":
                    pe.wait_ge(c_loaded, 48)
                    for k in range(2):
                        for a in range(2):
                            pe.transpose(out[:, 0, (2 * k + a) * P:(2 * k + a + 1) * P], cc[:, a, k * P:(k + 1) * P],
                                         L.ident)
                    for a in range(2):
                        mm = pe.transpose(out[:, 1, a * P:(a + 1) * P], cr[:, a, :, :], L.ident)
                elif kind in ("sumkv", "sumq"):
                    pe.wait_ge(ip_consts, 2)
                    pe.wait_ge(summed, 1 if kind == "sumkv" else 3)
                    for b, (c0, w) in enumerate(BLOCKS):
                        mm = pe.matmul(out[:, b, :w], L.ones[:], L.xbcT[:, 0, c0:c0 + w], start=True, stop=True)
                elif kind == "out":
                    pe.wait_ge(kvn_ready, 2)
                    pe.wait_ge(dve_read, 1)
                    for a in range(2):
                        for k in range(2):
                            pe.transpose(out[:, 0, (2 * a + k) * P:(2 * a + k + 1) * P],
                                         L.xbcT[:, 6 + k, N_LAT + a * P:N_LAT + (a + 1) * P], L.ident)
                    for a in range(2):
                        mm = pe.transpose(out[:, 1, a * P:(a + 1) * P], rope_p[:, a * P:(a + 1) * P], L.ident)
                else:
                    s = ct % 2
                    pe.wait_ge(lo_ready, ct + 1)
                    for b, (c0, w) in enumerate(BLOCKS):
                        if m == 0:
                            pe.wait_ge(turn.h_ready, 8 * b + 8)
                        for k in range(KD):
                            if m == 0 and b < 2 and k % 4 == 0:
                                turn.pe(pe, 8 * b + 8 + k, 8 * b + 12 + k)
                            mm = split3(pe, out[:, b, :w], w_hi[:, s, k, :], w_lo[:, s, k, :],
                                        L.hT_hi[:, k, c0:c0 + w], L.hT_lo[:, k, c0:c0 + w], k == 0, k == KD - 1)
                mm.then_inc(used, 1)
                if ct is not None and 1 <= ct <= last_mod:
                    mod.pe_turn(pe, MOD_EARLY + ct - 1)
                if ct is not None and ct < last_mod:
                    mod.pe_product(pe, MOD_EARLY + ct)


def phase_ssm(L):
    nc = L.nc
    L.next_phase()
    with ExitStack() as st:
        xs = L.sb(st, "xs", [P, NT, SW])
        bt = L.sb(st, "bt", [P, NT, 2, DS])
        mix_out = L.sb(st, "ssm_mix", [P, NT, SW])
        zt = mix_out
        zc = L.sb(st, "zc", [P, 2, 4, P])
        sb_in = L.sb(st, "sb_in", [P, NT, SW])
        sf = L.sb(st, "sf", [P, 2, SW])
        xw = L.sb(st, "xw", [P, 2, SW])
        tmp, off_b, yn, decayed = (L.sb(st, n, [P, SW]) for n in ("s_tmp", "off_b", "yn", "decayed"))
        yv = L.sb(st, "yv", [P, 2, SW])
        st_in = L.sb(st, "st_in", [P, 2, 4, DS])
        fin = L.sb(st, "fin", [P, 2, SW])
        seg = L.sb(st, "seg", [P, 16, P])
        cb = L.sb(st, "cb", [P, 2, P])
        wt = L.sb(st, "wt", [P, SH, P])
        dskip = L.cols[:, C_DS:C_DS + 4]
        ddiag = L.sb(st, "ddiag", [P, 4, P])
        rate = L.sb(st, "ssm_rate", [P, 16])
        feats = [L.sb(st, f"dt_{n}", [P, NT, 16]) for n in (
            "v", "e", "w", "lw", "c", "dt", "da", "u", "up", "eoff", "wgt", "t", "cdrow")]
        v, e, w, lw, cc, dt, da, u, up, eoff, wgt, t3, cdrow = feats
        rnd = L.sb(st, "dt_rnd", [P, NT, 16], F32R)
        pack = flat(seg[:])[:, 0:2 * NT * 64].rearrange("p (i c k) -> p i c k", i=2, c=NT)
        u2 = L.sb(st, "u2", [64, T])
        up2 = L.sb(st, "up2", [66, T], F32R)
        pick = L.sb(st, "pick", [66, 2, 16, P], F32R)
        maskb = L.sb(st, "maskb", [P, 2, 4, P], BF16)
        identb = L.sb(st, "identb", [P, P], BF16)
        ss, ms, rs, nh = (L.sb(st, f"y_{n}", [P, NT] if n != "nh" else [P, 1]) for n in ("ss", "ms", "rs", "nh"))
        A = [L.ps(st, f"psA{i}", [P, 512]) for i in range(4)]
        Q = L.ps(st, "psQ", [P, 4, 512])
        z_loaded = [L.sem(f"ss_z{i}") for i in range(2)]
        u_loaded = [L.own_sem(f"ss_u{i}") for i in range(2)]
        u_stored, ones_set = L.sem("ss_u_stored"), L.sem("ss_ones")
        (xwf_ready, mix_stored, st_loaded, st_turned,
         dt_turned, dt_pe, dt_act, dt_dve, dch, packed, u_turned, u_read, x_turned, x_copied,
         xw_ready, s_mm, s_ready, cb_done, cb_read, seg_done, exp_done, off_done, off_read, w_ready, diag_done,
         y_ready, squared, rstd_ready, yn_ready, y_turned, mix_ready, sf_ready, dec_ready, fin_mm, fin_cp, fin_out,
         consts, pch) = (L.sem("ss_" + n) for n in (
             "xwf_ready", "mix_stored", "st_loaded", "st_turned",
             "dt_turned", "dt_pe", "dt_act", "dt_dve", "dch", "packed", "u_turned", "u_read",
             "x_turned", "x_copied", "xw_ready", "s_mm", "s_ready", "cb_done", "cb_read", "seg_done", "exp_done",
             "off_done", "off_read", "w_ready", "diag_done", "y_ready", "squared", "rstd", "yn_ready", "y_turned",
             "mix_ready", "sf_ready", "dec_ready", "fin_mm", "fin_cp", "fin_out", "consts", "pch"))
        block = st.enter_context(nc.Block())
        down = list(range(NT_LAT - 1, -1, -1)) + list(range(NT - 1, NT_LAT - 1, -1))
        heads = lambda ap: ap.rearrange("p (h q) -> p h q", q=SP_)
        chunk = lambda c: slice(c * P, (c + 1) * P)
        krow = lambda c: L.const[:, c:c + 16].unsqueeze(1).to_broadcast([P, NT, 16])
        row = lambda ap: ap.unsqueeze(1).to_broadcast([P, NT, 16])
        U_GROUPS = [(which, c0, min(4, NT - c0)) for which in range(2) for c0 in range(0, NT, 4)]

        @block.sync
        def _(sp):
            for d in range(2):
                sp.dma_start(st_in[:, d, :, :], L.dram["state_ssm"][0, 0, d].rearrange("(a h) p n -> (h p) a n", a=4)
                             ).then_inc(st_loaded, 16)
            for i, c in enumerate(down):
                if i >= 2:
                    sp.wait_ge(x_turned, i - 1)
                sp.dma_start(zc[:, i % 2, :, :], L.staged[0:N_Z].rearrange("a p t -> p a t")[:, :, chunk(c)]
                             ).then_inc(z_loaded[i % 2], 16)
            L.clear_old()
            sp.wait_ge(u_read, 3)
            for i in range(2):
                sp.dma_start(L.u_s[i], u2[32 * i:32 * i + 16, :]).then_inc(u_stored, 16)
            for c in range(NT):
                if c == NT - 1:
                    sp.wait_ge(fin_cp, 2)
                    for d in range(2):
                        sp.dma_start(L.outs["ssm"][0, 0, d].rearrange("(a h) p n -> (h p) a n", a=4),
                                     st_in[:, d, :, :]).then_inc(fin_out, 16)
                sp.wait_ge(mix_ready, c + 1)
                sp.dma_start(L.mixS[c], mix_out[:, c, :]).then_inc(mix_stored, 16)
            sp.wait_ge(fin_out, 32)
            sp.wait_ge(mix_stored, 16 * NT)

        @block.gpsimd
        def _(pool):
            p = Chain(pool, pch)
            p.mark(pool.memset(nh[:], -0.5))
            pool.memset(pack, 0.0).then_inc(consts, 1)
            pool.tensor_scalar(pick[0:64, 0, :, :], across(L.const[0:64, K_SEL:K_SEL + 16], P), -1.0, None, ALU.mult
                               ).then_inc(consts, 1)
            pool.tensor_scalar(pick[0:64, 1, :, :], across(L.const[0:64, K_SEL:K_SEL + 16], P), -1.0, None, ALU.mult
                               ).then_inc(consts, 1)
            for d in range(2):
                pool.tensor_copy(maskb[:, d, :, :], L.const[:, K_MASK + d * P:K_MASK + (d + 1) * P]
                                 .unsqueeze(1).to_broadcast([P, 4, P])).then_inc(consts, 1)
            pool.tensor_copy(identb[:], L.ident).then_inc(consts, 1)
            pool.tensor_tensor(ddiag[:], L.ident.unsqueeze(1).to_broadcast([P, 4, P]), across(dskip, P), ALU.mult
                               ).then_inc(consts, 1)
            p.wait()

            def decay(c):
                if c == NT_LAT - 1:
                    return
                pool.wait_ge(sf_ready, c + 1)
                if c == 0:
                    pool.wait_ge(dt_act, 5)
                pool.tensor_tensor(heads(decayed[:]), heads(sf[:, c % 2, :]), across(cdrow[:, c, 0:8], SP_), ALU.mult
                                   ).then_inc(dec_ready, 1)

            def rstd(c):
                pool.wait_ge(squared, c + 1)
                p.link(pool.tensor_scalar(ms[:, c:c + 1], ss[:, c:c + 1], 1.0 / SW, EPS, ALU.mult, ALU.add))
                pool.tensor_tensor(rs[:, c:c + 1], ms[:, c:c + 1], nh[:], ALU.pow).then_inc(rstd_ready, 1)

            def load_u(c):
                if c >= 2:
                    pool.wait_ge(seg_done, c - 1)
                pool.dma_start(pick[64:66, c % 2, :, :], L.u_s[:, :, chunk(c)]).then_inc(u_loaded[c % 2], 16)

            pool.wait_ge(u_stored, 32)
            load_u(0)
            load_u(1)
            def weigh(c):
                pool.wait_ge(s_mm, NT + c)
                pool.tensor_tensor(heads(xw[:, 0, :]), heads(xs[:, c, :]), across(wgt[:, c, 0:8], SP_), ALU.mult
                                   ).then_inc(xwf_ready, 1)

            pool.wait_ge(s_ready, NT)
            for c in range(NT):
                weigh(c)
                decay(c)
                if c >= 1:
                    rstd(c - 1)
                if c + 2 < NT:
                    load_u(c + 2)
            rstd(NT - 1)

        @block.scalar
        def _(act):
            def copies(i):
                c = down[i]
                act.wait_ge(x_turned, i + 1)
                act.activation(xs[:, c, :], A[i % 2][:], ACT.Copy).then_inc(x_copied, 1)
                act.activation(flat(bt[:, c, :, :]), A[2 + i % 2][:, 0:2 * DS], ACT.Copy).then_inc(x_copied, 1)
                act.activation(zt[:, c, :], Q[:, 2 + i % 2, :], ACT.Copy).then_inc(x_copied, 1)

            act.activation(up2[64:66, :], L.ones[64:66, 0:1].to_broadcast([2, T]), ACT.Copy).then_inc(ones_set, 1)
            act.activation(rate[:], L.cols[:, C_AL:C_AL + 16], ACT.Exp).then_inc(dt_act, 1)
            act.wait_ge(dt_dve, 1)
            act.activation(e[:], e[:], ACT.Exp).then_inc(dt_act, 1)
            act.wait_ge(dt_dve, 2)
            act.activation(lw[:], w[:], ACT.Ln).then_inc(dt_act, 1)
            act.wait_ge(dt_dve, 3)
            act.activation(w[:], w[:], ACT.Ln).then_inc(dt_act, 1)
            copies(0)
            copies(1)
            act.wait_ge(dt_pe, 1)
            act.activation(flat(cdrow[:]), Q[:, 0, 0:NT * 16], ACT.Exp).then_inc(dt_act, 1)
            act.wait_ge(dt_dve, 5)
            act.activation(eoff[:], eoff[:], ACT.Exp).then_inc(dt_act, 1)
            act.activation(wgt[:], wgt[:], ACT.Exp).then_inc(dt_act, 1)
            for i in range(2, NT):
                copies(i)

            def square(c):
                act.wait_ge(y_ready, c + 1)
                if c >= 1:
                    act.wait_ge(y_turned, c)
                act.activation(yn[:], yv[:, c % 2, :], ACT.Square, accum_out=ss[:, c:c + 1]).then_inc(squared, 1)

            def scale(c):
                act.wait_ge(rstd_ready, c + 1)
                act.wait_ge(squared, c + 1)
                act.activation(yn[:], yv[:, c % 2, :], ACT.Copy, scale=rs[:, c:c + 1]).then_inc(yn_ready, 1)

            for c in range(NT):
                if c >= 1:
                    act.wait_ge(w_ready, c)
                act.wait_ge(seg_done, c + 1)
                act.activation(flat(seg[:]), flat(Q[:]), ACT.Exp).then_inc(exp_done, 1)
                if c >= 1:
                    square(c - 1)
                act.wait_ge(cb_done, c + 1)
                act.activation(flat(cb[:]), A[0][:, 0:2 * P], ACT.Copy).then_inc(cb_read, 1)
                if c >= 1:
                    scale(c - 1)
            square(NT - 1)
            scale(NT - 1)

        @block.vector
        def _(dve):
            f = Chain(dve, dch)
            dve.wait_ge(dt_turned, 1)
            f.link(dve.tensor_tensor(v[:], Q[:, 0, 0:NT * 16].rearrange("p (c h) -> p c h", h=16),
                                     row(L.cols[:, C_DB:C_DB + 16]), ALU.add))
            dve.scalar_tensor_tensor(e[:], v[:], -1.0, v[:], ALU.mult, ALU.min).then_inc(dt_dve, 1)
            dve.wait_ge(dt_act, 2)
            dve.tensor_scalar(w[:], e[:], 1.0, None, ALU.add).then_inc(dt_dve, 1)
            dve.wait_ge(dt_dve, 2)
            f.mark(dve.scalar_tensor_tensor(cc[:], w[:], 1.0, e[:], ALU.subtract, ALU.subtract))
            f.link(dve.tensor_scalar(t3[:], w[:], 0.5, -1.5, ALU.mult, ALU.add))
            f.link(dve.tensor_tensor(cc[:], cc[:], t3[:], ALU.mult))
            dve.wait_ge(dt_act, 3)
            f.link(dve.tensor_tensor(lw[:], lw[:], cc[:], ALU.add))
            f.link(dve.scalar_tensor_tensor(dt[:], v[:], 0.0, lw[:], ALU.max, ALU.add))
            dve.tensor_scalar(w[:], dt[:], 2.0 ** -60, None, ALU.max).then_inc(dt_dve, 1)
            dve.scalar_tensor_tensor(da[:], dt[:], -1.0, row(rate[:]), ALU.mult, ALU.mult).then_inc(dt_dve, 1)
            dve.wait_ge(st_turned, 1)
            f.mark(dve.tensor_copy(sb_in[:, down[0], :], A[2][:]))
            f.link(dve.tensor_copy(sf[:, 0, :], A[3][:]))
            dve.sem_inc(sf_ready, 1)
            f.mark(dve.memset(sb_in[:, NT - 1, :], 0.0))
            dve.wait_ge(dt_pe, 2)
            cum = Q[:, 1, 0:NT * 16].rearrange("p (c h) -> p c h", h=16)
            tot = Q[:, 0, 0:NT * 16].rearrange("p (c h) -> p c h", h=16)
            f.mark(dve.tensor_tensor(u[:], cum, krow(K_SA), ALU.mult))
            f.link(dve.tensor_tensor(t3[:], da[:], krow(K_SB), ALU.mult))
            f.link(dve.tensor_tensor(u[:], u[:], t3[:], ALU.add))
            dve.wait_ge(dt_act, 5)
            f.mark(dve.tensor_tensor(eoff[:], tot, krow(K_MT), ALU.mult))
            f.link(dve.tensor_tensor(wgt[:], tot, krow(K_MD), ALU.mult))
            f.mark(dve.tensor_tensor(eoff[:], eoff[:], u[:], ALU.add))
            dve.tensor_tensor(wgt[:], wgt[:], u[:], ALU.subtract).then_inc(dt_dve, 1)
            f.link(dve.tensor_tensor(w[:], w[:], v[:], ALU.min))
            f.link(dve.tensor_tensor(up[:], u[:], w[:], ALU.subtract))
            dve.wait_ge(consts, 1)
            for i, x in enumerate((u, up)):
                f.link(dve.tensor_copy(rnd[:], x[:]))
                f.link(dve.tensor_copy(pack[:, i, :, 0:16], rnd[:].bitcast(F32)))
                dve.tensor_tensor(pack[:, i, :, 32:48], x[:], rnd[:].bitcast(F32), ALU.subtract).then_inc(packed, 1)
                dve.wait_ge(packed, i + 1)
            dve.wait_ge(dt_act, 7)
            f.mark(dve.tensor_tensor(wgt[:], wgt[:], dt[:], ALU.mult))
            for n, (which, c0, k) in enumerate(U_GROUPS):
                dve.wait_ge(u_turned, n + 1)
                dst = (u2, up2)[which]
                dve.tensor_copy(dst[0:64, c0 * P:(c0 + k) * P], Q[0:64, n % 2, 0:k * P]).then_inc(u_read, 1)
            f.wait()

            def weigh(n, c, slot, first):
                dve.tensor_tensor(heads(xw[:, slot, :]), heads(xs[:, c, :]), across(wgt[:, c, first:first + 8], SP_),
                                  ALU.mult).then_inc(xw_ready, 1)

            for i, c in enumerate(down):
                for j in ((0, 1) if i == 0 else (i + 1,)):
                    if j < NT:
                        dve.wait_ge(x_copied, 3 * j + 3)
                        if j >= 2:
                            dve.wait_ge(s_mm, j - 1)
                        weigh(j, down[j], j % 2, 8)
                dve.wait_ge(s_mm, i + 1)
                if c != 0:
                    f.link(dve.tensor_tensor(heads(tmp[:]), heads(sb_in[:, c, :]), across(cdrow[:, c, 8:16], SP_),
                                             ALU.mult))
                    dst = fin[:, 1, :] if c == NT_LAT else sb_in[:, c - 1, :]
                    f.link(dve.tensor_tensor(dst, tmp[:], Q[:, i % 2, :], ALU.add))
                dve.sem_inc(s_ready, 1)

            def mix(c):
                dve.wait_ge(y_turned, c + 1)
                dve.tensor_tensor(mix_out[:, c, :].rearrange("p (a t) -> p a t", a=4),
                                  A[0][:].rearrange("p (a t) -> p a t", a=4),
                                  across(L.cols[:, C_GS:C_GS + 4], P), ALU.mult).then_inc(mix_ready, 1)

            for c in range(NT):
                dve.wait_ge(off_done, c + 1)
                if c >= 2:
                    dve.wait_ge(yn_ready, c - 1)
                f.mark(dve.tensor_tensor(heads(yv[:, c % 2, :]), heads(A[1][:]), across(eoff[:, c, 0:8], SP_), ALU.mult))
                f.link(dve.tensor_tensor(heads(off_b[:]), heads(A[2][:]), across(eoff[:, c, 8:16], SP_), ALU.mult))
                dve.sem_inc(off_read, 1)
                f.link(dve.tensor_tensor(yv[:, c % 2, :], yv[:, c % 2, :], off_b[:], ALU.add))
                dve.wait_ge(exp_done, c + 1)
                if c >= 1:
                    dve.wait_ge(diag_done, c)
                f.link(dve.tensor_tensor(wt[:], seg[:, 0:SH, :], seg[:, SH:2 * SH, :], ALU.add))
                dve.wait_ge(cb_read, c + 1)
                dve.tensor_tensor(wt[:].rearrange("p (g r) l -> p g r l", g=2),
                                  wt[:].rearrange("p (g r) l -> p g r l", g=2),
                                  cb[:].unsqueeze(2).to_broadcast([P, 2, 4, P]), ALU.mult).then_inc(w_ready, 1)
                dve.wait_ge(s_mm, NT + c + 1)
                if c == NT_LAT - 1:
                    f.link(dve.memset(sf[:, 1 - c % 2, :], 0.0))
                else:
                    dve.wait_ge(dec_ready, c + 1 - (c >= NT_LAT))
                    dst = fin[:, 0, :] if c == NT - 1 else sf[:, 1 - c % 2, :]
                    f.link(dve.tensor_tensor(dst, decayed[:], A[1][:], ALU.add))
                dve.sem_inc(sf_ready, 1)
                if c >= 1:
                    mix(c - 1)
                dve.wait_ge(diag_done, c + 1)
                f.link(dve.tensor_tensor(yv[:, c % 2, :], yv[:, c % 2, :], A[3][:], ALU.add))
                dve.tensor_tensor(yv[:, c % 2, :], yv[:, c % 2, :], zt[:, c, :], ALU.mult).then_inc(y_ready, 1)
            for d in range(2):
                dve.wait_ge(fin_mm, d + 1)
                dve.tensor_copy(st_in[:, d, :, :], A[1 + d][:].rearrange("p (a n) -> p a n", a=4)).then_inc(fin_cp, 1)
            mix(NT - 1)

        @block.tensor
        def _(pe):
            for c in range(NT):
                mm = pe.transpose(Q[:, 0, c * 16:(c + 1) * 16], L.dtT[0:16, chunk(c)], L.const[0:16, 0:16])
            mm.then_inc(dt_turned, 1)
            pe.wait_ge(st_loaded, 32)
            for a in range(4):
                pe.transpose(A[2][:, chunk(a)], st_in[:, 1, a, :], L.ident)
            for a in range(4):
                mm = pe.transpose(A[3][:, chunk(a)], st_in[:, 0, a, :], L.ident)
            mm.then_inc(st_turned, 1)
            pe.wait_ge(dt_dve, 4)
            pe.matmul(Q[:, 0, 0:NT * 16], L.ones[:], flat(da[:]), start=True, stop=True).then_inc(dt_pe, 1)
            pe.matmul(Q[:, 1, 0:NT * 16], L.const[:, K_TRI:K_TRI + P], flat(da[:]), start=True, stop=True
                      ).then_inc(dt_pe, 1)

            def turn(i):
                c = down[i]
                if i >= 2:
                    pe.wait_ge(x_copied, 3 * i - 3)
                else:
                    pe.wait_ge(sf_ready, 1)
                for a in range(4):
                    pe.transpose(A[i % 2][:, chunk(a)], L.xbcT[:, a, chunk(c)], L.ident)
                for g in range(2):
                    pe.transpose(A[2 + i % 2][:, chunk(g)], L.xbcT[:, 4 + g, chunk(c)], L.ident)
                pe.wait_ge(z_loaded[i % 2], 16 * (i // 2 + 1))
                for a in range(4):
                    mm = pe.transpose(Q[:, 2 + i % 2, chunk(a)], zc[:, i % 2, a, :], L.ident)
                mm.then_inc(x_turned, 1)

            turn(0)
            turn(1)
            for n, (which, c0, k) in enumerate(U_GROUPS):
                if n == 0:
                    pe.wait_ge(dt_dve, 5)
                pe.wait_ge(packed, which + 1)
                if n >= 2:
                    pe.wait_ge(u_read, n - 1)
                for j in range(k):
                    mm = pe.transpose(Q[0:64, n % 2, chunk(j)], pack[:, which, c0 + j, :], L.ident)
                mm.then_inc(u_turned, 1)

            def contribution(n, c, slot, dst):
                if n < NT:
                    pe.wait_ge(xw_ready, n + 1)
                else:
                    pe.wait_ge(xwf_ready, c + 1)
                for g in range(2):
                    mm = pe.matmul(dst[:, g * 256:(g + 1) * 256], bt[:, c, g, :], xw[:, slot, g * 256:(g + 1) * 256],
                                   start=True, stop=True)
                mm.then_inc(s_mm, 1)

            for i, c in enumerate(down):
                if 2 <= i + 1 < NT:
                    turn(i + 1)
                if i == 0:
                    pe.wait_ge(u_read, len(U_GROUPS))
                if i >= 2:
                    pe.wait_ge(s_ready, i - 1)
                contribution(i, c, i % 2, Q[:, i % 2, :])

            def segments(c):
                if c >= 1:
                    pe.wait_ge(exp_done, c)
                pe.wait_ge(u_loaded[c % 2], 16 * (c // 2 + 1))
                for q in range(4):
                    pe.matmul(Q[:, q, :], up2[:, chunk(c)], flat(pick[:, c % 2, 4 * q:4 * q + 4, :]), start=True,
                              stop=False)
                    mm = pe.matmul(Q[:, q, :], identb[:], flat(maskb[:, q // 2, :, :]), start=False, stop=True)
                mm.then_inc(seg_done, 1)

            def y_turn(c):
                pe.wait_ge(yn_ready, c + 1)
                for a in range(4):
                    mm = pe.transpose(A[0][:, chunk(a)], yn[:, chunk(a)], L.ident)
                mm.then_inc(y_turned, 1)

            pe.wait_ge(consts, 7)
            pe.wait_ge(ones_set, 1)
            pe.wait_ge(s_ready, NT)
            pe.wait_ge(x_copied, 3 * NT)
            segments(0)
            for c in range(NT):
                if c >= 1:
                    pe.wait_ge(cb_read, c)
                if c >= 2:
                    pe.wait_ge(mix_ready, c - 1)
                for g in range(2):
                    mm = pe.matmul(A[0][:, chunk(g)], L.xbcT[:, 4 + g, chunk(c)], L.xbcT[:, 6 + g, chunk(c)],
                                   start=True, stop=True)
                mm.then_inc(cb_done, 1)
                pe.wait_ge(sf_ready, c + 1)
                if c >= 1:
                    pe.wait_ge(off_read, c)
                for d, state in ((0, sf[:, c % 2, :]), (1, sb_in[:, c, :])):
                    for g in range(2):
                        mm = pe.matmul(A[1 + d][:, g * 256:(g + 1) * 256], L.xbcT[:, 6 + g, chunk(c)],
                                       state[:, g * 256:(g + 1) * 256], start=True, stop=True)
                mm.then_inc(off_done, 1)
                if c + 1 < NT:
                    segments(c + 1)
                pe.wait_ge(off_read, c + 1)
                contribution(NT + c, c, 0, A[1])
                if c >= 1:
                    pe.wait_ge(y_ready, c)
                for a in range(4):
                    pe.matmul(A[3][:, chunk(a)], L.xbcT[:, a, chunk(c)], ddiag[:, a, :], start=(a == 0), stop=False)
                if c >= 1:
                    pe.wait_ge(cb_read, c + 1)
                    y_turn(c - 1)
                pe.wait_ge(w_ready, c + 1)
                for h in range(SH):
                    mm = pe.matmul(A[3][:, h * SP_:(h + 1) * SP_], wt[:, h, :], xs[:, c, h * SP_:(h + 1) * SP_],
                                   start=False, stop=(h == SH - 1))
                mm.then_inc(diag_done, 1)
            pe.wait_ge(sf_ready, NT + 1)
            for d in range(2):
                for a in range(4):
                    mm = pe.transpose(A[1 + d][:, chunk(a)], fin[:, d, chunk(a)], L.ident)
                mm.then_inc(fin_mm, 1)
            pe.wait_ge(mix_ready, NT - 1)
            y_turn(NT - 1)


def phase_attention(L):
    nc = L.nc
    L.next_phase()
    with ExitStack() as st:
        wq_raw = L.sb(st, "wq_raw", [P, KQ, 256])
        wk_raw = L.sb(st, "wk_raw", [P, KKV, P])
        wv_raw = L.sb(st, "wv_raw", [P, KKV, 256])
        wq_hi, wq_lo = (L.sb(st, f"wq_{n}", [P, KQ, 256], F32R) for n in ("hi", "lo"))
        wk_hi, wk_lo = (L.sb(st, f"wk_{n}", [P, KKV, P], F32R) for n in ("hi", "lo"))
        wv_hi, wv_lo = (L.sb(st, f"wv_{n}", [P, KKV, 256], F32R) for n in ("hi", "lo"))
        kn_hi, kn_lo = (L.sb(st, f"kn_{n}", [P, NKEY], F32R) for n in ("hi", "lo"))
        v_hi, v_lo = (L.sb(st, f"v_{n}", [P, NKEY // P, 2, VD], F32R) for n in ("hi", "lo"))
        q_hi, q_lo = (L.sb(st, f"q_{n}", [P, T], F32R) for n in ("hi", "lo"))
        qr = L.sb(st, "q_rope", [P, T], F32R)
        prod = L.sb(st, "q_prod", [P, T])
        prob = L.sb(st, "prob", [P, 3, T])
        pt_hi, pt_lo = (L.sb(st, f"pt_{n}", [P, NT, 2 * P], F32R) for n in ("hi", "lo"))
        mx, nm, sm, rc = (L.sb(st, f"sm_{n}", [P, HEADS * NT]) for n in ("mx", "nm", "sum", "rec"))
        psS = L.ps(st, "psScore", [P, 5, 512])
        psPT = L.ps(st, "psPT", [P, 2, 4, P])
        psO = L.ps(st, "psO", [P, 4 * P])
        rb = L.sb(st, "reciprocals", [P, 2 * P])
        (wl, wvl, w_hi_r, w_split, proj, drained, hi_done, score, m_ready, nm_ready, e_ready,
         pt_done, pth_ready, ptl_ready, pv, o_read, dch) = (L.sem("at_" + n) for n in (
             "wl", "wvl", "w_hi", "w_split", "proj", "drained", "hi_done", "score", "m_ready",
             "nm_ready", "e_ready", "pt_done", "pth_ready", "ptl_ready", "pv", "o_read", "dch"))
        S = flat(psS[:])
        q_in, kv_in = prob, flat(L.mixA[:])[:, 0:KKV * NKEY].rearrange("p (k t) -> p k t", k=KKV)
        kr_in = flat(L.mixA[:])[:, KKV * NKEY:(KKV + 1) * NKEY]
        keys3 = [(0, 512), (512, 512), (1024, 512)]
        landed = ([(q_in[:, :, c:c + w], L.qn_hi[:, :, c:c + w], L.qn_lo[:, :, c:c + w],
                    L.q_s.rearrange("a p t -> p a t")[:, :, c:c + w]) for c, w in BLOCKS] +
                  [(kv_in[:, :, c:c + w], L.ckv_hi[:, :, c:c + w], L.ckv_lo[:, :, c:c + w],
                    L.kv_s.rearrange("a p t -> p a t")[:, :, c:c + w]) for c, w in keys3] +
                  [(kr_in, L.kr_hi[:], L.kr_lo[:], L.kr_s)])
        in_loaded = [L.sem(f"at_in_loaded{i}") for i in range(len(landed))]
        rc_ready, rb_ready, in_hi, in_lo, t_loaded = (L.sem("at_" + n) for n in ("rc", "rb", "in_hi", "in_lo", "table"))
        units = [(h, t) for h in range(HEADS) for t in range(NT)]
        key_tiles = lambda t: list(range(NT_LAT, NT)) if t >= NT_LAT else list(range(NT_LAT)) + [NT, NT + 1]
        groups = lambda t: [list(range(g, min(g + 4, len(key_tiles(t))))) for g in range(0, len(key_tiles(t)), 4)]
        n_groups = lambda u: sum(len(groups(units[i][1])) for i in range(u))
        width = lambda t: len(key_tiles(t)) * P

        def pieces(u):
            t, base = units[u][1], T * (u % 2)
            if t >= NT_LAT:
                return [(base, N_LAT, N_PROMPT)]
            if base == 0:
                return [(0, 0, 512), (512, 512, 512), (1024, T, N_CACHE)]
            return [(1536, 0, 512), (2048, 512, 512), (1280, T, N_CACHE)]

        def tile_col(u, i):
            kt = key_tiles(units[u][1])[i]
            for col, k0, w in pieces(u):
                if k0 <= kt * P < k0 + w:
                    return col - T * (u % 2) + kt * P - k0
            raise ValueError(i)

        block = st.enter_context(nc.Block())
        RING = [3, 4, 1, 0, 2]
        KEY_BLOCKS = [(0, 512), (512, 512), (1024, 512)]
        stage = {"qrope": BLOCKS, "k": KEY_BLOCKS, "fold": BLOCKS, "q": BLOCKS, "v": [(2 * i, 2) for i in range(6)]}
        order = ["qrope", "k", "fold", "q", "v"]

        def projections(h):
            kinds = order if h % 2 == 0 else order[:-1]
            return [(kind, b) for kind in kinds for b in range(len(stage[kind]))]

        n_proj = lambda h: sum(len(projections(i)) for i in range(h))
        n_high = lambda h: n_proj(h) - 3 * h

        def of_kind(h, kind):
            return [(b, n_proj(h) + i, i) for i, (k, b) in enumerate(projections(h)) if k == kind]

        def high_index(h, i):
            return n_high(h) + i - 3

        def operand(kind, b):
            c0, w = stage[kind][b]
            if kind == "v":
                return v_hi[:, c0:c0 + 2, :, :], v_lo[:, c0:c0 + 2, :, :], 512
            if kind == "fold":
                return qr[:, c0:c0 + w], qr[64:128, c0:c0 + w], w
            hi, lo = (kn_hi, kn_lo) if kind == "k" else (q_hi, q_lo)
            return hi[:, c0:c0 + w], lo[:, c0:c0 + w], w

        @block.sync
        def _(sp):
            for h in range(HEADS):
                if h >= 1:
                    sp.wait_ge(w_split, h)
                sp.dma_start(wq_raw[:], L.dram["w_uq"][h]).then_inc(wl, 16)
                sp.dma_start(wk_raw[:], L.dram["w_uk"][h]).then_inc(wl, 16)
                if h % 2 == 0:
                    sp.dma_start(wv_raw[:], L.dram["w_uv"][h // 2]).then_inc(wvl, 16)
                if h == 0:
                    for i, (dst, _, _, src) in enumerate(landed):
                        sp.dma_start(dst, src).then_inc(in_loaded[i], 16)
                        if i == 0:
                            sp.dma_start(L.table[:], L.dram["rope_table"]).then_inc(t_loaded, 16)
            L.clear_old()

        @block.scalar
        def _(act):
            def split(h):
                act.wait_ge(wl, 32 * (h + 1))
                if h >= 1:
                    act.wait_ge(proj, n_proj(h))
                act.activation(wq_hi[:], wq_raw[:], ACT.Copy).then_inc(w_hi_r, 1)
                act.activation(wk_hi[:], wk_raw[:], ACT.Copy).then_inc(w_hi_r, 1)
                if h % 2 == 0:
                    act.wait_ge(wvl, 16 * (h // 2 + 1))
                    act.activation(wv_hi[:], wv_raw[:], ACT.Copy).then_inc(w_hi_r, 1)

            def high(h, kind):
                for b, n, i in of_kind(h, kind):
                    hi, _, w = operand(kind, b)
                    src = psS[:, RING[i % 5], :w]
                    act.wait_ge(proj, n + 1)
                    if kind == "v":
                        src = src.rearrange("p (a h v) -> p a h v", a=2, h=2)
                    act.activation(hi, src, ACT.Copy).then_inc(hi_done, 1)

            def exp(u):
                w, base = width(units[u][1]), T * (u % 2)
                act.wait_ge(nm_ready, u + 1)
                act.activation(prob[:, u % 3, 0:w], S[:, base:base + w], ACT.Exp, bias=nm[:, u:u + 1], scale=SCALE,
                               accum_out=sm[:, u:u + 1]).then_inc(e_ready, 1)

            def pt(u):
                g0, r = n_groups(u), (u % 2) * P
                if u >= 2:
                    act.wait_ge(pv, u // 2)
                for i, g in enumerate(groups(units[u][1])):
                    act.wait_ge(pt_done, g0 + i + 1)
                    act.activation(pt_hi[:, g[0]:g[-1] + 1, r:r + P], psPT[:, (g0 + i) % 2, 0:len(g), :], ACT.Copy
                                   ).then_inc(pth_ready, 1)

            def out(pair):
                act.wait_ge(pv, pair + 1)
                if pair >= 1:
                    act.wait_ge(o_read, pair)
                act.activation(rb[:], psO[:, 2 * P:4 * P], ACT.Copy).then_inc(rb_ready, 1)

            split(0)
            for i, (src, hi, _, _) in enumerate(landed):
                act.wait_ge(in_loaded[i], 16)
                act.activation(hi, src, ACT.Copy).then_inc(in_hi, 1)
            for kind in order[1:]:
                high(0, kind)
            act.wait_ge(in_lo, len(landed))
            for h in range(HEADS):
                for t in range(NT):
                    u = h * NT + t
                    if t % 2 == 0 and t >= 4:
                        out(u // 2 - 2)
                    if t >= 2:
                        pt(u - 2)
                    exp(u)
                    if t == 5 and h + 1 < HEADS:
                        split(h + 1)
                out(u // 2 - 1)
                pt(u - 1)
                if h + 1 < HEADS:
                    high(h + 1, "k")
                pt(u)
                if h + 1 < HEADS:
                    high(h + 1, "fold")
                out(u // 2)
                if h + 1 < HEADS:
                    high(h + 1, "q")
                    high(h + 1, "v")

        @block.vector
        def _(dve):
            c = Chain(dve, dch)

            def split(h):
                dve.wait_ge(w_hi_r, 2 * h + 2 + (h + 1) // 2)
                c.mark(dve.tensor_tensor(wq_lo[:], wq_raw[:], wq_hi[:].bitcast(F32), ALU.subtract))
                c.mark(dve.tensor_tensor(wk_lo[:], wk_raw[:], wk_hi[:].bitcast(F32), ALU.subtract))
                if h % 2 == 0:
                    dve.wait_ge(w_hi_r, 2 * h + 3 + h // 2)
                    c.mark(dve.tensor_tensor(wv_lo[:], wv_raw[:], wv_hi[:].bitcast(F32), ALU.subtract))
                c.wait()
                dve.sem_inc(w_split, 1)

            def rotate(h):
                for b, n, i in of_kind(h, "qrope"):
                    c0, w = BLOCKS[b]
                    dve.wait_ge(proj, n + 1)
                    dve.tensor_tensor(prod[:, c0:c0 + w], psS[:, RING[i % 5], :w], L.table[:, c0:c0 + w], ALU.mult
                                      ).then_inc(drained, 1)

            def low(h, kind):
                for b, n, i in of_kind(h, kind):
                    hi, lo, w = operand(kind, b)
                    src = psS[:, RING[i % 5], :w]
                    dve.wait_ge(hi_done, high_index(h, i) + 1)
                    if kind == "v":
                        src = src.rearrange("p (a h v) -> p a h v", a=2, h=2)
                    if kind == "fold":
                        src, hi = src[64:128, :], lo
                    dve.tensor_tensor(lo, src, hi.bitcast(F32), ALU.subtract).then_inc(drained, 1)

            def maximum(u):
                w, base = width(units[u][1]), T * (u % 2)
                dve.wait_ge(score, u + 1)
                dve.tensor_reduce(mx[:, u:u + 1], S[:, base:base + w], AX_X, ALU.max).then_inc(m_ready, 1)
                dve.wait_ge(m_ready, u + 1)
                dve.tensor_scalar(nm[:, u:u + 1], mx[:, u:u + 1], -SCALE, None, ALU.mult).then_inc(nm_ready, 1)

            def invert(u):
                dve.wait_ge(e_ready, u + 1)
                dve.reciprocal(rc[:, u:u + 1], sm[:, u:u + 1]).then_inc(rc_ready, 1)

            def out(pair):
                h, t = units[2 * pair]
                dve.wait_ge(rb_ready, pair + 1)
                dve.tensor_tensor(L.mixA[:, h, t * P:(t + 2) * P], psO[:, 0:2 * P], rb[:], ALU.mult
                                  ).then_inc(o_read, 1)

            def pt(u, part):
                g0, r = n_groups(u), (u % 2) * P
                for i, g in enumerate(groups(units[u][1])):
                    if (i >= 2) == bool(part):
                        dve.wait_ge(pth_ready, g0 + i + 1)
                        dve.tensor_tensor(pt_lo[:, g[0]:g[-1] + 1, r:r + P], psPT[:, (g0 + i) % 2, 0:len(g), :],
                                          pt_hi[:, g[0]:g[-1] + 1, r:r + P].bitcast(F32), ALU.subtract
                                          ).then_inc(ptl_ready, 1)

            def split_in(first, last):
                for i in range(first, last):
                    src, hi, lo, _ = landed[i]
                    dve.wait_ge(in_hi, i + 1)
                    dve.tensor_tensor(lo, src, hi.bitcast(F32), ALU.subtract).then_inc(in_lo, 1)

            split(0)
            split_in(0, 3)
            dve.wait_ge(t_loaded, 16)
            rotate(0)
            split_in(3, 7)
            for kind in order[1:]:
                low(0, kind)
            for h in range(HEADS):
                for t in range(NT):
                    u = h * NT + t
                    if t >= 2:
                        pt(u - 2, 0)
                    if t % 2 == 0 and t >= 4:
                        out(u // 2 - 2)
                    maximum(u)
                    if t >= 2:
                        pt(u - 2, 1)
                    if t >= 1:
                        invert(u - 1)
                    if t == 5 and h + 1 < HEADS:
                        split(h + 1)
                if h + 1 < HEADS:
                    rotate(h + 1)
                invert(u)
                out(u // 2 - 1)
                for part in range(2):
                    pt(u - 1, part)
                if h + 1 < HEADS:
                    low(h + 1, "k")
                for part in range(2):
                    pt(u, part)
                if h + 1 < HEADS:
                    low(h + 1, "fold")
                out(u // 2)
                if h + 1 < HEADS:
                    low(h + 1, "q")
                    low(h + 1, "v")

        @block.tensor
        def _(pe):
            def project(h, kind):
                for b, n, i in of_kind(h, kind):
                    if i == 0:
                        pe.wait_ge(w_split, h + 1)
                    if i >= 5:
                        pe.wait_ge(drained, n - 4)
                    elif h >= 1:
                        pe.wait_ge(e_ready, h * NT - (0 if i == 4 else 1 if i == 3 else 2))
                    if h == 0 and kind in ("qrope", "k"):
                        pe.wait_ge(in_lo, b + 1 if kind == "qrope" else b + 4)
                    c0, w = stage[kind][b]
                    bank = psS[:, RING[i % 5], :]
                    if kind == "fold":
                        pe.wait_ge(drained, n_proj(h) + b + 1)
                        mm = pe.matmul(bank[:, :w], L.fold, prod[:, c0:c0 + w], start=True, stop=True)
                    elif kind == "v":
                        for j in range(2):
                            ks = slice((c0 + j) * P, (c0 + j + 1) * P)
                            for k in range(KKV):
                                mm = split3(pe, bank[:, j * 256:(j + 1) * 256], L.ckv_hi[:, k, ks], L.ckv_lo[:, k, ks],
                                            wv_hi[:, k, :], wv_lo[:, k, :], k == 0, k == KKV - 1)
                    else:
                        w_hi, w_lo, x_hi, x_lo, kn = ((wk_hi, wk_lo, L.ckv_hi, L.ckv_lo, KKV) if kind == "k" else
                                                      (wq_hi, wq_lo, L.qn_hi, L.qn_lo, KQ))
                        cols = slice(128, 256) if kind == "qrope" else slice(0, 128)
                        for k in range(kn):
                            mm = split3(pe, bank[:, :w], w_hi[:, k, cols], w_lo[:, k, cols], x_hi[:, k, c0:c0 + w],
                                        x_lo[:, k, c0:c0 + w], k == 0, k == kn - 1)
                    mm.then_inc(proj, 1)

            def scores(u, part):
                t, shared = units[u][1], pieces(u)[-1:]
                if len(pieces(u)) == 1 and u % 2 == 0:
                    shared = []
                todo = shared if part else pieces(u)[:len(pieces(u)) - len(shared)]
                if u == 0:
                    pe.wait_ge(in_lo, len(landed))
                if u % NT == 0 and part == 0:
                    pe.wait_ge(drained, n_proj(units[u][0] + 1))
                elif u % NT >= 1 + (part == 0):
                    pe.wait_ge(e_ready, u - 1 + part)
                q = slice(t * P, (t + 1) * P)
                for col, k0, w in todo:
                    out, ks = S[:, col:col + w], slice(k0, k0 + w)
                    pe.matmul(out, q_hi[:, q], kn_hi[:, ks], start=True, stop=False)
                    pe.matmul(out, q_hi[:, q], kn_lo[:, ks], start=False, stop=False)
                    pe.matmul(out, q_lo[:, q], kn_hi[:, ks], start=False, stop=False)
                    pe.matmul(out, qr[:, q], L.kr_hi[:, ks], start=False, stop=False)
                    mm = pe.matmul(out, qr[:, q], L.kr_lo[:, ks], start=False, stop=True)
                    if (col, k0, w) == pieces(u)[-1]:
                        mm.then_inc(score, 1)

            def transposes(u, part):
                g0 = n_groups(u)
                pe.wait_ge(e_ready, u + 1)
                for i, g in enumerate(groups(units[u][1])):
                    if (i >= 2) != bool(part):
                        continue
                    if g0 + i >= 2:
                        pe.wait_ge(ptl_ready, g0 + i - 1)
                    for n, kt in enumerate(g):
                        mm = pe.transpose(psPT[:, (g0 + i) % 2, n, :],
                                          prob[:, u % 3, tile_col(u, kt):tile_col(u, kt) + P], L.ident)
                    mm.then_inc(pt_done, 1)

            def values(pair, part):
                h, t = units[2 * pair]
                kts = key_tiles(t)
                cut = min(4, len(kts))
                g = n_groups(2 * pair + 1)
                if part == 0:
                    if pair >= 1:
                        pe.wait_ge(o_read, pair)
                    pe.wait_ge(ptl_ready, g + 1)
                else:
                    pe.wait_ge(ptl_ready, n_groups(2 * pair + 2))
                for n, kt in list(enumerate(kts))[(0, cut)[part]:(cut, len(kts))[part]]:
                    split3(pe, psO[:, 0:2 * P], v_hi[:, kt, h % 2, :], v_lo[:, kt, h % 2, :], pt_hi[:, n, :],
                           pt_lo[:, n, :], n == 0, n == len(kts) - 1)
                if part == 0:
                    return
                pe.wait_ge(rc_ready, 2 * pair + 2)
                for j in range(2):
                    u = 2 * pair + j
                    mm = pe.matmul(psO[:, (2 + j) * P:(3 + j) * P], rc[:, u:u + 1].to_broadcast([P, P]), L.ident,
                                   start=True, stop=True)
                mm.then_inc(pv, 1)

            for kind in order:
                project(0, kind)
            for h in range(HEADS):
                for t in range(NT):
                    u = h * NT + t
                    scores(u, 0)
                    if t % 2 == 0 and t >= 4:
                        values(u // 2 - 2, 1)
                    if t >= 2:
                        transposes(u - 2, 0)
                    scores(u, 1)
                    if t >= 2:
                        transposes(u - 2, 1)
                    if t >= 3 and t % 2 == 1:
                        values(u // 2 - 1, 0)
                if h + 1 < HEADS:
                    project(h + 1, "qrope")
                values(u // 2 - 1, 1)
                for part in range(2):
                    transposes(u - 1, part)
                if h + 1 < HEADS:
                    project(h + 1, "k")
                for part in range(2):
                    transposes(u, part)
                if h + 1 < HEADS:
                    project(h + 1, "fold")
                for part in range(2):
                    values(u // 2, part)
                if h + 1 < HEADS:
                    project(h + 1, "q")
                    if (h + 1) % 2 == 0:
                        project(h + 1, "v")


class GateRows:

    def __init__(self, L, st, tag, part, g_post):
        self.L, self.part, self.g_post = L, part, g_post
        self.rows = L.sb(st, f"{tag}_rows", [P, 2, D])
        self.b = L.sb(st, f"{tag}_b", [P, D])
        self.g = L.sb(st, f"{tag}_g", [P, D])
        self.loaded = [L.sem(f"{tag}_g_loaded{g}") for g in range(2)]
        self.ready = L.sem(f"{tag}_g_ready")

    def load(self, eng):
        c = slice(self.part * D, (self.part + 1) * D)
        row = lambda g: eng.dma_start(self.rows[:, g, :], self.L.gate_rows[g:g + 1, c].to_broadcast([P, D])
                                      ).then_inc(self.loaded[g], 16)
        row(0)
        eng.dma_start(self.b[:], self.L.dram["b_mod"][:, c].to_broadcast([P, D])).then_inc(self.loaded[0], 16)
        eng.dma_start(self.g[:], self.L.dram[self.g_post].to_broadcast([P, D])).then_inc(self.loaded[0], 16)
        row(1)

    def dve(self, dve, g):
        dve.wait_ge(self.loaded[g], (48, 16)[g])
        dve.tensor_tensor(self.rows[:, g, :], self.rows[:, g, :], self.b[:], ALU.add).then_inc(self.ready, 1)
        dve.wait_ge(self.ready, 2 * g + 1)
        dve.tensor_tensor(self.rows[:, g, :], self.rows[:, g, :], self.g[:], ALU.mult).then_inc(self.ready, 1)
        dve.wait_ge(self.ready, 2 * g + 2)


def phase_out_proj(L):
    nc = L.nc
    L.next_phase()
    with ExitStack() as st:
        raw = L.sb(st, "wo_raw", [P, 4, D])
        w_hi, w_lo = (L.sb(st, f"wo_{n}", [P, KD, D], F32R) for n in ("hi", "lo"))
        m_hi, m_lo = (L.sb(st, f"mix_{n}", [P, 2, KD, P], F32R) for n in ("hi", "lo"))
        mixS = L.sb(st, "op_mixS", [P, 2, 4, P])
        xin = L.sb(st, "op_x", [P, 2, D])
        y = L.sb(st, "op_y", [P, 2, D])
        junk = L.sb(st, "op_sq", [P, D])
        ss, ms, rs, nh = (L.sb(st, f"op_{n}", [P, NT] if n != "nh" else [P, 1]) for n in ("ss", "ms", "rs", "nh"))
        ss2, ms2, rs2 = (L.sb(st, f"op_{n}2", [P, NT]) for n in ("ss", "ms", "rs"))
        gate = GateRows(L, st, "op", 2, "g_post_mix")
        psY = L.ps(st, "psY", [P, 2, 2, 512])
        w_loaded = [L.sem(f"wo_loaded{i}") for i in range(4)]
        x_loaded = [L.sem(f"op_x_loaded{i}") for i in range(2)]
        s_loaded = [L.sem(f"op_s_loaded{i}") for i in range(2)]
        y_stored = [L.sem(f"op_y_stored{i}") for i in range(2)]
        (sq2, ms2_r, rs2_r, xn_r, w_hi_r, w_lo_r, m_hi_r, m_lo_r, done, sq, ms_r, rs_r, yt, y_r, pch) = (
            L.sem("op_" + n) for n in ("y_squared", "y_ms", "y_rstd", "xn", "w_hi", "w_lo", "m_hi", "m_lo", "product",
                                       "squared", "ms", "rstd", "scaled", "y", "pool"))
        block = st.enter_context(nc.Block())

        def x_tile(t):
            if t < NT_LAT:
                return L.dram["x_sample"][t * P:(t + 1) * P, :]
            return L.dram["x_prompt"][(t - NT_LAT) * P:(t - NT_LAT + 1) * P, :]

        def mixes(t):
            return L.mixA[:, :, t * P:(t + 1) * P], mixS[:, t % 2, :, :]

        @block.sync
        def _(sp):
            def load_mix(t):
                if t >= 2:
                    sp.wait_ge(m_lo_r, 2 * t - 2)
                sp.dma_start(flat(mixS[:, t % 2, :, :]), L.mixS[t]).then_inc(s_loaded[t % 2], 16)

            load_mix(0)
            load_mix(1)
            for k in range(KD):
                if k >= 4:
                    sp.wait_ge(w_lo_r, k - 3)
                sp.dma_start(raw[:, k % 4, :], L.dram["w_out"][k * P:(k + 1) * P, :]).then_inc(w_loaded[k % 4], 16)
            gate.load(sp)
            for t in range(NT):
                if t >= 2:
                    sp.wait_ge(y_r, t - 1)
                sp.dma_start(xin[:, t % 2, :], x_tile(t)).then_inc(x_loaded[t % 2], 16)
                if t + 2 < NT:
                    load_mix(t + 2)
                if t >= 1:
                    sp.wait_ge(y_r, t)
                    sp.dma_start(L.y1[t - 1], y[:, (t - 1) % 2, :]).then_inc(y_stored[(t - 1) % 2], 16)
            L.clear_old()
            sp.wait_ge(y_r, NT)
            sp.dma_start(L.y1[NT - 1], y[:, (NT - 1) % 2, :]).then_inc(y_stored[(NT - 1) % 2], 16)
            for i in range(2):
                sp.wait_ge(y_stored[i], 16 * (NT // 2))

        @block.gpsimd
        def _(pool):
            pool.memset(nh[:], -0.5).then_inc(pch, 1)
            pool.wait_ge(pch, 1)
            for t in range(NT):
                pool.wait_ge(ms_r, t + 1)
                pool.tensor_tensor(rs[:, t:t + 1], ms[:, t:t + 1], nh[:], ALU.pow).then_inc(rs_r, 1)
                pool.wait_ge(ms2_r, t + 1)
                pool.tensor_tensor(rs2[:, t:t + 1], ms2[:, t:t + 1], nh[:], ALU.pow).then_inc(rs2_r, 1)

        @block.scalar
        def _(act):
            def mix_hi(t):
                if t >= 2:
                    act.wait_ge(done, t - 1)
                act.wait_ge(s_loaded[t % 2], 16 * (t // 2 + 1))
                for i, mix in enumerate(mixes(t)):
                    act.activation(m_hi[:, t % 2, 4 * i:4 * i + 4, :], mix, ACT.Copy
                                   ).then_inc(m_hi_r, 1)

            mix_hi(0)
            for k in range(KD):
                act.wait_ge(w_loaded[k % 4], 16 * (k // 4 + 1))
                act.activation(w_hi[:, k, :], raw[:, k % 4, :], ACT.Copy).then_inc(w_hi_r, 1)
            for t in range(NT):
                if t + 1 < NT:
                    mix_hi(t + 1)
                act.wait_ge(done, t + 1)
                if t >= 1:
                    act.wait_ge(sq2, t)
                act.activation(junk[:], flat(psY[:, t % 2, :, :]), ACT.Square, accum_out=ss[:, t:t + 1]
                               ).then_inc(sq, 1)
                act.wait_ge(y_r, t + 1)
                act.wait_ge(sq, t + 1)
                act.activation(L.facc[:, t, :], y[:, t % 2, :], ACT.Square, accum_out=ss2[:, t:t + 1]
                               ).then_inc(sq2, 1)

        @block.vector
        def _(dve):
            def mix_lo(t):
                dve.wait_ge(m_hi_r, 2 * t + 2)
                for i, mix in enumerate(mixes(t)):
                    dve.tensor_tensor(m_lo[:, t % 2, 4 * i:4 * i + 4, :], mix,
                                      m_hi[:, t % 2, 4 * i:4 * i + 4, :].bitcast(F32), ALU.subtract
                                      ).then_inc(m_lo_r, 1)

            mix_lo(0)
            for k in range(KD):
                dve.wait_ge(w_hi_r, k + 1)
                dve.tensor_tensor(w_lo[:, k, :], raw[:, k % 4, :], w_hi[:, k, :].bitcast(F32), ALU.subtract
                                  ).then_inc(w_lo_r, 1)
            for t in range(NT):
                if t + 1 < NT:
                    mix_lo(t + 1)
                if t in (0, 4):
                    gate.dve(dve, t // 4)
                s, g = t % 2, int(t >= NT_LAT)
                dve.wait_ge(sq, t + 1)
                dve.tensor_scalar(ms[:, t:t + 1], ss[:, t:t + 1], 1.0 / D, EPS, ALU.mult, ALU.add).then_inc(ms_r, 1)
                dve.wait_ge(rs_r, t + 1)
                if t >= 2:
                    dve.wait_ge(y_stored[s], 16 * (t // 2))
                    dve.wait_ge(xn_r, t - 1)
                dve.scalar_tensor_tensor(y[:, s, :], flat(psY[:, s, :, :]), rs[:, t:t + 1], gate.rows[:, g, :],
                                         ALU.mult, ALU.mult).then_inc(yt, 1)
                dve.wait_ge(yt, t + 1)
                dve.wait_ge(x_loaded[s], 16 * (t // 2 + 1))
                dve.tensor_tensor(y[:, s, :], y[:, s, :], xin[:, s, :], ALU.add).then_inc(y_r, 1)
                dve.wait_ge(sq2, t + 1)
                dve.tensor_scalar(ms2[:, t:t + 1], ss2[:, t:t + 1], 1.0 / D, EPS, ALU.mult, ALU.add
                                  ).then_inc(ms2_r, 1)
                dve.wait_ge(rs2_r, t + 1)
                dve.tensor_scalar(L.facc[:, t, :], y[:, s, :], rs2[:, t:t + 1], None, ALU.mult).then_inc(xn_r, 1)

        @block.tensor
        def _(pe):
            for t in range(NT):
                pe.wait_ge(m_lo_r, 2 * t + 2)
                if t >= 2:
                    pe.wait_ge(yt, t - 1)
                for k, half in ([(k, half) for k in range(KD) for half in range(2)] if t == 0 else
                                [(k, half) for half in range(2) for k in range(KD)]):
                    cols = slice(half * 512, (half + 1) * 512)
                    if t == 0 and half == 0:
                        pe.wait_ge(w_lo_r, k + 1)
                    mm = split3(pe, psY[:, t % 2, half, :], m_hi[:, t % 2, k, :], m_lo[:, t % 2, k, :],
                                w_hi[:, k, cols], w_lo[:, k, cols], k == 0, k == KD - 1)
                mm.then_inc(done, 1)


def phase_ffn(L):
    nc = L.nc
    L.next_phase()
    PAIRS = FT // 2
    GU = [(s, b) for s in range(2) for b in range(len(BLOCKS))]
    NG = len(GU)
    ND = 2 * NT
    with ExitStack() as st:
        raw_gu = L.sb(st, "raw_gu", [P, 2, D])
        raw_d = L.sb(st, "raw_d", [P, D])
        gu_hi, gu_lo = (L.sb(st, f"gu_{n}", [P, 2, 2, D], F32R) for n in ("hi", "lo"))
        d_hi, d_lo, h_hi, h_lo = L.d_hi, L.d_lo, L.h_hi, L.h_lo
        hid = L.sb(st, "hid", [P, 2, 512])
        psG = L.ps(st, "psG", [P, 2, 2, 512])
        psF = L.ps(st, "psF", [P, 4, 512])
        (gu_loaded, d_loaded, gu_hi_r, gu_lo_r, d_hi_r, d_lo_r, gu_used, silu, h_full, h_hi_r, h_lo_r, down,
         flushed) = (L.sem("ff_" + n) for n in (
             "gu_loaded", "d_loaded", "gu_hi", "gu_lo", "d_hi", "d_lo", "gu_used", "silu", "h_full", "h_hi", "h_lo",
             "down", "flushed"))
        turn = Turn(L, "n2", L.facc, psF, raw_d[:].rearrange("p (a n) -> p a n", a=2), L.h2_hi, L.h2_lo, L.scale2,
                    L.mod[:, 3 * KD:4 * KD, :])
        block = st.enter_context(nc.Block())

        def over_pairs(eng, body):
            body(0, True, False)
            with eng.Fori(1, PAIRS - 1) as i:
                body(i, False, False)
            body(PAIRS - 1, False, True)

        @block.sync
        def _(sp):
            def load_gu(n, first=False):
                if not first:
                    sp.wait_ge(gu_lo_r, n)
                for i, w in enumerate(("w_gate", "w_up")):
                    sp.dma_start(raw_gu[:, i, :], L.dram[w][bass.ds(n, 1)].rearrange("a p n -> (a p) n")
                                 ).then_inc(gu_loaded, 16)

            def load_d(n, first=False):
                if not first:
                    sp.wait_ge(d_lo_r, n)
                sp.dma_start(raw_d[:], L.dram["w_down"][bass.ds(n, 1)].rearrange("a p n -> (a p) n")
                             ).then_inc(d_loaded, 16)

            load_gu(0, True)
            load_gu(1)
            sp.wait_ge(turn.h_ready, len(turn.steps))
            load_d(0, True)
            load_d(1)
            with sp.Fori(1, PAIRS) as i:
                load_gu(2 * i)
                load_gu(2 * i + 1)
                load_d(2 * i)
                load_d(2 * i + 1)
            L.clear_old()

        @block.scalar
        def _(act):
            def split_gu(n, s, first=False):
                act.wait_ge(gu_loaded, n * 32 + 32)
                if not first:
                    act.wait_ge(gu_used, n * 3 - 3)
                act.activation(gu_hi[:, s, :, :], raw_gu[:], ACT.Copy).then_inc(gu_hi_r, 1)

            def split_d(n, s, i, first=False):
                act.wait_ge(d_loaded, n * 16 + 16)
                if not first:
                    act.wait_ge(down, i * ND)
                act.activation(d_hi[:, s, :], raw_d[:], ACT.Copy).then_inc(d_hi_r, 1)

            def body(i, first, last):
                for n, (s, b) in enumerate(GU):
                    c0, w = BLOCKS[b]
                    act.wait_ge(gu_used, i * NG + (n + 1))
                    if not (first and n < 2):
                        act.wait_ge(h_lo_r, i * NG + (n - 1))
                    act.activation(hid[:, n % 2, :w], psG[:, n % 2, 0, :w], ACT.Silu).then_inc(silu, 1)
                    act.wait_ge(h_full, i * NG + (n + 1))
                    act.activation(h_hi[:, s, c0:c0 + w], hid[:, n % 2, :w], ACT.Copy).then_inc(h_hi_r, 1)
                    if first and n == 0:
                        turn.act(act, 16, 24)
                    if first and n in (1, 3):
                        split_d(n // 2, n // 2, 0, True)
                    if b == 2 and not last:
                        split_gu(i * 2 + (2 + s), s)
                if not last:
                    for s in range(2):
                        split_d(i * 2 + (2 + s), s, i + 1)

            for s in range(2):
                turn.act(act, 8 * s, 8 * s + 8)
                split_gu(s, s, True)
            over_pairs(act, body)

        @block.vector
        def _(dve):
            def split_gu(n, s):
                dve.wait_ge(gu_hi_r, n + 1)
                dve.tensor_tensor(gu_lo[:, s, :, :], raw_gu[:], gu_hi[:, s, :, :].bitcast(F32), ALU.subtract
                                  ).then_inc(gu_lo_r, 1)

            def split_d(n, s):
                dve.wait_ge(d_hi_r, n + 1)
                dve.tensor_tensor(d_lo[:, s, :], raw_d[:], d_hi[:, s, :].bitcast(F32), ALU.subtract
                                  ).then_inc(d_lo_r, 1)

            def body(i, first, last):
                for n, (s, b) in enumerate(GU):
                    c0, w = BLOCKS[b]
                    dve.wait_ge(silu, i * NG + (n + 1))
                    dve.tensor_tensor(hid[:, n % 2, :w], hid[:, n % 2, :w], psG[:, n % 2, 1, :w], ALU.mult
                                      ).then_inc(h_full, 1)
                    dve.wait_ge(h_hi_r, i * NG + (n + 1))
                    dve.tensor_tensor(h_lo[:, s, c0:c0 + w], hid[:, n % 2, :w], h_hi[:, s, c0:c0 + w].bitcast(F32),
                                      ALU.subtract).then_inc(h_lo_r, 1)
                    if first and n == 0:
                        turn.dve(dve, 16, 24)
                    if first and n in (1, 3):
                        split_d(n // 2, n // 2)
                    if n == 2 and not last:
                        split_gu(i * 2 + 2, 0)
                for r in range(0 if last else ND):
                    t, cols = r // 2, slice((r % 2) * 512, (r % 2) * 512 + 512)
                    dve.wait_ge(down, i * ND + (r + 1))
                    if first:
                        dve.tensor_copy(L.facc[:, t, cols], psF[:, r % 4, :]).then_inc(flushed, 1)
                    else:
                        dve.wait_ge(flushed, i * ND + (r - ND + 1))
                        dve.tensor_tensor(L.facc[:, t, cols], L.facc[:, t, cols], psF[:, r % 4, :], ALU.add
                                          ).then_inc(flushed, 1)
                    if r == 5:
                        split_gu(i * 2 + 3, 1)
                if not last:
                    for s in range(2):
                        split_d(i * 2 + (2 + s), s)

            for s in range(2):
                turn.dve(dve, 8 * s, 8 * s + 8)
                split_gu(s, s)
            over_pairs(dve, body)

        @block.tensor
        def _(pe):
            def body(i, first, last):
                for n, (s, b) in enumerate(GU):
                    c0, w = BLOCKS[b]
                    if b == 0:
                        pe.wait_ge(gu_lo_r, i * 2 + (s + 1))
                    if not (first and n < 2):
                        pe.wait_ge(h_full, i * NG + (n - 1))
                    if first and s == 0:
                        pe.wait_ge(turn.h_ready, 8 * b + 8)
                    for j in range(2):
                        if first and n == 0:
                            turn.pe(pe, 8 + 4 * j, 12 + 4 * j)
                        if first and n == 1:
                            turn.pe(pe, 16 + 4 * j, 20 + 4 * j)
                        for k in range(KD):
                            ks = slice(k * P, (k + 1) * P)
                            mm = split3(pe, psG[:, n % 2, j, :w], gu_hi[:, s, j, ks], gu_lo[:, s, j, ks],
                                        L.h2_hi[:, k, c0:c0 + w], L.h2_lo[:, k, c0:c0 + w], k == 0, k == KD - 1)
                    mm.then_inc(gu_used, 1)
                if last:
                    return
                pe.wait_ge(d_lo_r, i * 2 + 2)
                for r in range(ND):
                    t, cols = r // 2, slice((r % 2) * 512, (r % 2) * 512 + 512)
                    if r in (0, 8, 16):
                        pe.wait_ge(h_lo_r, i * NG + (4 + r // 8))
                    if not (first and r < 4):
                        pe.wait_ge(flushed, i * ND + (r - 3))
                    ts = slice(t * P, (t + 1) * P)
                    for s in range(2):
                        mm = split3(pe, psF[:, r % 4, :], h_hi[:, s, ts], h_lo[:, s, ts], d_hi[:, s, cols],
                                    d_lo[:, s, cols], s == 0, s == 1)
                    mm.then_inc(down, 1)

            turn.pe(pe, 0, 8)
            over_pairs(pe, body)


def phase_final(L):
    nc = L.nc
    L.next_phase()
    with ExitStack() as st:
        yin = L.sb(st, "fi_y", [P, 4, D])
        out = L.sb(st, "fi_out", [P, 3, D])
        junk = L.sb(st, "fi_sq", [P, D])
        ss, ms, rs, nh = (L.sb(st, f"fi_{n}", [P, NT] if n != "nh" else [P, 1]) for n in ("ss", "ms", "rs", "nh"))
        psF = L.ps(st, "fi_psF", [P, 4, 512])
        gate = GateRows(L, st, "fi", 5, "g_post_ffn")
        y_loaded = [L.sem(f"fi_y_loaded{i}") for i in range(4)]
        stored = [L.sem(f"fi_stored{i}") for i in range(3)]
        down, flushed = L.sem("fi_down"), L.sem("fi_flushed")
        sq, ms_r, rs_r, yt, pch = (L.sem("fi_" + n) for n in ("sq", "ms", "rs", "yt", "pool"))
        y_r = [L.sem(f"fi_y{i}") for i in range(2)]
        block = st.enter_context(nc.Block())

        def add(eng, u):
            eng.wait_ge(yt, u + 1)
            eng.wait_ge(y_loaded[u % 4], 16 * (u // 4 + 1))
            eng.tensor_tensor(out[:, u % 3, :], out[:, u % 3, :], yin[:, u % 4, :], ALU.add).then_inc(y_r[u % 2], 1)

        @block.sync
        def _(sp):
            gate.load(sp)
            for t in range(4):
                sp.dma_start(yin[:, t, :], L.y1[t]).then_inc(y_loaded[t], 16)
            for t in range(NT):
                sp.wait_ge(y_r[t % 2], t // 2 + 1)
                dst = (L.outs["sample"][0, t * P:(t + 1) * P, :] if t < NT_LAT else
                       L.outs["prompt"][0, (t - NT_LAT) * P:(t - NT_LAT + 1) * P, :])
                sp.dma_start(dst, out[:, t % 3, :]).then_inc(stored[t % 3], 16)
                if t + 4 < NT:
                    sp.dma_start(yin[:, t % 4, :], L.y1[t + 4]).then_inc(y_loaded[t % 4], 16)
            for i in range(3):
                sp.wait_ge(stored[i], 16 * len(range(i, NT, 3)))

        @block.gpsimd
        def _(pool):
            pool.memset(nh[:], -0.5).then_inc(pch, 1)
            pool.wait_ge(pch, 1)
            for t in range(NT + 1):
                if t < NT:
                    pool.wait_ge(ms_r, t + 1)
                    pool.tensor_tensor(rs[:, t:t + 1], ms[:, t:t + 1], nh[:], ALU.pow).then_inc(rs_r, 1)
                if t % 2 == 1:
                    add(pool, t - 1)

        @block.scalar
        def _(act):
            for t in range(NT):
                act.wait_ge(flushed, t + 1)
                if t >= 1:
                    act.wait_ge(sq, t)
                act.activation(junk[:], L.facc[:, t, :], ACT.Square, accum_out=ss[:, t:t + 1]).then_inc(sq, 1)

        @block.vector
        def _(dve):
            for t in range(NT + 2):
                if t < NT:
                    b = 2 * (t % 2)
                    dve.wait_ge(down, t + 1)
                    dve.tensor_tensor(L.facc[:, t, :], L.facc[:, t, :], flat(psF[:, b:b + 2, :]), ALU.add
                                      ).then_inc(flushed, 1)
                if t in (0, 5):
                    gate.dve(dve, t // 5)
                if 1 <= t <= NT:
                    dve.wait_ge(sq, t)
                    dve.tensor_scalar(ms[:, t - 1:t], ss[:, t - 1:t], 1.0 / D, EPS, ALU.mult, ALU.add
                                      ).then_inc(ms_r, 1)
                if t < 2:
                    continue
                u = t - 2
                dve.wait_ge(rs_r, u + 1)
                if u >= 3:
                    dve.wait_ge(stored[u % 3], 16 * (u // 3))
                dve.scalar_tensor_tensor(out[:, u % 3, :], L.facc[:, u, :], rs[:, u:u + 1],
                                         gate.rows[:, int(u >= NT_LAT), :], ALU.mult, ALU.mult).then_inc(yt, 1)
                if u % 2 == 1:
                    add(dve, u)

        @block.tensor
        def _(pe):
            for t in range(NT):
                if t >= 2:
                    pe.wait_ge(flushed, t - 1)
                ts = slice(t * P, (t + 1) * P)
                for half in range(2):
                    cols = slice(half * 512, half * 512 + 512)
                    for s in range(2):
                        mm = split3(pe, psF[:, 2 * (t % 2) + half, :], L.h_hi[:, s, ts], L.h_lo[:, s, ts],
                                    L.d_hi[:, s, cols], L.d_lo[:, s, cols], s == 0, s == 1)
                mm.then_inc(down, 1)


def hybrid_layer_kernel(nc, dram, outs):
    with ExitStack() as stack:
        L = Layer(nc, dram, outs)
        sb = L.sb
        L.const = sb(stack, "const", [P, N_CONST])
        L.ident = L.const[:, K_ID:K_ID + P]
        L.fold = L.const[:, K_FOLD:K_FOLD + P]
        L.cols = sb(stack, "cols", [P, N_COLS])
        L.mod = sb(stack, "mod", [P, 6 * KD, 2])
        L.scale1, L.scale2 = (sb(stack, f"scale{i}", [P, KD, 2]) for i in (1, 2))
        L.y1 = nc.dram_tensor("y1_scratch", (NT, P, D), F32, kind="Internal").ap()
        L.mixS = nc.dram_tensor("ssm_mix_scratch", (NT, P, SW), F32, kind="Internal").ap()
        L.staged = nc.dram_tensor("staged_scratch", (N_Z, P, T), F32, kind="Internal").ap()
        L.u_s = nc.dram_tensor("u_scratch", (2, 16, T), F32, kind="Internal").ap()
        L.q_s = nc.dram_tensor("q_scratch", (KQ, P, T), F32, kind="Internal").ap()
        L.kv_s = nc.dram_tensor("kv_scratch", (KKV, P, NKEY), F32, kind="Internal").ap()
        L.kr_s = nc.dram_tensor("kr_scratch", (P, NKEY), F32, kind="Internal").ap()
        L.gate_rows = nc.dram_tensor("gate_rows", (2, 6 * D), F32, kind="Internal").ap()
        with ExitStack() as ssm:
            L.xbcT = sb(ssm, "xbcT", [P, N_XBC, T], side="right")
            L.dtT = sb(ssm, "dtT", [P, T], side="right")
            L.ones = sb(ssm, "ones", [P, P], side="right")
            L.xn = L.xbcT[:].rearrange("p a t -> p (a t)").rearrange("p (t d) -> p t d", d=D)
            with ExitStack() as proj:
                L.cond_st = sb(proj, "cond_st", [P, KD, P], F32R)
                phase_norm1(L)
                L.hT_hi, L.hT_lo = (sb(proj, f"hT_{n}", [P, KD, T], F32R) for n in ("hi", "lo"))
                phase_in_proj(L)
            phase_ssm(L)
        with ExitStack() as mixer:
            L.mixA = sb(mixer, "mixA", [P, HEADS, T])
            with ExitStack() as attn:
                L.table = sb(attn, "rope_table", [P, T])
                L.qn_hi, L.qn_lo = (sb(attn, f"qn_{n}", [P, KQ, T], F32R) for n in ("hi", "lo"))
                L.ckv_hi, L.ckv_lo = (sb(attn, f"ckv_{n}", [P, KKV, NKEY], F32R) for n in ("hi", "lo"))
                L.kr_hi, L.kr_lo = (sb(attn, f"kr_{n}", [P, NKEY], F32R) for n in ("hi", "lo"))
                phase_attention(L)
            ffn = ExitStack()
            L.facc = sb(ffn, "facc", [P, NT, D], side="right")
            phase_out_proj(L)
        with ffn:
            L.d_hi, L.d_lo = (sb(ffn, f"d_{n}", [P, 2, D], F32R) for n in ("hi", "lo"))
            L.h_hi, L.h_lo = (sb(ffn, f"h_{n}", [P, 2, T], F32R) for n in ("hi", "lo"))
            with ExitStack() as h:
                L.h2_hi, L.h2_lo = (sb(h, f"h2_{n}", [P, KD, T], F32R) for n in ("hi", "lo"))
                phase_ffn(L)
            phase_final(L)


_OUTS = [("prompt", (1, N_PROMPT, D)), ("sample", (1, N_LAT, D)), ("ckv", (1, 1, N_PROMPT, KV_LORA)),
         ("krope", (1, 1, N_PROMPT, ROPE)), ("ssm", (1, 1, 2, SH, SP_, DS))]


def shape_constants(np):
    const = np.zeros((P, N_CONST), np.float32)
    i, j = np.arange(P)[:, None], np.arange(P)[None, :]
    const[:, K_ID:K_ID + P] = i == j
    const[:, K_MASK:K_MASK + P] = np.where(j >= i, 0.0, -1e30)
    const[:, K_MASK + P:K_MASK + 2 * P] = np.where(j <= i, 0.0, -1e30)
    h = np.arange(16)[None, :]
    const[:, K_SEL:K_SEL + 16] = (i == h) | (i == 32 + h)
    const[:, K_FOLD:K_FOLD + P] = (i % 64) == (j % 64)
    const[:, K_TRI:K_TRI + P] = i <= j
    const[:, K_SUM:K_SUM + 2] = (i % 32 == 0) & (i // 64 == np.arange(2)[None, :])
    forward = np.arange(16) < SH
    const[:, K_SA:K_SA + 16] = np.where(forward, 1.0, -1.0)
    const[:, K_SB:K_SB + 16] = np.where(forward, 0.0, 1.0)
    const[:, K_MD:K_MD + 16] = forward
    quarter = ROPE // 4
    inv = (np.float32(10000.0) ** (-np.arange(quarter, dtype=np.float32) / np.float32(quarter))).astype(np.float32)
    pos = np.arange(N_LAT)
    table = np.zeros((P, T), np.float32)
    table[0:ROPE, N_LAT:] = 1.0
    for half, where in enumerate((pos // 64, pos % 64)):
        ang = inv[:, None] * where[None, :].astype(np.float32)
        for part, sign in ((0, -1.0), (1, 1.0)):
            r = half * 2 * quarter + part * quarter
            table[r:r + quarter, 0:N_LAT] = np.cos(ang)
            table[ROPE + r:ROPE + r + quarter, 0:N_LAT] = sign * np.sin(ang)
    return const, table


def kernel(**inputs):
    import numpy as np
    import concourse.bacc as bacc
    from concourse.bass_utils import run_bass_kernel_spmd

    a = {k: np.asarray(v) for k, v in inputs.items()}
    const, table = shape_constants(np)
    swap = np.concatenate([np.arange(16, 32), np.arange(0, 16), np.arange(48, 64), np.arange(32, 48)])

    def col(v):
        return v.reshape(-1, P).T

    def k_tiles(w):
        return w.reshape(-1, P, w.shape[1]).transpose(1, 0, 2)

    w_in = a["w_in"][0]
    o_kv, o_r = Q_LORA, Q_LORA + KV_LORA
    o_z = o_r + ROPE
    o_x = o_z + SW
    o_dt = o_x + N_XBC * P
    start = {"xbc": o_x, "z": o_z, "q": 0, "kv": o_kv}
    rope = w_in[:, o_r:o_z]

    def in_tile(kind, i):
        if kind == "rope":
            return np.concatenate([rope, rope[:, swap]], axis=1)
        if kind == "dt":
            return np.tile(w_in[:, o_dt:o_dt + 16], (1, 8))
        return w_in[:, start[kind] + P * i:start[kind] + P * (i + 1)]

    w_uq = a["w_uq"][0].reshape(Q_LORA, HEADS, NOPE + ROPE).transpose(1, 0, 2)
    w_uq = np.concatenate([w_uq, w_uq[:, :, NOPE + swap]], axis=2)

    w_ukv = a["w_ukv"][0].reshape(KV_LORA, HEADS, NOPE + VD)

    def f_tiles(w):
        return w.reshape(KD, P, FT, P).transpose(2, 1, 0, 3).reshape(FT, P, D)

    dram_arrays = {
        "x_sample": a["x_sample"][0], "x_prompt": a["x_prompt"][0],
        "cond": np.stack([a["c"][0].reshape(KD, P), a["c_ctx"].reshape(KD, P)]).transpose(2, 1, 0).reshape(P, 2 * KD),
        "const": const, "rope_table": table,
        "cols": np.concatenate([
            col(a["g_pre_mix"][0]), col(a["g_pre_ffn"][0]), col(a["b_mod"][0]), col(a["g_q"][0]), col(a["g_kv"][0]),
            col(a["conv_w"][0][0]), col(a["conv_w"][0][1]), col(a["conv_w"][0][2]), col(a["conv_b"][0]),
            col(a["g_ssm_out"][0]), np.tile(a["dt_bias"].reshape(1, 16), (P, 1)),
            np.tile(a["a_log"].reshape(1, 16), (P, 1)),
            np.repeat(a["d_skip"][0].reshape(4, 2).T, P // 2, axis=0)], axis=1),
        "b_mod": a["b_mod"], "g_post_mix": a["g_post_mix"], "g_post_ffn": a["g_post_ffn"],
        "w_mod": a["w_mod"][0], "w_in": np.stack([k_tiles(in_tile(*e)) for e in TILES]),
        "w_uq": np.stack([k_tiles(w) for w in w_uq]), "w_uk": np.stack([k_tiles(w_ukv[:, h, :NOPE]) for h in range(HEADS)]),
        "w_uv": np.stack([k_tiles(w_ukv[:, h:h + 2, NOPE:].reshape(KV_LORA, 2 * VD)) for h in range(0, HEADS, 2)]), "w_out": a["w_out"][0],
        "w_gate": f_tiles(a["w_gate"][0]), "w_up": f_tiles(a["w_up"][0]), "w_down": a["w_down"][0].reshape(FT, P, D),
        "cache_ckv": a["cache_ckv"], "cache_krope": a["cache_krope"], "state_ssm": a["state_ssm"],
    }
    nc = bacc.Bacc("TRN2", target_bir_lowering=False, num_devices=1)
    arrays, dram = {}, {}
    for name, v in dram_arrays.items():
        arrays[f"in_{name}"] = np.ascontiguousarray(v)
        dram[name] = nc.dram_tensor(f"in_{name}", v.shape, F32, kind="ExternalInput").ap()
    outs = {n: nc.dram_tensor(f"out_{n}", shape, F32, kind="ExternalOutput").ap() for n, shape in _OUTS}
    hybrid_layer_kernel(nc, dram, outs)
    r = run_bass_kernel_spmd(nc, [arrays], core_ids=[0])
    return tuple(r.results[0][f"out_{n}"] for n, _ in _OUTS)
```
